# Optimizing a Trainium2 kernel written in Bass

```python
import math
import jax, jax.numpy as jnp
from jax import lax
import numpy as np

D_MODEL = 1024
BATCH = 1
SEQ = 256
DEPTH = 2
DEC_BATCH = 8
DEC_SEQ = 4
PAST_LEN = 2048
PAGE_SIZE = 128

N_EVEN = (DEPTH + 1) // 2
N_ODD = DEPTH // 2
CHUNK = 128
EPS = 1e-6

A_HEADS = 4
A_DK = 128
A_DV = 256
A_WIDTH = A_HEADS * A_DV
B_HEADS = 16
B_HEADDIM = 64
B_WIDTH = B_HEADS * B_HEADDIM
B_GROUPS = 2
B_STATE = 128
B_CONV = 4
B_CONV_DIM = B_WIDTH + 2 * B_GROUPS * B_STATE
C_HEADS = 8
C_DK = 128
C_DV = 256
C_WIDTH = C_HEADS * C_DV
ROPE_BASE = 10000.0
D_FF = 2816
FFN_CONV = 3

A_IN = 2 * A_HEADS * A_DK + A_WIDTH + 2 * A_HEADS + A_WIDTH
B_IN = B_WIDTH + B_CONV_DIM + B_HEADS
EVEN_IN = A_IN + B_IN
EVEN_MIX = A_WIDTH + B_WIDTH
ODD_IN = 2 * C_HEADS * C_DK + 2 * C_WIDTH

kernel_name = 'mlstm_ssd_retention_convffn_hybrid_step'

def rmsnorm(x, g):
    xf = x.astype(jnp.float32)
    y = xf * lax.rsqrt(jnp.mean(xf * xf, axis=-1, keepdims=True) + EPS)
    return (y * g.astype(jnp.float32)).astype(x.dtype)

def head_norm(h, g):
    mu = jnp.mean(h, axis=-1, keepdims=True)
    hc = h - mu
    y = hc * lax.rsqrt(jnp.mean(hc * hc, axis=-1, keepdims=True) + EPS)
    return y.reshape(h.shape[0], h.shape[1], -1) * g.astype(jnp.float32)

def causal_dwconv(x, buf, w, b):
    width = w.shape[0]
    T = x.shape[1]
    xx = jnp.concatenate([buf.astype(x.dtype), x], axis=1)
    y = b + xx[:, 0:T] * w[0]
    for j in range(1, width):
        y = y + xx[:, j:j + T] * w[j]
    return y, xx[:, T:]

def rope(x, pos):
    half = x.shape[-1] // 2
    inv = ROPE_BASE ** (-jnp.arange(half, dtype=jnp.float32) / half)
    ang = pos.astype(jnp.float32)[:, None] * inv[None, :]
    cos = jnp.cos(ang)[None, :, None, :]
    sin = jnp.sin(ang)[None, :, None, :]
    x = x.astype(jnp.float32)
    x1, x2 = x[..., :half], x[..., half:]
    return jnp.concatenate([x1 * cos - x2 * sin, x1 * sin + x2 * cos], axis=-1)

def _chunks(a, L):
    b, t = a.shape[0], a.shape[1]
    return jnp.swapaxes(a.reshape((b, t // L, L) + a.shape[2:]), 0, 1)

def _unchunks(a):
    a = jnp.swapaxes(a, 0, 1)
    return a.reshape((a.shape[0], a.shape[1] * a.shape[2]) + a.shape[3:])

def mlstm_chunked(q, k, v, i_pre, f_pre, C0, n0, m0):
    f32 = jnp.float32
    T = q.shape[1]
    L = math.gcd(T, CHUNK)
    q = q.astype(f32)
    k = k.astype(f32) * (A_DK ** -0.5)
    v = v.astype(f32)
    log_i = i_pre.astype(f32)
    log_f = jax.nn.log_sigmoid(f_pre.astype(f32))
    causal = jnp.tril(jnp.ones((L, L), dtype=bool))

    def step(carry, inp):
        C, n, m = carry
        qc, kc, vc, li, lf = inp
        b = jnp.swapaxes(jnp.cumsum(lf, axis=1), 1, 2)
        li = jnp.swapaxes(li, 1, 2)
        logw = jnp.where(causal, b[..., :, None] - b[..., None, :] + li[..., None, :], -jnp.inf)
        log_prev = b + m[..., None]
        m_t = jnp.maximum(log_prev, jnp.max(logw, axis=-1))
        w_in = jnp.exp(logw - m_t[..., None])
        w_prev = jnp.exp(log_prev - m_t)
        s = jnp.einsum('blhd,bshd->bhls', qc, kc) * w_in
        num = jnp.einsum('bhls,bshv->bhlv', s, vc) + jnp.einsum('blhd,bhdv->bhlv', qc, C) * w_prev[..., None]
        den = jnp.sum(s, axis=-1) + jnp.einsum('blhd,bhd->bhl', qc, n) * w_prev
        h = num / jnp.maximum(jnp.abs(den), jnp.exp(-m_t))[..., None]
        b_last = b[..., -1]
        log_g = b_last[..., None] - b + li
        m_new = jnp.maximum(b_last + m, jnp.max(log_g, axis=-1))
        g = jnp.swapaxes(jnp.exp(log_g - m_new[..., None]), 1, 2)[..., None]
        decay = jnp.exp(b_last + m - m_new)
        C_new = C * decay[..., None, None] + jnp.einsum('bshd,bshv->bhdv', kc * g, vc)
        n_new = n * decay[..., None] + jnp.sum(kc * g, axis=1)
        return (C_new, n_new, m_new), jnp.swapaxes(h, 1, 2)

    xs = (_chunks(q, L), _chunks(k, L), _chunks(v, L), _chunks(log_i, L), _chunks(log_f, L))
    (C, n, m), h = lax.scan(step, (C0.astype(f32), n0.astype(f32), m0.astype(f32)), xs)
    return _unchunks(h), C, n, m

def ssd_chunked(x, Bm, Cm, dt, A, h0):
    f32 = jnp.float32
    bsz, T = x.shape[0], x.shape[1]
    L = math.gcd(T, CHUNK)
    E = B_HEADS // B_GROUPS
    x = x.astype(f32).reshape(bsz, T, B_GROUPS, E, B_HEADDIM)
    dt = dt.astype(f32).reshape(bsz, T, B_GROUPS, E)
    a = dt * A.astype(f32).reshape(B_GROUPS, E)
    Bm = Bm.astype(f32)
    Cm = Cm.astype(f32)
    causal = jnp.tril(jnp.ones((L, L), dtype=bool))

    def step(S, inp):
        xc, bc, cc, dtc, ac = inp
        acum = jnp.cumsum(ac, axis=1)
        at = jnp.moveaxis(acum, 1, -1)
        seg = at[..., :, None] - at[..., None, :]
        decay = jnp.where(causal, jnp.exp(jnp.where(causal, seg, 0.0)), 0.0)
        cb = jnp.einsum('blgn,bsgn->bgls', cc, bc)
        M = cb[:, :, None] * decay * jnp.moveaxis(dtc, 1, -1)[..., None, :]
        y = jnp.einsum('bgels,bsgep->blgep', M, xc)
        y = y + jnp.einsum('blgn,bgepn->blgep', cc, S) * jnp.exp(acum)[..., None]
        a_last = acum[:, -1]
        w = jnp.exp(a_last[:, None] - acum) * dtc
        S_new = S * jnp.exp(a_last)[..., None, None] + jnp.einsum('bsgep,bsgn->bgepn', xc * w[..., None], bc)
        return S_new, y

    S0 = h0.astype(f32).reshape(bsz, B_GROUPS, E, B_HEADDIM, B_STATE)
    xs = (_chunks(x, L), _chunks(Bm, L), _chunks(Cm, L), _chunks(dt, L), _chunks(a, L))
    S, y = lax.scan(step, S0, xs)
    return _unchunks(y).reshape(bsz, T, B_HEADS, B_HEADDIM), S.reshape(bsz, B_HEADS, B_HEADDIM, B_STATE)

def retention_chunked(q, k, v, S0):
    f32 = jnp.float32
    T = q.shape[1]
    L = math.gcd(T, CHUNK)
    k = k * (C_DK ** -0.5)
    v = v.astype(f32)
    log_gamma = jnp.log1p(-jnp.exp2(-5.0 - jnp.arange(C_HEADS, dtype=f32)))
    idx = jnp.arange(L, dtype=f32)
    diff = idx[:, None] - idx[None, :]
    intra = jnp.where(diff >= 0, jnp.exp(log_gamma[:, None, None] * jnp.maximum(diff, 0.0)), 0.0)
    cross = jnp.exp(log_gamma[:, None] * (idx + 1.0)).T[:, :, None]
    into = jnp.exp(log_gamma[:, None] * (L - 1.0 - idx)).T[:, :, None]
    chunk_decay = jnp.exp(log_gamma * L)

    def step(S, inp):
        qc, kc, vc = inp
        s = jnp.einsum('blhd,bshd->bhls', qc, kc) * intra
        o = jnp.einsum('bhls,bshv->blhv', s, vc) + jnp.einsum('blhd,bhdv->blhv', qc, S) * cross
        S_new = S * chunk_decay[:, None, None] + jnp.einsum('bshd,bshv->bhdv', kc * into, vc)
        return S_new, o

    S, o = lax.scan(step, S0.astype(f32), (_chunks(q, L), _chunks(k, L), _chunks(v, L)))
    return _unchunks(o), S

def even_mixer(h, C0, n0, m0, conv0, ssm0, w_in, ig_b, fg_b, a_norm_g, conv_w, conv_b,
               dt_bias, A_log, D_skip, b_norm_g, w_out):
    f32 = jnp.float32
    bsz, T, _ = h.shape
    p = h @ w_in
    sizes = [A_HEADS * A_DK, A_HEADS * A_DK, A_WIDTH, A_HEADS, A_HEADS, A_WIDTH, B_WIDTH, B_CONV_DIM, B_HEADS]
    q, k, v, ig, fg, og, z, xbc, dt = jnp.split(p, np.cumsum(sizes)[:-1].tolist(), axis=-1)
    ha, C, n, m = mlstm_chunked(q.reshape(bsz, T, A_HEADS, A_DK), k.reshape(bsz, T, A_HEADS, A_DK),
                                v.reshape(bsz, T, A_HEADS, A_DV), ig + ig_b, fg + fg_b, C0, n0, m0)
    ya = head_norm(ha, a_norm_g) * jax.nn.sigmoid(og.astype(f32))
    xbc, conv_new = causal_dwconv(xbc, conv0, conv_w, conv_b)
    xbc = jax.nn.silu(xbc.astype(f32))
    xs, Bm, Cm = jnp.split(xbc, [B_WIDTH, B_WIDTH + B_GROUPS * B_STATE], axis=-1)
    xs = xs.reshape(bsz, T, B_HEADS, B_HEADDIM)
    dt = jax.nn.softplus(dt.astype(f32) + dt_bias)
    A = -jnp.exp(A_log.astype(f32))
    yb, ssm = ssd_chunked(xs, Bm.reshape(bsz, T, B_GROUPS, B_STATE), Cm.reshape(bsz, T, B_GROUPS, B_STATE), dt, A, ssm0)
    yb = (yb + D_skip.astype(f32)[:, None] * xs).reshape(bsz, T, B_WIDTH) * jax.nn.silu(z.astype(f32))
    yg = yb.reshape(bsz, T, B_GROUPS, -1)
    yg = yg * lax.rsqrt(jnp.mean(yg * yg, axis=-1, keepdims=True) + EPS)
    yb = yg.reshape(bsz, T, B_WIDTH) * b_norm_g.astype(f32)
    out = jnp.concatenate([ya, yb], axis=-1).astype(h.dtype) @ w_out
    return out, C, n, m, conv_new, ssm

def odd_mixer(h, pos, S0, w_in, norm_g, w_out):
    f32 = jnp.float32
    bsz, T, _ = h.shape
    p = h @ w_in
    q, k, v, g = jnp.split(p, [C_HEADS * C_DK, 2 * C_HEADS * C_DK, 2 * C_HEADS * C_DK + C_WIDTH], axis=-1)
    q = rope(q.reshape(bsz, T, C_HEADS, C_DK), pos)
    k = rope(k.reshape(bsz, T, C_HEADS, C_DK), pos)
    o, S = retention_chunked(q, k, v.reshape(bsz, T, C_HEADS, C_DV), S0)
    y = head_norm(o, norm_g) * jax.nn.silu(g.astype(f32))
    return y.astype(h.dtype) @ w_out, S

def conv_ffn(h, buf, w_up, conv_w, conv_b, w_down):
    u = h @ w_up
    u, buf_new = causal_dwconv(u, buf, conv_w, conv_b)
    gate, val = jnp.split(u, 2, axis=-1)
    return (jax.nn.silu(gate) * val) @ w_down, buf_new

def trunk(x, pos, st_C, st_n, st_m, st_conv, st_h, st_S, st_f,
          norm_mix_g, norm_ffn_g, norm_final_g,
          even_w_in, mlstm_igate_b, mlstm_fgate_b, mlstm_norm_g, ssd_conv_w, ssd_conv_b,
          ssd_dt_bias, ssd_A_log, ssd_D, ssd_norm_g, even_w_out,
          odd_w_in, ret_norm_g, odd_w_out,
          ffn_w_up, ffn_conv_w, ffn_conv_b, ffn_w_down):
    nC, nn_, nm, nconv, nh, nS, nf = [], [], [], [], [], [], []
    for layer in range(DEPTH):
        j = layer // 2
        h = rmsnorm(x, norm_mix_g[layer])
        if layer % 2 == 0:
            mix, C, n, m, cv, hs = even_mixer(h, st_C[j], st_n[j], st_m[j], st_conv[j], st_h[j],
                                              even_w_in[j], mlstm_igate_b[j], mlstm_fgate_b[j], mlstm_norm_g[j],
                                              ssd_conv_w[j], ssd_conv_b[j], ssd_dt_bias[j], ssd_A_log[j],
                                              ssd_D[j], ssd_norm_g[j], even_w_out[j])
            nC.append(C); nn_.append(n); nm.append(m); nconv.append(cv); nh.append(hs)
        else:
            mix, S = odd_mixer(h, pos, st_S[j], odd_w_in[j], ret_norm_g[j], odd_w_out[j])
            nS.append(S)
        x = x + mix.astype(x.dtype)
        f, fb = conv_ffn(rmsnorm(x, norm_ffn_g[layer]), st_f[layer], ffn_w_up[layer],
                         ffn_conv_w[layer], ffn_conv_b[layer], ffn_w_down[layer])
        nf.append(fb)
        x = x + f.astype(x.dtype)
    y = rmsnorm(x, norm_final_g)
    new_state = (jnp.stack(nC).astype(st_C.dtype), jnp.stack(nn_).astype(st_n.dtype),
                 jnp.stack(nm).astype(st_m.dtype), jnp.stack(nconv).astype(st_conv.dtype),
                 jnp.stack(nh).astype(st_h.dtype), jnp.stack(nS).astype(st_S.dtype),
                 jnp.stack(nf).astype(st_f.dtype))
    return y, new_state

def _fresh(s, bsz):
    return jnp.zeros((s.shape[0], bsz) + s.shape[2:], s.dtype)

def setup_inputs(seed: int = 0) -> dict:
    key = jax.random.key(seed)
    ks = iter(jax.random.split(key, 48))
    f32 = jnp.float32

    def nrm(shape, scale):
        return jax.random.normal(next(ks), shape, f32) * scale

    def gain(shape):
        return 1.0 + nrm(shape, 0.02)

    x_prompt = nrm((BATCH, SEQ, D_MODEL), 1.0)
    x_sample = nrm((DEC_BATCH, DEC_SEQ, D_MODEL), 1.0)
    state_mlstm_C = nrm((N_EVEN, DEC_BATCH, A_HEADS, A_DK, A_DV), 0.05)
    state_mlstm_n = nrm((N_EVEN, DEC_BATCH, A_HEADS, A_DK), 0.05)
    state_mlstm_m = nrm((N_EVEN, DEC_BATCH, A_HEADS), 0.5)
    state_ssd_conv = nrm((N_EVEN, DEC_BATCH, B_CONV - 1, B_CONV_DIM), 1.0)
    state_ssd_h = nrm((N_EVEN, DEC_BATCH, B_HEADS, B_HEADDIM, B_STATE), 0.1)
    state_ret_S = nrm((N_ODD, DEC_BATCH, C_HEADS, C_DK, C_DV), 0.1)
    state_ffn_conv = nrm((DEPTH, DEC_BATCH, FFN_CONV - 1, 2 * D_FF), 1.0)

    norm_mix_g = gain((DEPTH, D_MODEL))
    norm_ffn_g = gain((DEPTH, D_MODEL))
    norm_final_g = gain((D_MODEL,))

    even_w_in = nrm((N_EVEN, D_MODEL, EVEN_IN), D_MODEL ** -0.5)
    mlstm_igate_b = nrm((N_EVEN, A_HEADS), 0.1)
    mlstm_fgate_b = jnp.linspace(3.0, 6.0, A_HEADS, dtype=f32)[None, :] + nrm((N_EVEN, A_HEADS), 0.1)
    mlstm_norm_g = gain((N_EVEN, A_WIDTH))
    ssd_conv_w = nrm((N_EVEN, B_CONV, B_CONV_DIM), B_CONV ** -0.5)
    ssd_conv_b = nrm((N_EVEN, B_CONV_DIM), 0.02)
    dt0 = jnp.exp(jax.random.uniform(next(ks), (N_EVEN, B_HEADS), f32, math.log(1e-3), math.log(1e-1)))
    ssd_dt_bias = dt0 + jnp.log(-jnp.expm1(-dt0))
    ssd_A_log = jnp.log(jax.random.uniform(next(ks), (N_EVEN, B_HEADS), f32, 1.0, 16.0))
    ssd_D = gain((N_EVEN, B_HEADS))
    ssd_norm_g = gain((N_EVEN, B_WIDTH))
    even_w_out = nrm((N_EVEN, EVEN_MIX, D_MODEL), EVEN_MIX ** -0.5)

    odd_w_in = nrm((N_ODD, D_MODEL, ODD_IN), D_MODEL ** -0.5)
    ret_norm_g = gain((N_ODD, C_WIDTH))
    odd_w_out = nrm((N_ODD, C_WIDTH, D_MODEL), C_WIDTH ** -0.5)

    ffn_w_up = nrm((DEPTH, D_MODEL, 2 * D_FF), D_MODEL ** -0.5)
    ffn_conv_w = nrm((DEPTH, FFN_CONV, 2 * D_FF), FFN_CONV ** -0.5)
    ffn_conv_b = nrm((DEPTH, 2 * D_FF), 0.02)
    ffn_w_down = nrm((DEPTH, D_FF, D_MODEL), D_FF ** -0.5)

    return {'x_prompt': x_prompt, 'x_sample': x_sample,
            'state_mlstm_C': state_mlstm_C, 'state_mlstm_n': state_mlstm_n, 'state_mlstm_m': state_mlstm_m,
            'state_ssd_conv': state_ssd_conv, 'state_ssd_h': state_ssd_h, 'state_ret_S': state_ret_S,
            'state_ffn_conv': state_ffn_conv,
            'norm_mix_g': norm_mix_g, 'norm_ffn_g': norm_ffn_g, 'norm_final_g': norm_final_g,
            'even_w_in': even_w_in, 'mlstm_igate_b': mlstm_igate_b, 'mlstm_fgate_b': mlstm_fgate_b,
            'mlstm_norm_g': mlstm_norm_g, 'ssd_conv_w': ssd_conv_w, 'ssd_conv_b': ssd_conv_b,
            'ssd_dt_bias': ssd_dt_bias, 'ssd_A_log': ssd_A_log, 'ssd_D': ssd_D, 'ssd_norm_g': ssd_norm_g,
            'even_w_out': even_w_out,
            'odd_w_in': odd_w_in, 'ret_norm_g': ret_norm_g, 'odd_w_out': odd_w_out,
            'ffn_w_up': ffn_w_up, 'ffn_conv_w': ffn_conv_w, 'ffn_conv_b': ffn_conv_b, 'ffn_w_down': ffn_w_down}

def reference(x_prompt, x_sample, state_mlstm_C, state_mlstm_n, state_mlstm_m, state_ssd_conv, state_ssd_h,
              state_ret_S, state_ffn_conv, norm_mix_g, norm_ffn_g, norm_final_g,
              even_w_in, mlstm_igate_b, mlstm_fgate_b, mlstm_norm_g, ssd_conv_w, ssd_conv_b,
              ssd_dt_bias, ssd_A_log, ssd_D, ssd_norm_g, even_w_out,
              odd_w_in, ret_norm_g, odd_w_out,
              ffn_w_up, ffn_conv_w, ffn_conv_b, ffn_w_down):
    weights = (norm_mix_g, norm_ffn_g, norm_final_g,
               even_w_in, mlstm_igate_b, mlstm_fgate_b, mlstm_norm_g, ssd_conv_w, ssd_conv_b,
               ssd_dt_bias, ssd_A_log, ssd_D, ssd_norm_g, even_w_out,
               odd_w_in, ret_norm_g, odd_w_out,
               ffn_w_up, ffn_conv_w, ffn_conv_b, ffn_w_down)
    bsz = x_prompt.shape[0]
    pos_prompt = jnp.arange(x_prompt.shape[1], dtype=jnp.int32)
    pos_sample = PAST_LEN + jnp.arange(x_sample.shape[1], dtype=jnp.int32)
    y_prompt, (p_C, p_n, p_m, p_conv, p_h, p_S, p_f) = trunk(
        x_prompt, pos_prompt,
        _fresh(state_mlstm_C, bsz), _fresh(state_mlstm_n, bsz), _fresh(state_mlstm_m, bsz),
        _fresh(state_ssd_conv, bsz), _fresh(state_ssd_h, bsz), _fresh(state_ret_S, bsz),
        _fresh(state_ffn_conv, bsz), *weights)
    y_sample, (s_C, s_n, s_m, s_conv, s_h, s_S, s_f) = trunk(
        x_sample, pos_sample, state_mlstm_C, state_mlstm_n, state_mlstm_m, state_ssd_conv, state_ssd_h,
        state_ret_S, state_ffn_conv, *weights)
    return (y_prompt, y_sample, p_C, p_n, p_m, p_conv, p_h, p_S, p_f, s_C, s_n, s_m, s_conv, s_h, s_S, s_f)


_drawn_inputs = setup_inputs


def setup_inputs(seed=0):
    import zlib

    import numpy as np

    out = dict(_drawn_inputs(seed))
    spreads = {}
    factors = {'norm_final_g': 2.818,
     'mlstm_norm_g': 6.515,
     'ssd_D': 5.523,
     'ssd_norm_g': 3.252,
     'ret_norm_g': 6.859,
     'ffn_conv_b': 2.97}
    for name, (base, spread) in spreads.items():
        noise = np.random.default_rng([zlib.crc32(name.encode()), seed]).standard_normal(out[name].shape)
        drawn = base * np.exp(spread * noise) if base else spread * noise
        out[name] = __import__('jax').numpy.asarray(drawn.astype(out[name].dtype))
    for name, factor in factors.items():
        out[name] = (out[name] * factor).astype(out[name].dtype)
    return out
```

```python
import math
from contextlib import ExitStack

import numpy as np

import concourse.bass as bass
from concourse import mybir

F32 = mybir.dt.float32
F32R = mybir.dt.float32r
ALU = mybir.AluOpType
ACT = mybir.ActivationFunctionType

P = 128
D = 1024
KD = D // P
TP, NB, TS = 256, 8, 4
NS = NB * TS
T = TP + NS
EPS = 1e-6
AH, AV = 4, 256
CH, CV = 8, 256
BH, BP, BG = 16, 64, 2
HG = BH // BG
GW = HG * BP
KSCALE = P ** -0.5
FF = 2816
KF = FF // P
XB = 12
W1, W2 = 3, 2
CHUNK = 8
RING = 4
BLK = 2 * P + P + NS
LOG_GAMMA = [math.log1p(-2.0 ** (-5.0 - h)) for h in range(CH)]

EVEN = [("q", i) for i in range(AH)] + [("k", i) for i in range(AH)] + [("v", i) for i in range(8)] \
    + [("gates", 0)] + [("og", i) for i in range(8)] + [("z", i) for i in range(8)] \
    + [("xbc", i) for i in range(XB)]
ODD = [("rq", i) for i in range(CH)] + [("rk", i) for i in range(CH)] + [("rv", i) for i in range(16)] \
    + [("rg", i) for i in range(16)]
UP = [("up", i) for i in range(2 * KF)]
OUT = [("out", i) for i in range(KD)]
PHASES = [("even", EVEN, KD), ("even_out", OUT, 16), ("up0", UP, KD), ("down0", OUT, KF),
          ("odd", ODD, KD), ("odd_out", OUT, 16), ("up1", UP, KD), ("down1", OUT, KF)]


def plan_tiles():
    tiles, start, at = [], {}, 0
    for phase, kinds, k in PHASES:
        start[phase] = len(tiles)
        for kind, i in kinds:
            tiles.append((phase, kind, i, k, at))
            at += k
    assert at % CHUNK == 0
    return tiles, start, at // CHUNK


TILES, START, CHUNKS = plan_tiles()
BY_DVE = ("gates", "out", "rq", "rk")


def last_chunk(t):
    return (TILES[t][4] + TILES[t][3] - 1) // CHUNK


def emptied_by(t):
    return "dve" if TILES[t][1] in BY_DVE else "act"


EMPTIED = []
for _t in range(len(TILES)):
    EMPTIED.append(1 + sum(emptied_by(u) == emptied_by(_t) for u in range(_t)))

JOBS = []


def _jobs():
    def job(name, by):
        JOBS.append((name, by))

    def heads(kind, n):
        for h in range(n):
            if kind == "a":
                job(f"abc{h}", "dve")
            job(f"{kind}sc{h}", "dve")
            job(f"{kind}kn{h}", "dve")
            job(f"{kind}o0{h}", "act")
            job(f"{kind}o1{h}", "act")
            job(f"{kind}oi{h}", "dve")
            job(f"{kind}os{h}", "dve")
            job(f"{kind}sp{h}", "act")
            for b in range(NB):
                job(f"{kind}ss{h}.{b}", "dve")
            for i in range(2):
                job(f"{kind}yt{2 * h + i}", "dve")

    job("norm0", "act")
    for i in range(8):
        job(f"v{i}", "dve")
    for name in ("col0", "col1", "adec", "sdec"):
        job(name, "dve")
    heads("a", AH)
    for i in range(8):
        job(f"xn{i}", "dve")
    for g in range(BG):
        job(f"bn{g}", "act")
    for g in range(BG):
        job(f"cb{g}", "dve")
    for h in range(BH):
        job(f"sbc{h}", "dve")
        if h:
            job(f"say{h - 1}", "act")
    job(f"say{BH - 1}", "act")
    for g in range(BG):
        job(f"si{g}", "dve")
        job(f"sp{g}", "act")
        for b in range(NB):
            job(f"su{g}.{b}", "dve")
    for i in range(8):
        job(f"sy{i}", "dve")
    for g in range(BG):
        job(f"sn{g}", "act")
    job("norm1", "act")
    job("norm2", "act")
    for i in range(16):
        job(f"rv{i}", "dve")
    heads("r", CH)
    job("norm3", "act")
    job("norm4", "act")


_jobs()
JOB = {name: n for n, (name, _) in enumerate(JOBS)}
JOB_EMPTIED = [1 + sum(by == JOBS[n][1] for _, by in JOBS[:n]) for n in range(len(JOBS))]

CONSTS = {}
_at = 0
for _name, _w in (("ident", P), ("ones", P), ("mask", BLK), ("dist", BLK), ("own", NB * NS), ("mine", NB),
                  ("cos", T), ("sin", T), ("retk", 3 * CH), ("retq", CH)):
    CONSTS[_name] = (_at, _w)
    _at += _w
CONST_W = _at
VECS = {}
_at = 0
for _name, _w in (("norm0", 8), ("norm1", 8), ("norm2", 8), ("norm3", 8), ("norm4", 8), ("ag", 8),
                  ("scw", XB * 4), ("scb", XB), ("D", 8), ("sg", 8), ("rg", 16), ("fcw", 2 * 44 * 3),
                  ("fcb", 2 * 44), ("igb", 1), ("fgb", 1), ("dtb", 1), ("alog", 1), ("m0", NB), ("eps", 1)):
    VECS[_name] = (_at, _w)
    _at += _w
VEC_W = _at


CHUNK_READ = []
_mid = 0
for _c in range(CHUNKS):
    _end = (_c + 1) * CHUNK
    _t = next(t for t in range(len(TILES)) if TILES[t][4] + TILES[t][3] >= _end)
    if TILES[_t][4] + TILES[_t][3] == _end:
        CHUNK_READ.append(("tile", _t + 1))
    else:
        _mid += 1
        CHUNK_READ.append(("mid", _mid))


def build(nc, xin, wts, consts, starts, vecs, sconv, fconv, c_in, r_in, h_in,
          y_out, c_out, cp_out, m_out, sconv_out, h_out, hp_out, r_out, rp_out, f_out):
    ctx = ExitStack()
    with ctx:
        words = nc.sbuf_bytes_remaining // 4 - 32
        at0 = nc.sbuf_base
        ctx.enter_context(nc.sbuf_tensor("arena", [P, words], F32))
        top = at0 + 4 * words

        class Area:

            def __init__(self, at):
                self.at = (at + 31) // 32 * 32

            def take(self, name, shape, dt=F32):
                t = nc.alloc_sbuf_tensor_at(name, shape, dt, offset=self.at)
                self.at += (int(np.prod(shape[1:])) * 4 + 31) // 32 * 32
                assert self.at <= top, name
                return t

        keep = Area(at0)
        xT = keep.take("xT", [P, KD, T])
        hH = keep.take("hH", [P, KD, T], F32R)
        hL = keep.take("hL", [P, KD, T], F32R)
        hF = keep.take("hF", [P, KD, T])
        raw = keep.take("raw", [P, RING, CHUNK * P])
        wh = keep.take("wh", [P, RING, CHUNK * P], F32R)
        wl = keep.take("wl", [P, RING, CHUNK * P], F32R)
        cst = keep.take("cst", [P, CONST_W])
        vec = keep.take("vec", [P, VEC_W])
        sst = keep.take("sst", [P, XB, NB, W1])
        fst = keep.take("fst", [P, 2, 2 * KF, NB, W2])
        fout = keep.take("fout", [P, 2 * KF, (NB + 1) * W2])
        sout = keep.take("sout", [P, XB, (NB + 1) * W1])
        rstd = keep.take("rstd", [P, T])

        conv = Area(keep.at)
        pad = conv.take("pad", [P, 4, 320])
        cy = conv.take("cy", [P, 4, 312])
        ffn = Area(conv.at)
        sgate = ffn.take("sgate", [P, 2, 312])
        hidF = ffn.take("hidF", [P, 3, T])
        HH = ffn.take("HH", [P, KF, T], F32R)
        HL = ffn.take("HL", [P, KF, T], F32R)

        att = Area(conv.at)
        E = att.take("E", [P, 2, BLK])
        Sp = att.take("Sp", [P, 2, BLK])
        qTm = att.take("qTm", [P, 2, NB, NS])
        kg = att.take("kg", [P, 2, 2, P])
        kgm = att.take("kgm", [P, NB, P])
        num = att.take("num", [P, 2, 3, AV + 1])
        at_pout = att.at
        pout = att.take("pout", [P, 2, AV + 1])
        inter = att.take("inter", [P, AV + 1])
        yF = att.take("yF", [P, 2, T])
        vT = att.take("vT", [P, 2, T])
        stats = att.take("stats", [P, 3, 6])
        mv = att.take("mv", [P, 3, 2])
        sm = att.take("sm", [P, 8, 3])
        st = att.take("st", [P, 3, 4, AV + 1])

        ml = Area(att.at)
        qT = ml.take("qT", [P, AH, T])
        kT = ml.take("kT", [P, AH, T])
        vA = ml.take("vA", [P, 3, AH, AV + 1])
        y2 = Area(att.at)
        YH = y2.take("YH", [P, 8, T], F32R)
        YL = y2.take("YL", [P, 8, T], F32R)
        even = Area(max(ml.at, y2.at))
        xbcT = even.take("xbcT", [P, XB, T])
        zT = even.take("zT", [P, 8, T])
        cols = even.take("cols", [P, 3, 2 * P])
        adec = even.take("adec", [P, AH, NB])
        sdec = even.take("sdec", [P, NB, BH])
        nM = even.take("nM", [P, T])
        ac = even.take("ac", [P, T])
        rsm = even.take("rsm", [P, 6, 16])

        rw = Area(conv.at)
        slab = rw.take("slab", [P, 2, T])
        rows = rw.take("rows", [P, 9, T])
        dg = rw.take("dg", [P, NB, BH])
        resets = rw.take("resets", [P, 2, T])
        assert rw.at <= at_pout

        sd = Area(keep.at)
        rst2 = sd.take("rst2", [P, BG, T])
        xdt = sd.take("xdt", [P, 3, D])
        yn = sd.take("yn", [P, 3, D])
        bnat = sd.take("bnat", [P, 3, BG, P])
        bm = sd.take("bm", [P, NB, BG, P])
        cm = sd.take("cm", [P, BG, NB, NS])
        cbm = sd.take("cbm", [P, BG, BLK])
        E2 = sd.take("E2", [P, 2, BLK])
        ty = sd.take("ty", [P, 2, T])
        itmp = sd.take("itmp", [P, GW])
        pst = sd.take("pst", [P, 2, GW])
        sts = sd.take("sts", [P, NB, GW])
        assert sd.at <= ml.at

        odd = Area(att.at)
        rqT = odd.take("rqT", [P, CH, T])
        rkT = odd.take("rkT", [P, CH, T])
        rvA = odd.take("rvA", [P, 3, CH, CV])
        gT = odd.take("gT", [P, 8, T])
        y3 = Area(att.at)
        RH = y3.take("RH", [P, 8, T], F32R)
        RL = y3.take("RL", [P, 8, T], F32R)

        def const(name):
            at, w = CONSTS[name]
            return cst[:, at:at + w]

        def v(name, i=0, p=P):
            return vec[0:p, VECS[name][0] + i:VECS[name][0] + i + 1]

        ident, ones, mask, dist = (const(n) for n in ("ident", "ones", "mask", "dist"))
        own = const("own").rearrange("p (b l) -> p b l", b=NB)
        mine = const("mine")
        m0 = vec[0:AH, VECS["m0"][0]:VECS["m0"][0] + NB]

        bank = [ctx.enter_context(nc.psum_tensor(f"gemm{i}", [P, 512], F32)) for i in range(4)]
        mixb = [ctx.enter_context(nc.psum_tensor(f"mix{i}", [P, 512], F32)) for i in range(4)]

        def mb(name):
            return mixb[JOB[name] % 4]

        def sem(name):
            return ctx.enter_context(nc.semaphore(name))

        resets_in, scratch_free = sem("resets_in"), sem("scratch_free")
        x_in, const_in, vec_in, sst_in, fst_in = (sem(n) for n in ("x_in", "const_in", "vec_in", "sst_in", "fst_in"))
        raw_in = [sem(f"raw_in{i}") for i in range(RING)]
        st_in = [sem(f"st_in{i}") for i in range(3)]
        st_out = [sem(f"st_out{i}") for i in range(3)]
        sts_in = [sem(f"sts_in{i}") for i in range(NB)]
        sts_out = [sem(f"sts_out{i}") for i in range(NB)]
        pout_out = [sem(f"pout_out{i}") for i in range(2)]
        pst_out, fout_out, small_out, y_stored = (sem(n) for n in ("pst_out", "fout_out", "small_out", "y_stored"))
        act_step, dve_step, pool_step = sem("act_step"), sem("dve_step"), sem("pool_step")
        hi_ready, lo_ready, mid_read = sem("hi_ready"), sem("lo_ready"), sem("mid_read")
        gemm_done, mix_done = sem("gemm_done"), sem("mix_done")
        gemm_act, gemm_dve = sem("gemm_act"), sem("gemm_dve")
        mix_act, mix_dve = sem("mix_act"), sem("mix_dve")
        x_ready, sq_ready, rstd_ready = sem("x_ready"), sem("sq_ready"), sem("rstd_ready")
        h_ready, xhi_ready, xlo_ready = sem("h_ready"), sem("xhi_ready"), sem("xlo_ready")
        zeroed, fill_done, tail_done, conv_done = (sem(n) for n in ("zeroed", "fill_done", "tail_done", "conv_done"))
        silu_done, hid_ready, hidhi_ready, hidlo_ready = (sem(n) for n in ("silu_done", "hid_ready", "hidhi_ready", "hidlo_ready"))
        row_dve, row_act, slab_ready = sem("row_dve"), sem("row_act"), sem("slab_ready")
        exp_ready, w_ready, qm_ready = sem("exp_ready"), sem("w_ready"), sem("qm_ready")
        var_ready, inv_ready, yn_ready = sem("var_ready"), sem("inv_ready"), sem("yn_ready")
        yhi_ready, ylo_ready = sem("yhi_ready"), sem("ylo_ready")
        bm_ready, exp2_ready, e_ready, xw_ready = (sem(n) for n in ("bm_ready", "exp2_ready", "e_ready", "xw_ready"))
        dec_ready, ynat_ready = sem("dec_ready"), sem("ynat_ready")
        zq_ready, sq2_ready, srs_ready, yg_ready = (sem(n) for n in ("zq_ready", "sq2_ready", "srs_ready", "yg_ready"))
        rope_ready, y_ready = sem("rope_ready"), sem("y_ready")

        class Steps:

            def __init__(self, eng, own_sem):
                self.eng, self.own, self.count, self.last = eng, own_sem, {}, None

            def do(self, ins, s=None):
                s = self.own if s is None else s
                self.count[s.name] = self.count.get(s.name, 0) + 1
                ins.then_inc(s, 1)
                self.last = (s, self.count[s.name])

            def settle(self):
                self.eng.wait_ge(*self.last)

        def wait_tile(eng, t):
            eng.wait_ge(gemm_done, t + 1)

        def wait_tile_empty(eng, t):
            eng.wait_ge(gemm_act if emptied_by(t) == "act" else gemm_dve, EMPTIED[t])

        def wait_job(eng, name):
            eng.wait_ge(mix_done, JOB[name] + 1)

        def wait_empty(eng, name):
            n = JOB[name]
            eng.wait_ge(mix_act if JOBS[n][1] == "act" else mix_dve, JOB_EMPTIED[n])

        def wait_read(eng, c):
            kind, n = CHUNK_READ[c]
            eng.wait_ge(gemm_done if kind == "tile" else mid_read, n)

        def smp(ap):
            return ap[:, TP:T].rearrange("p (b t) -> p b t", b=NB)

        def padded(ap, w, at=0):
            s = at + w + TP
            return ap[:, s:s + NB * (w + TS)].rearrange("p (b t) -> p b t", b=NB)

        def bc(ap, axis, n):
            a = ap.unsqueeze(axis)
            return a.broadcast_to([*a.shape[:axis], n, *a.shape[axis + 1:]])

        YA = ((hH, hL), (YH, YL))
        YR = ((hH, hL), (RH, RL))
        T0 = START["even"]
        XBC0 = T0 + 33

        HEADS = [("a", h, h) for h in range(AH)] + [("r", h, AH + h) for h in range(CH)]

        def state_dram(n, out):
            hg, x = divmod(n, 2)
            kind, h, _ = HEADS[hg]
            t = (c_out if out else c_in) if kind == "a" else (r_out if out else r_in)
            w = AV + 1 if kind == "a" else CV
            return t[h][:, 4 * x:4 * x + 4, :], w

        block = ctx.enter_context(nc.Block())

        @block.sync
        def _(sp):
            sp.dma_start(xT[:], xin).then_inc(x_in, 16)
            sp.dma_start(vec[:], vecs).then_inc(vec_in, 16)
            sp.dma_start(cst[:], consts).then_inc(const_in, 16)
            sp.dma_start(resets[0:BH], starts).then_inc(resets_in, 16)
            for c in range(CHUNKS):
                if c >= RING:
                    sp.wait_ge(lo_ready, c - RING + 1)
                sp.dma_start(raw[:, c % RING, :], wts[c]).then_inc(raw_in[c % RING], 16)
            sp.wait_ge(y_ready, KD)
            sp.dma_start(y_out, hF[:]).then_inc(y_stored, 16)
            sp.wait_ge(y_stored, 16)

        @block.tensor
        def _(pe):
            mm = nc.tensor.matmul

            def tile(t, rhs, operand=None):
                _, kind, _, K, w0 = TILES[t]
                if t >= 4:
                    wait_tile_empty(pe, t - 4)
                out = bank[t % 4][:, 0:T]
                for k in range(K):
                    c, pos = divmod(w0 + k, CHUNK)
                    if k == 0 or pos == 0:
                        pe.wait_ge(lo_ready, c + 1)
                    if operand is not None:
                        pe.wait_ge(operand[0], operand[1] + k + 1)
                    xh, xl = rhs(k)
                    h = wh[:, c % RING, pos * P:(pos + 1) * P]
                    lo = wl[:, c % RING, pos * P:(pos + 1) * P]
                    mm(out, h, xh, start=(k == 0), stop=False)
                    mm(out, h, xl, start=False, stop=False)
                    last = mm(out, lo, xh, start=False, stop=(k == K - 1))
                    if pos == CHUNK - 1 and k < K - 1:
                        last.then_inc(mid_read, 1)
                last.then_inc(gemm_done, 1)

            turn_of = [0]

            def free_bank(name):
                n = JOB[name]
                assert n == turn_of[0], name
                turn_of[0] += 1
                if n >= 4:
                    wait_empty(pe, JOBS[n - 4][0])
                return mb(name)

            def norm(n):
                out = free_bank(f"norm{n}")[:, 0:T]
                for i in range(KD):
                    pe.wait_ge(sq_ready, KD * n + i + 1)
                    last = mm(out, ones, hF[:, i, :], start=(i == 0), stop=(i == KD - 1))
                last.then_inc(mix_done, 1)

            def normed(k):
                return hH[:, k, :], hL[:, k, :]

            def turn(name, src):
                out = free_bank(name)
                for g, (a, n) in enumerate(((0, P), (P, P), (TP, NS))):
                    last = nc.tensor.transpose(out[0:n, g * P:(g + 1) * P], src[:, a:a + n], ident)
                last.then_inc(mix_done, 1)

            def turn_back(name, src):
                out = free_bank(name)
                for g, (a, n) in enumerate(((0, P), (P, P), (TP, NS))):
                    last = nc.tensor.transpose(out[:, a:a + n], src(g)[0:n], ident[0:n, 0:n])
                last.then_inc(mix_done, 1)

            def scores(out, k, q):
                mm(out[:, 0:TP], k[:, 0:P], q[:, 0:TP], start=True, stop=True)
                mm(out[:, TP:TP + P], k[:, P:TP], q[:, P:TP], start=True, stop=True)
                return mm(out[0:NS, TP + P:BLK], k[:, TP:T], q[:, TP:T], start=True, stop=True)

            def head(kind, h, hg, q, k, va, w):
                if kind == "a":
                    out = free_bank(f"abc{h}")
                    mm(out[:, 0:T], ident[0:AH, h:h + 1].broadcast_to([AH, P]), nM[0:AH, :],
                       start=True, stop=True).then_inc(mix_done, 1)
                else:
                    pe.wait_ge(rope_ready, CH + h + 1)
                out = free_bank(f"{kind}sc{h}")
                scores(out, k, q).then_inc(mix_done, 1)
                turn(f"{kind}kn{h}", k)
                s = Sp[:, hg % 2, :]
                wait_empty(pe, f"{kind}sc{h}")
                out = free_bank(f"{kind}o0{h}")
                mm(out[:, 0:w], s[:, 0:P], va(0), start=True, stop=True).then_inc(mix_done, 1)
                out = free_bank(f"{kind}o1{h}")
                mm(out[:, 0:w], s[:, P:TP], va(0), start=True, stop=False)
                mm(out[:, 0:w], s[:, TP:TP + P], va(1), start=False, stop=True).then_inc(mix_done, 1)
                out = free_bank(f"{kind}oi{h}")
                pe.wait_ge(qm_ready, hg + 1)
                for b in range(NB):
                    n = 2 * hg + b // 4
                    pe.wait_ge(st_in[n % 3], 16 * (n // 3 + 1))
                    last = mm(out[0:NS, 0:w], qTm[:, hg % 2, b, :], st[:, n % 3, b % 4, 0:w],
                              start=(b == 0), stop=(b == NB - 1))
                last.then_inc(mix_done, 1)
                out = free_bank(f"{kind}os{h}")
                mm(out[0:NS, 0:w], s[0:NS, TP + P:BLK], va(2)[0:NS], start=True, stop=True).then_inc(mix_done, 1)
                out = free_bank(f"{kind}sp{h}")
                wait_empty(pe, f"{kind}kn{h}")
                mm(out[:, 0:w], kg[:, hg % 2, 0, :], va(0), start=True, stop=False)
                mm(out[:, 0:w], kg[:, hg % 2, 1, :], va(1), start=False, stop=True).then_inc(mix_done, 1)
                for b in range(NB):
                    out = free_bank(f"{kind}ss{h}.{b}")
                    mm(out[:, 0:w], kgm[0:NS, b, :], va(2)[0:NS], start=True, stop=True).then_inc(mix_done, 1)
                pe.wait_ge(yn_ready, hg + 1)
                for i in range(2):
                    turn_back(f"{kind}yt{2 * h + i}", lambda g: num[:, hg % 2, g, i * P:(i + 1) * P])

            def ffn(l):
                norm(2 * l + 1)
                for i in range(2 * KF):
                    tile(START[f"up{l}"] + i, normed, (xlo_ready, KD * (2 * l + 1)) if i == 0 else None)
                for i in range(KD):
                    tile(START[f"down{l}"] + i, lambda k: (HH[:, k, :], HL[:, k, :]),
                         (hidlo_ready, KF * l) if i == 0 else None)

            pe.wait_ge(const_in, 16)
            norm(0)
            for t in range(T0, START["even_out"]):
                tile(t, normed, (xlo_ready, 0) if t == T0 else None)
                if 9 <= t <= 16:
                    wait_tile_empty(pe, t - 1)
                    turn(f"v{t - 9}", vT[:, (t - 9) % 2, :])
            pe.wait_ge(slab_ready, 1)
            for s in range(2):
                turn(f"col{s}", slab[:, s, :])
            out = free_bank("adec")
            for h in range(AH):
                last = mm(out[:, h * NB:(h + 1) * NB], ident[0:AH, h:h + 1].broadcast_to([AH, P]),
                          rsm[0:AH, 2, 0:NB], start=True, stop=True)
            last.then_inc(mix_done, 1)
            out = free_bank("sdec")
            mm(out[:, 0:NB * BH], ones[0:BH, :], dg[0:BH, :, :].rearrange("p b h -> p (b h)"),
               start=True, stop=True).then_inc(mix_done, 1)
            for h in range(AH):
                head("a", h, h, qT[:, h, :], kT[:, h, :], lambda g: vA[:, g, h, :], AV + 1)
            pe.wait_ge(silu_done, XB)
            for i in range(8):
                turn(f"xn{i}", xbcT[:, i, :])
            for g in range(BG):
                turn(f"bn{g}", xbcT[:, 8 + g, :])
            for g in range(BG):
                out = free_bank(f"cb{g}")
                scores(out, xbcT[:, 8 + g, :], xbcT[:, 10 + g, :]).then_inc(mix_done, 1)

            def say(h):
                out = free_bank(f"say{h}")
                pe.wait_ge(e_ready, h + 1)
                e = E2[:, h % 2, :]
                x = xdt[:, :, h * BP:(h + 1) * BP]
                mm(out[:, 0:BP], e[:, 0:P], x[:, 0, :], start=True, stop=True)
                mm(out[:, BP:2 * BP], e[:, P:TP], x[:, 0, :], start=True, stop=False)
                mm(out[:, BP:2 * BP], e[:, TP:TP + P], x[:, 1, :], start=False, stop=True)
                mm(out[0:NS, 2 * BP:3 * BP], e[0:NS, TP + P:BLK], x[0:NS, 2, :], start=True, stop=True)\
                    .then_inc(mix_done, 1)

            for h in range(BH):
                out = free_bank(f"sbc{h}")
                mm(out[:, 0:T], ident[0:BH, h:h + 1].broadcast_to([BH, P]), ac[0:BH, :],
                   start=True, stop=True).then_inc(mix_done, 1)
                if h:
                    say(h - 1)
            say(BH - 1)
            for g in range(BG):
                sl = slice(g * GW, (g + 1) * GW)
                out = free_bank(f"si{g}")
                pe.wait_ge(bm_ready, BG)
                for b in range(NB):
                    pe.wait_ge(sts_in[b], 16 * (g + 1))
                    last = mm(out[0:NS, :], cm[:, g, b, :], sts[:, b, :], start=(b == 0), stop=(b == NB - 1))
                last.then_inc(mix_done, 1)
                out = free_bank(f"sp{g}")
                pe.wait_ge(xw_ready, 1)
                mm(out[:, :], bnat[:, 0, g, :], xdt[:, 0, sl], start=True, stop=False)
                mm(out[:, :], bnat[:, 1, g, :], xdt[:, 1, sl], start=False, stop=True).then_inc(mix_done, 1)
                for b in range(NB):
                    out = free_bank(f"su{g}.{b}")
                    mm(out[:, :], bm[0:NS, b, g, :], xdt[0:NS, 2, sl], start=True, stop=True).then_inc(mix_done, 1)
            pe.wait_ge(ynat_ready, BG)
            for i in range(8):
                turn_back(f"sy{i}", lambda g: yn[:, g, i * P:(i + 1) * P])
            for g in range(BG):
                out = free_bank(f"sn{g}")
                for i in range(4):
                    pe.wait_ge(sq2_ready, 4 * g + i + 1)
                    last = mm(out[:, 0:T], ones, xbcT[:, 4 * g + i, :], start=(i == 0), stop=(i == 3))
                last.then_inc(mix_done, 1)
            for i in range(KD):
                tile(START["even_out"] + i,
                     lambda k: (hH[:, k, :], hL[:, k, :]) if k < 8 else (YH[:, k - 8, :], YL[:, k - 8, :]),
                     (ylo_ready, 0) if i == 0 else None)
            ffn(0)
            norm(2)
            for i in range(len(ODD)):
                t = START["odd"] + i
                tile(t, normed, (xlo_ready, 2 * KD) if i == 0 else None)
                if 17 <= i <= 32:
                    wait_tile_empty(pe, t - 1)
                    turn(f"rv{i - 17}", vT[:, (i - 17) % 2, :])
            for h in range(CH):
                head("r", h, AH + h, rqT[:, h, :], rkT[:, h, :], lambda g: rvA[:, g, h, :], CV)
            for i in range(KD):
                tile(START["odd_out"] + i,
                     lambda k: (hH[:, k, :], hL[:, k, :]) if k < 8 else (RH[:, k - 8, :], RL[:, k - 8, :]),
                     (ylo_ready, 16) if i == 0 else None)
            ffn(1)
            norm(4)

        @block.scalar
        def _(eng):
            s = Steps(eng, act_step)
            act = nc.scalar.activation
            at = [0]

            def split(upto):
                while at[0] <= min(upto, CHUNKS - 1):
                    c = at[0]
                    eng.wait_ge(raw_in[c % RING], 16 * (c // RING + 1))
                    if c >= RING:
                        wait_read(eng, c - RING)
                    s.do(act(wh[:, c % RING, :], raw[:, c % RING, :], ACT.Copy), hi_ready)
                    at[0] += 1

            def rsqrt(dst, src, n, ready):
                s.do(act(dst, src, ACT.Ln, scale=1.0 / n, bias=eps[0:dst.shape[0]]))
                s.settle()
                s.do(act(dst, dst, ACT.Exp, scale=-0.5), ready)

            eps = vec[:, VEC_W - 1:VEC_W]

            def norm(n):
                if n == 0:
                    eng.wait_ge(x_in, 16)
                    eng.wait_ge(vec_in, 16)
                else:
                    eng.wait_ge(xlo_ready, KD * n)
                if n in (1, 3):
                    eng.wait_ge(ylo_ready, 16 if n == 1 else 32)
                for i in range(KD):
                    if n:
                        eng.wait_ge(x_ready, KD * (n - 1) + i + 1)
                    s.do(act(hF[:, i, :], xT[:, i, :], ACT.Square), sq_ready)
                wait_job(eng, f"norm{n}")
                s.do(act(rstd[:], mb(f"norm{n}")[:, 0:T], ACT.Ln, scale=1.0 / D, bias=eps), mix_act)
                s.settle()
                s.do(act(rstd[:], rstd[:], ACT.Exp, scale=-0.5), rstd_ready)
                if n == 4:
                    return
                for i in range(KD):
                    eng.wait_ge(h_ready, KD * n + i + 1)
                    s.do(act(hH[:, i, :], hF[:, i, :], ACT.Copy), xhi_ready)

            def y_high(n, dst, src):
                s.do(act(dst, src, ACT.Copy), yhi_ready)

            def head(kind, h, hg, Y, w):
                wait = f"{kind}sc{HEADS[hg - 2][1]}"
                if kind == "a":
                    wait_empty(eng, f"abc{h}")
                    s.do(act(E[:, hg % 2, 0:TP + P], E[:, hg % 2, 0:TP + P], ACT.Exp))
                    s.do(act(E[0:NS, hg % 2, TP + P:BLK], E[0:NS, hg % 2, TP + P:BLK], ACT.Exp), exp_ready)
                else:
                    if h == 0:
                        eng.wait_ge(rope_ready, 2 * CH)
                    if h >= 2:
                        wait_empty(eng, f"rsc{h - 2}")
                    s.do(act(E[:, hg % 2, :], dist, ACT.Exp, scale=LOG_GAMMA[h]), exp_ready)
                if h == 0:
                    eng.wait_ge(zeroed, 3 if kind == "a" else 5)
                if hg >= 2:
                    kk, hh, _ = HEADS[hg - 2]
                    wait_job(eng, f"{kk}yt{2 * hh + 1}")
                for g in range(2):
                    wait_job(eng, f"{kind}o{g}{h}")
                    s.do(act(num[:, hg % 2, g, 0:w], mb(f"{kind}o{g}{h}")[:, 0:w], ACT.Copy), mix_act)
                if hg >= 2:
                    eng.wait_ge(pout_out[hg % 2], 16 * (hg // 2))
                wait_job(eng, f"{kind}sp{h}")
                s.do(act(pout[:, hg % 2, 0:w], mb(f"{kind}sp{h}")[:, 0:w], ACT.Copy), mix_act)
                eng.wait_ge(var_ready, hg + 1)
                s.do(act(sm[:, 5, :], sm[:, 4, :], ACT.Ln, bias=eps))
                s.settle()
                s.do(act(sm[:, 6, :], sm[:, 5, :], ACT.Exp, scale=-0.5), inv_ready)
                for i in range(2):
                    n = 2 * h + i
                    wait_empty(eng, f"{kind}yt{n}")
                    y_high(n, Y[n // 8][0][:, n % 8, :], yF[:, n % 2, :])

            def ffn(l):
                norm(2 * l + 1)
                t0 = START[f"up{l}"]

                eng.wait_ge(zeroed, 4 + 2 * l)

                def silu(j):
                    eng.wait_ge(conv_done, XB + 2 * KF * l + 2 * j + 1)
                    if j >= 2:
                        eng.wait_ge(hid_ready, KF * l + j - 1)
                    s.do(act(sgate[:, j % 2, 0:304], cy[:, 2 * (j % 2), 0:304], ACT.Silu), silu_done)

                def high(j):
                    eng.wait_ge(hid_ready, KF * l + j + 1)
                    s.do(act(HH[:, j, :], hidF[:, j % 3, :], ACT.Copy), hidhi_ready)

                for j in range(KF + 2):
                    if j < KF:
                        for x in range(2):
                            i = 2 * j + x
                            split(last_chunk(t0 + i) + 3)
                            wait_tile(eng, t0 + i)
                            n = XB + 2 * KF * l + i
                            if n >= 4:
                                eng.wait_ge(conv_done, n - 3)
                                eng.wait_ge(tail_done, n - 3)
                            b = bank[(t0 + i) % 4]
                            p = pad[:, n % 4, 1:]
                            s.do(act(p[:, W2:W2 + TP], b[:, 0:TP], ACT.Copy))
                            s.do(act(padded(p, W2)[:, :, W2:], smp(b), ACT.Copy), gemm_act)
                    if 1 <= j <= KF:
                        silu(j - 1)
                    if j >= 2:
                        high(j - 2)
                for i in range(KD):
                    split(last_chunk(START[f"down{l}"] + i) + 3)

            def silu_x(i):
                eng.wait_ge(conv_done, i + 1)
                s.do(act(xbcT[:, i, 0:TP], cy[:, i % 4, 0:TP], ACT.Silu))
                s.do(act(smp(xbcT[:, i, :]), padded(cy[:, i % 4, :], W1, -W1)[:, :, W1:], ACT.Silu), silu_done)

            split(2)
            norm(0)
            eng.wait_ge(zeroed, 1)
            for t in range(T0, START["even_out"]):
                kind, i = TILES[t][1:3]
                split(last_chunk(t) + 3)
                if kind != "gates":
                    wait_tile(eng, t)
                b = bank[t % 4]
                if kind in ("q", "k"):
                    s.do(act((qT if kind == "q" else kT)[:, i, :], b[:, 0:T], ACT.Copy), gemm_act)
                elif kind == "v":
                    if i >= 2:
                        wait_job(eng, f"v{i - 2}")
                    s.do(act(vT[:, i % 2, :], b[:, 0:T], ACT.Copy), gemm_act)
                elif kind == "gates":
                    eng.wait_ge(row_dve, 1)
                    s.do(act(rows[0:AH, 3, :], rows[0:AH, 3, :], ACT.Exp))
                    s.do(act(rows[0:BH, 4, :], rows[0:BH, 4, :], ACT.Exp))
                    s.do(act(rsm[0:BH, 5, 0:1], v("alog", p=BH), ACT.Exp))
                    s.settle()
                    s.do(act(rows[0:AH, 3, :], rows[0:AH, 3, :], ACT.Ln, bias=1.0))
                    s.do(act(rows[0:BH, 4, :], rows[0:BH, 4, :], ACT.Ln, bias=1.0), row_act)
                    eng.wait_ge(row_dve, 2)
                    s.do(act(slab[64:64 + AH, 0, :], rows[0:AH, 3, :], ACT.Exp, scale=-1.0))
                    s.do(act(slab[32:32 + AH, 0, TP:T], rows[0:AH, 4, TP:T], ACT.Exp))
                    s.do(act(rows[0:AH, 5, :], rows[0:AH, 5, :], ACT.Exp))
                    s.do(act(rsm[0:AH, 2, 0:NB], rsm[0:AH, 2, 0:NB], ACT.Exp))
                    s.do(act(slab[96:96 + BH, 1, :], rows[0:BH, 2, :], ACT.Exp, scale=-1.0))
                    s.do(act(slab[64:64 + BH, 1, :], ac[0:BH, :], ACT.Exp))
                    s.do(act(rsm[0:BH, 3, 0:NB], smp(ac[0:BH, :])[:, :, TS - 1], ACT.Exp), row_act)
                elif kind == "og":
                    if i == 0:
                        eng.wait_ge(xlo_ready, KD)
                    s.do(act(hF[:, i, :], b[:, 0:T], ACT.Sigmoid), gemm_act)
                elif kind == "z":
                    s.do(act(zT[:, i, :], b[:, 0:T], ACT.Silu), gemm_act)
                elif kind == "xbc":
                    if i >= 4:
                        eng.wait_ge(conv_done, i - 3)
                        eng.wait_ge(tail_done, i - 3)
                    p = pad[:, i % 4, :]
                    s.do(act(p[:, W1:W1 + TP], b[:, 0:TP], ACT.Copy))
                    s.do(act(padded(p, W1)[:, :, W1:], smp(b), ACT.Copy), gemm_act)
                    if i >= 1:
                        silu_x(i - 1)
            silu_x(XB - 1)
            for h in range(AH):
                head("a", h, h, YA, AV + 1)
            eng.wait_ge(scratch_free, 1)
            for g in range(BG):
                wait_job(eng, f"bn{g}")
                b = mb(f"bn{g}")
                s.do(act(bnat[:, 0:2, g, :], b[:, 0:TP].rearrange("p (g n) -> p g n", g=2), ACT.Copy))
                s.do(act(bnat[0:NS, 2, g, :], b[0:NS, TP:TP + P], ACT.Copy), mix_act)
            for h in range(BH + 1):
                if h < BH:
                    wait_empty(eng, f"sbc{h}")
                    s.do(act(E2[:, h % 2, 0:TP + P], E2[:, h % 2, 0:TP + P], ACT.Exp))
                    s.do(act(E2[0:NS, h % 2, TP + P:BLK], E2[0:NS, h % 2, TP + P:BLK], ACT.Exp), exp2_ready)
                if h:
                    wait_job(eng, f"say{h - 1}")
                    b = mb(f"say{h - 1}")
                    sl = slice((h - 1) * BP, h * BP)
                    s.do(act(yn[:, 0:2, sl], b[:, 0:2 * BP].rearrange("p (g n) -> p g n", g=2), ACT.Copy))
                    s.do(act(yn[0:NS, 2, sl], b[0:NS, 2 * BP:3 * BP], ACT.Copy), mix_act)
            for g in range(BG):
                wait_job(eng, f"sp{g}")
                s.do(act(pst[:, g, :], mb(f"sp{g}")[:, :], ACT.Copy), mix_act)
            for i in range(8):
                eng.wait_ge(zq_ready, i + 1)
                s.do(act(xbcT[:, i, :], zT[:, i, :], ACT.Square), sq2_ready)
            for g in range(BG):
                wait_job(eng, f"sn{g}")
                s.do(act(rst2[:, g, :], mb(f"sn{g}")[:, 0:T], ACT.Ln, scale=1.0 / GW, bias=eps), mix_act)
                s.settle()
                s.do(act(rst2[:, g, :], rst2[:, g, :], ACT.Exp, scale=-0.5), srs_ready)
            for b in range(NB):
                eng.wait_ge(sts_out[b], 16 * BG)
            for i in range(8):
                eng.wait_ge(yg_ready, i + 1)
                y_high(8 + i, YH[:, i, :], zT[:, i, :])
            for i in range(KD):
                split(last_chunk(START["even_out"] + i) + 3)
            ffn(0)
            norm(2)
            for j in range(len(ODD)):
                t = START["odd"] + j
                kind, i = TILES[t][1:3]
                split(last_chunk(t) + 3)
                b = bank[t % 4]
                if kind == "rv":
                    wait_tile(eng, t)
                    if i >= 2:
                        wait_job(eng, f"rv{i - 2}")
                    s.do(act(vT[:, i % 2, :], b[:, 0:T], ACT.Copy), gemm_act)
                elif kind == "rg":
                    wait_tile(eng, t)
                    if i == 8:
                        eng.wait_ge(xlo_ready, 3 * KD)
                    s.do(act(gT[:, i, :] if i < 8 else hF[:, i - 8, :], b[:, 0:T], ACT.Silu), gemm_act)
            for h in range(CH):
                head("r", h, AH + h, YR, CV)
            for i in range(KD):
                split(last_chunk(START["odd_out"] + i) + 3)
            ffn(1)
            norm(4)

        @block.vector
        def _(eng):
            s = Steps(eng, dve_step)
            do, settle = s.do, s.settle
            ts, tt, stt = nc.vector.tensor_scalar, nc.vector.tensor_tensor, nc.vector.scalar_tensor_tensor
            copy = nc.vector.tensor_copy
            at = [0]

            def split(upto):
                while at[0] <= min(upto, CHUNKS - 1):
                    c = at[0]
                    eng.wait_ge(hi_ready, c + 1)
                    if c >= RING:
                        wait_read(eng, c - RING)
                    do(tt(wl[:, c % RING, :], raw[:, c % RING, :], wh[:, c % RING, :].bitcast(F32), ALU.subtract), lo_ready)
                    at[0] += 1

            def norm(n):
                if n == 0:
                    eng.wait_ge(vec_in, 16)
                eng.wait_ge(rstd_ready, n + 1)
                for i in range(KD):
                    do(stt(out=hF[:, i, :], in0=xT[:, i, :], scalar=v(f"norm{n}", i), in1=rstd[:],
                           op0=ALU.mult, op1=ALU.mult), h_ready if n < 4 else y_ready)
                if n == 4:
                    return
                for i in range(KD):
                    eng.wait_ge(xhi_ready, KD * n + i + 1)
                    do(tt(hL[:, i, :], hF[:, i, :], hH[:, i, :].bitcast(F32), ALU.subtract), xlo_ready)

            def out_tiles(phase, n):
                for i in range(KD):
                    t = START[phase] + i
                    split(last_chunk(t) + 3)
                    wait_tile(eng, t)
                    do(tt(xT[:, i, :], bank[t % 4][:, 0:T], xT[:, i, :], ALU.add), gemm_dve)
                    settle()
                    eng.sem_inc(x_ready, 1)

            def turned(name, dst):
                wait_job(eng, name)
                b = mb(name)
                do(copy(dst(slice(0, 2), P), b[:, 0:TP].rearrange("p (g n) -> p g n", g=2)))
                do(copy(dst(2, NS), b[0:NS, TP:TP + P]), mix_dve)

            def column(s_, i, g):
                n = NS if g == 2 else P
                return cols[0:n, g, P * s_ + i:P * s_ + i + 1]

            def head(kind, h, hg, q, k, Y, w):
                sl = hg % 2
                if kind == "a":
                    wait_job(eng, f"abc{h}")
                    b = mb(f"abc{h}")
                    do(ts(E[:, sl, 0:TP], b[:, 0:TP], column(0, h, 0), 0.0, ALU.add, ALU.min))
                    do(ts(E[:, sl, TP:TP + P], b[:, P:TP], column(0, h, 1), 0.0, ALU.add, ALU.min))
                    do(ts(E[0:NS, sl, TP + P:BLK], b[0:NS, TP:T], column(0, h, 2), 0.0, ALU.add, ALU.min), mix_dve)
                    eng.wait_ge(w_ready, hg + 1)
                else:
                    eng.wait_ge(exp_ready, hg + 1)
                wait_job(eng, f"{kind}sc{h}")
                b = mb(f"{kind}sc{h}")
                do(stt(out=Sp[:, sl, 0:TP + P], in0=b[:, 0:TP + P], scalar=KSCALE, in1=E[:, sl, 0:TP + P],
                       op0=ALU.mult, op1=ALU.mult))
                do(stt(out=Sp[0:NS, sl, TP + P:BLK], in0=b[0:NS, TP + P:BLK], scalar=KSCALE,
                       in1=E[0:NS, sl, TP + P:BLK], op0=ALU.mult, op1=ALU.mult), mix_dve)
                wait_job(eng, f"{kind}kn{h}")
                b = mb(f"{kind}kn{h}")
                if kind == "a":
                    wk = [column(0, 96 + h, g) for g in range(3)]
                else:
                    rk = const("retk")
                    wk = [rk[0:NS if g == 2 else P, g * CH + h:g * CH + h + 1] for g in range(3)]
                for g in range(2):
                    do(ts(kg[:, sl, g, :], b[:, g * P:(g + 1) * P], wk[g], None, ALU.mult))
                do(stt(out=kgm[0:NS], in0=bc(b[0:NS, TP:TP + P], 1, NB), scalar=wk[2],
                       in1=bc(mine[0:NS], 2, P), op0=ALU.mult, op1=ALU.mult), mix_dve)
                wait_job(eng, f"{kind}oi{h}")
                wq = column(0, 32 + h, 2) if kind == "a" else const("retq")[0:NS, h:h + 1]
                do(ts(inter[0:NS, 0:w], mb(f"{kind}oi{h}")[0:NS, 0:w], wq, None, ALU.mult), mix_dve)
                wait_job(eng, f"{kind}os{h}")
                settle()
                do(tt(num[0:NS, sl, 2, 0:w], mb(f"{kind}os{h}")[0:NS, 0:w], inter[0:NS, 0:w], ALU.add), mix_dve)
                for b_ in range(NB):
                    n = 2 * hg + b_ // 4
                    wait_job(eng, f"{kind}ss{h}.{b_}")
                    dec = adec[:, h, b_:b_ + 1] if kind == "a" else math.exp(LOG_GAMMA[h] * TS)
                    x = st[:, n % 3, b_ % 4, 0:w]
                    do(stt(out=x, in0=x, scalar=dec, in1=mb(f"{kind}ss{h}.{b_}")[:, 0:w],
                           op0=ALU.mult, op1=ALU.add), mix_dve)
                settle()
                wait_empty(eng, f"{kind}o1{h}")
                for g in range(3):
                    do(nc.vector.bn_stats(out=stats[0:NS if g == 2 else P, g, :], in_=num[0:NS if g == 2 else P, sl, g, 0:CV]))
                settle()
                for g in range(3):
                    do(nc.vector.bn_aggr(out=mv[0:NS if g == 2 else P, g, :], in_=stats[0:NS if g == 2 else P, g, :]))
                if kind == "a":
                    den = num[:, sl, :, AV]
                    do(stt(out=sm[:, 0, :], in0=den, scalar=-1.0, in1=den, op0=ALU.mult, op1=ALU.max))
                    settle()
                    do(tt(sm[:, 1, :], sm[:, 0, :], cols[:, :, 64 + h], ALU.max))
                    settle()
                    do(nc.vector.reciprocal(sm[:, 2, :], sm[:, 1, :]))
                    settle()
                    do(tt(sm[:, 3, :], mv[:, :, 1], sm[:, 2, :], ALU.mult))
                    settle()
                    do(tt(sm[:, 4, :], sm[:, 3, :], sm[:, 2, :], ALU.mult), var_ready)
                    eng.wait_ge(inv_ready, hg + 1)
                    do(tt(sm[:, 7, :], sm[:, 6, :], sm[:, 2, :], ALU.mult))
                else:
                    settle()
                    do(copy(sm[:, 4, :], mv[:, :, 1]), var_ready)
                    eng.wait_ge(inv_ready, hg + 1)
                    do(copy(sm[:, 7, :], sm[:, 6, :]))
                settle()
                for g in range(3):
                    n = NS if g == 2 else P
                    do(ts(num[0:n, sl, g, 0:CV], num[0:n, sl, g, 0:CV], mv[0:n, g, 0:1], sm[0:n, 7, g:g + 1],
                          ALU.subtract, ALU.mult), yn_ready if g == 2 else None)
                for i in range(2):
                    n = 2 * h + i
                    wait_job(eng, f"{kind}yt{n}")
                    if n >= 2:
                        eng.wait_ge(ylo_ready, (16 if kind == "r" else 0) + n - 1)
                    if kind == "a":
                        gate, gain = hF[:, n, :], v("ag", n)
                    else:
                        gate, gain = (gT[:, n, :] if n < 8 else hF[:, n - 8, :]), v("rg", n)
                    do(stt(out=yF[:, n % 2, :], in0=mb(f"{kind}yt{n}")[:, 0:T], scalar=gain, in1=gate,
                           op0=ALU.mult, op1=ALU.mult), mix_dve)
                for i in range(2):
                    n = 2 * h + i
                    eng.wait_ge(yhi_ready, (16 if kind == "r" else 0) + n + 1)
                    hi, lo = Y[n // 8]
                    do(tt(lo[:, n % 8, :], yF[:, n % 2, :], hi[:, n % 8, :].bitcast(F32), ALU.subtract), ylo_ready)

            def convolve(n, x, width, taps, bias):
                eng.wait_ge(fill_done, n + 1)
                y = cy[:, n % 4, 0:width]
                do(ts(y, x[:, 0:width], taps[0], bias, ALU.mult, ALU.add))
                for j in range(1, len(taps)):
                    settle()
                    do(stt(out=y, in0=x[:, j:j + width], scalar=taps[j], in1=y, op0=ALU.mult, op1=ALU.add),
                       conv_done if j == len(taps) - 1 else None)

            def ffn(l):
                norm(2 * l + 1)
                t0 = START[f"up{l}"]
                for j in range(KF + 2):
                    if j < KF:
                        for x in range(2):
                            i = 2 * j + x
                            n = XB + 2 * KF * l + i
                            split(last_chunk(t0 + i) + 3)
                            wait_tile_empty(eng, t0 + i)
                            if x == 0 and j >= 2:
                                eng.wait_ge(silu_done, XB + KF * l + j - 1)
                            convolve(n, pad[:, n % 4, 1:], 304,
                                     [v("fcw", (2 * KF * l + i) * 3 + d) for d in range(3)],
                                     v("fcb", 2 * KF * l + i))
                    if 1 <= j <= KF:
                        p, sl = j - 1, (j - 1) % 2
                        eng.wait_ge(silu_done, XB + KF * l + p + 1)
                        eng.wait_ge(conv_done, XB + 2 * KF * l + 2 * p + 2)
                        if p >= 3:
                            eng.wait_ge(hidlo_ready, KF * l + p - 2)
                        g, u, o = sgate[:, sl, :], cy[:, 2 * sl + 1, :], hidF[:, p % 3, :]
                        do(tt(o[:, 0:TP], g[:, 0:TP], u[:, 0:TP], ALU.mult))
                        do(tt(smp(o), padded(g, W2, -W2)[:, :, W2:], padded(u, W2, -W2)[:, :, W2:],
                              ALU.mult), hid_ready)
                    if j >= 2:
                        p = j - 2
                        eng.wait_ge(hidhi_ready, KF * l + p + 1)
                        do(tt(HL[:, p, :], hidF[:, p % 3, :], HH[:, p, :].bitcast(F32), ALU.subtract), hidlo_ready)
                out_tiles(f"down{l}", 2 * l + 1)

            def gate_rows(t):
                b = bank[t % 4]
                a4, b16 = slice(0, AH), slice(0, BH)
                li, fx, dx, f3, d4, lf, dt = (rows[a4, 0, :], rows[a4, 1, :], rows[b16, 2, :], rows[a4, 3, :],
                                              rows[b16, 4, :], rows[a4, 5, :], rows[b16, 6, :])
                wait_tile(eng, t)
                eng.wait_ge(const_in, 16)
                do(ts(li, b[0:AH, 0:T], v("igb", p=AH), None, ALU.add))
                do(ts(fx, b[32:32 + AH, 0:T], v("fgb", p=AH), None, ALU.add))
                do(ts(dx, b[64:64 + BH, 0:T], v("dtb", p=BH), None, ALU.add), gemm_dve)
                settle()
                do(stt(out=f3, in0=fx, scalar=-1.0, in1=fx, op0=ALU.mult, op1=ALU.min))
                do(stt(out=d4, in0=dx, scalar=-1.0, in1=dx, op0=ALU.mult, op1=ALU.min), row_dve)
                eng.wait_ge(row_act, 1)
                do(stt(out=lf, in0=fx, scalar=0.0, in1=f3, op0=ALU.min, op1=ALU.subtract))
                do(stt(out=dt, in0=dx, scalar=0.0, in1=d4, op0=ALU.max, op1=ALU.add))
                settle()
                do(copy(slab[32:32 + BH, 1, :], dt))
                do(ts(rows[b16, 7, :], dt, rsm[b16, 5, 0:1], -1.0, ALU.mult, ALU.mult))
                settle()
                kp, dp = resets[:, 0, :], resets[:, 1, :]
                eng.wait_ge(resets_in, 16)
                scan = nc.vector.tensor_tensor_scan
                cum = rows[a4, 8, :]
                do(scan(out=cum, data0=kp[a4], data1=lf, initial=0.0, op0=ALU.mult, op1=ALU.add))
                do(scan(out=ac[b16, :], data0=kp[b16], data1=rows[b16, 7, :], initial=0.0, op0=ALU.mult, op1=ALU.add))
                settle()
                do(copy(slab[b16, 1, :], ac[b16, :]))
                a = slab[a4, 0, :]
                do(tt(a, li, cum, ALU.subtract))
                settle()
                do(copy(li, a))
                settle()
                first = smp(li)[:, :, 0]
                do(tt(first, first, m0, ALU.max))
                settle()
                M = rows[a4, 1, :]
                do(scan(out=M, data0=dp[a4], data1=li, initial=0.0, op0=ALU.add, op1=ALU.max))
                settle()
                ends = rsm[a4, 0, 0:NB + 1]
                do(copy(ends[:, 0:1], M[:, TP - 1:TP]))
                do(copy(ends[:, 1:NB + 1], smp(M)[:, :, TS - 1]))
                do(ts(nM[a4, :], M, -1.0, None, ALU.mult))
                do(tt(rows[a4, 3, :], cum, M, ALU.add))
                settle()
                do(copy(rsm[a4, 1, 0:1], rows[a4, 3, TP - 1:TP]))
                do(copy(rsm[a4, 1, 1:NB + 1], smp(rows[a4, 3, :])[:, :, TS - 1]))
                do(tt(smp(rows[a4, 4, :]), bc(m0, 2, TS), smp(M), ALU.subtract))
                do(ts(rows[a4, 5, 0:TP], a[:, 0:TP], ends[:, 0:1], None, ALU.subtract))
                do(tt(smp(rows[a4, 5, :]), smp(a), bc(ends[:, 1:NB + 1], 2, TS), ALU.subtract))
                do(tt(rsm[a4, 2, 0:NB], m0, ends[:, 1:NB + 1], ALU.subtract))
                do(ts(rows[b16, 2, 0:TP], ac[b16, 0:TP], ac[b16, TP - 1:TP], None, ALU.subtract))
                do(tt(smp(rows[b16, 2, :]), smp(ac[b16, :]), bc(smp(ac[b16, :])[:, :, TS - 1], 2, TS), ALU.subtract), row_dve)
                eng.wait_ge(row_act, 2)
                do(ts(slab[96:96 + AH, 0, :], rows[a4, 5, :], KSCALE, None, ALU.mult))
                do(tt(dg[b16], bc(rsm[b16, 3, 0:NB], 2, BH), bc(ident[b16, 0:BH], 1, NB), ALU.mult), slab_ready)

            split(2)
            norm(0)
            for t in range(T0, START["even_out"]):
                kind, i = TILES[t][1:3]
                split(last_chunk(t) + 3)
                if kind == "gates":
                    eng.wait_ge(zeroed, 2)
                    gate_rows(t)
                if 10 <= t <= 17:
                    n = t - 10
                    if n == 0:
                        eng.wait_ge(zeroed, 2)
                    turned(f"v{n}", lambda g, p: vA[0:p, g, n // 2, (n % 2) * P:(n % 2) * P + P])
                if kind == "xbc" and i >= 1 or t == START["even_out"] - 1:
                    for m in ([i - 1] if t < START["even_out"] - 1 else [i - 1, i]):
                        wait_tile_empty(eng, XBC0 + m)
                        if m >= 4:
                            eng.wait_ge(silu_done, m - 3)
                        convolve(m, pad[:, m % 4, :], 312, [v("scw", m * 4 + d) for d in range(4)], v("scb", m))
            for c in range(2):
                turned(f"col{c}", lambda g, p: cols[0:p, g, c * P:(c + 1) * P])
            wait_job(eng, "adec")
            do(copy(adec[:], mb("adec")[:, 0:AH * NB].rearrange("p (h b) -> p h b", h=AH)), mix_dve)
            wait_job(eng, "sdec")
            do(copy(sdec[:], mb("sdec")[:, 0:NB * BH].rearrange("p (b h) -> p b h", b=NB)), mix_dve)
            settle()
            for h in range(AH):
                head("a", h, h, qT[:, h, :], kT[:, h, :], YA, AV + 1)
            eng.wait_ge(scratch_free, 1)
            for i in range(8):
                wait_job(eng, f"xn{i}")
                b = mb(f"xn{i}")
                dtc = cols[:, :, P + 32 + 2 * i:P + 32 + 2 * i + 2]
                for g in range(3):
                    n = NS if g == 2 else P
                    do(tt(xdt[0:n, g, i * P:(i + 1) * P].rearrange("p (h e) -> p h e", h=2),
                          b[0:n, g * P:(g + 1) * P].rearrange("p (h e) -> p h e", h=2),
                          bc(dtc[0:n, g, :], 2, BP), ALU.mult), mix_dve if g == 2 else None)
            for g in range(BG):
                wait_job(eng, f"cb{g}")
                b = mb(f"cb{g}")
                do(tt(cbm[:, g, 0:TP + P], b[:, 0:TP + P], mask[:, 0:TP + P], ALU.mult))
                do(tt(cbm[0:NS, g, TP + P:BLK], b[0:NS, TP + P:BLK], mask[0:NS, TP + P:BLK], ALU.mult), mix_dve)
            settle()
            for h in range(BH + 1):
                if h < BH:
                    wait_job(eng, f"sbc{h}")
                    if h >= 2:
                        wait_job(eng, f"say{h - 2}")
                    b, x = mb(f"sbc{h}"), E2[:, h % 2, :]
                    do(ts(x[:, 0:TP], b[:, 0:TP], column(1, h, 0), 0.0, ALU.subtract, ALU.min))
                    do(ts(x[:, TP:TP + P], b[:, P:TP], column(1, h, 1), 0.0, ALU.subtract, ALU.min))
                    do(ts(x[0:NS, TP + P:BLK], b[0:NS, TP:T], column(1, h, 2), 0.0, ALU.subtract, ALU.min), mix_dve)
                if h:
                    m = h - 1
                    eng.wait_ge(exp2_ready, m + 1)
                    x, c = E2[:, m % 2, :], cbm[:, m // HG, :]
                    do(tt(x[:, 0:TP + P], x[:, 0:TP + P], c[:, 0:TP + P], ALU.mult))
                    do(tt(x[0:NS, TP + P:BLK], x[0:NS, TP + P:BLK], c[0:NS, TP + P:BLK], ALU.mult), e_ready)
            wait_job(eng, f"say{BH - 1}")
            for g in range(3):
                n = NS if g == 2 else P
                x = xdt[0:n, g, :].rearrange("p (h e) -> p h e", h=BH)
                do(tt(x, x, bc(cols[0:n, g, P + 96:P + 96 + BH], 2, BP), ALU.mult), xw_ready if g == 2 else None)
            for g in range(BG):
                wait_job(eng, f"si{g}")
                r3 = lambda a: a.rearrange("p (h e) -> p h e", h=HG)
                do(tt(r3(itmp[0:NS, :]), r3(mb(f"si{g}")[0:NS, :]),
                      bc(cols[0:NS, 2, P + 64 + g * HG:P + 64 + (g + 1) * HG], 2, BP), ALU.mult), mix_dve)
                settle()
                wait_empty(eng, f"say{BH - 1}")
                y = yn[0:NS, 2, g * GW:(g + 1) * GW]
                do(tt(y, y, itmp[0:NS, :], ALU.add), ynat_ready)
                for b_ in range(NB):
                    wait_job(eng, f"su{g}.{b_}")
                    eng.wait_ge(dec_ready, g * NB + b_ + 1)
                    do(tt(sts[:, b_, :], mb(f"su{g}.{b_}")[:, :], sts[:, b_, :], ALU.add), mix_dve)
            for i in range(8):
                wait_job(eng, f"sy{i}")
                do(stt(out=ty[:, i % 2, :], in0=xbcT[:, i, :], scalar=v("D", i), in1=mb(f"sy{i}")[:, 0:T],
                       op0=ALU.mult, op1=ALU.add), mix_dve)
                settle()
                do(tt(zT[:, i, :], zT[:, i, :], ty[:, i % 2, :], ALU.mult), zq_ready)
            for i in range(8):
                eng.wait_ge(srs_ready, i // 4 + 1)
                do(stt(out=zT[:, i, :], in0=zT[:, i, :], scalar=v("sg", i), in1=rst2[:, i // 4, :],
                       op0=ALU.mult, op1=ALU.mult), yg_ready)
            for i in range(8):
                eng.wait_ge(yhi_ready, 8 + i + 1)
                do(tt(YL[:, i, :], zT[:, i, :], YH[:, i, :].bitcast(F32), ALU.subtract), ylo_ready)
            out_tiles("even_out", 0)
            ffn(0)
            norm(2)
            cos, sin = const("cos"), const("sin")
            for j in range(len(ODD)):
                t = START["odd"] + j
                kind, i = TILES[t][1:3]
                split(last_chunk(t) + 3)
                b = bank[t % 4]
                if kind in ("rq", "rk"):
                    wait_tile(eng, t)
                    if j >= 2:
                        eng.wait_ge(rope_ready, j - 1)
                    do(tt(E[:, j % 2, 0:T], b[:, 0:T], cos, ALU.mult))
                    do(tt(Sp[0:64, j % 2, 0:T], b[64:P, 0:T], sin[64:P], ALU.mult))
                    do(tt(Sp[64:P, j % 2, 0:T], b[0:64, 0:T], sin[0:64], ALU.mult), gemm_dve)
                if 18 <= j <= 33:
                    n = j - 18
                    turned(f"rv{n}", lambda g, p: rvA[0:p, g, n // 2, (n % 2) * P:(n % 2) * P + P])
            for h in range(CH):
                head("r", h, AH + h, rqT[:, h, :], rkT[:, h, :], YR, CV)
            out_tiles("odd_out", 2)
            ffn(1)
            norm(4)

        @block.gpsimd
        def _(eng):
            s = Steps(eng, pool_step)
            do, settle = s.do, s.settle
            tt, copy = nc.gpsimd.tensor_tensor, nc.gpsimd.tensor_copy

            eng.dma_start(sst[:], sconv).then_inc(sst_in, 16)
            eng.dma_start(fst[:], fconv).then_inc(fst_in, 16)
            do(nc.gpsimd.memset(pad[:], 0.0), zeroed)
            do(nc.gpsimd.memset(slab[:], 0.0))
            do(nc.gpsimd.memset(cols[:], 1.0))
            do(nc.gpsimd.memset(vA[:, :, :, AV:AV + 1], 1.0), zeroed)
            settle()

            def load(n):
                if n >= 3:
                    eng.wait_ge(st_out[n % 3], 16 * (n // 3))
                src, w = state_dram(n, False)
                eng.dma_start(st[:, n % 3, :, 0:w], src).then_inc(st_in[n % 3], 16)

            def zero_attention():
                do(nc.gpsimd.memset(num[:], 0.0))
                do(nc.gpsimd.memset(mv[:], 0.0), zeroed)

            def fill(n, x, kept, w):
                if n >= 4:
                    eng.wait_ge(conv_done, n - 3)
                do(copy(padded(x, w)[:, :, 0:w], kept), fill_done)

            def keep_rows(n, x, dst, w, t):
                wait_tile_empty(eng, t)
                do(copy(dst[:, 0:w], x[:, TP:TP + w]))
                do(copy(dst[:, w:(NB + 1) * w].rearrange("p (b r) -> p b r", b=NB), padded(x, w)[:, :, TS:TS + w]), tail_done)

            def head(kind, h, hg, q, w):
                sl = hg % 2
                if hg >= 2:
                    kk, hh, _ = HEADS[hg - 2]
                    wait_job(eng, f"{kk}oi{hh}")
                if kind == "r":
                    eng.wait_ge(rope_ready, h + 1)
                    if h == 0:
                        pass
                do(tt(qTm[:, sl], bc(q[:, TP:T], 1, NB), own, ALU.mult), qm_ready)
                if kind == "a":
                    eng.wait_ge(exp_ready, hg + 1)
                    do(tt(E[:, sl, 0:TP + P], E[:, sl, 0:TP + P], mask[:, 0:TP + P], ALU.mult))
                    do(tt(E[0:NS, sl, TP + P:BLK], E[0:NS, sl, TP + P:BLK], mask[0:NS, TP + P:BLK], ALU.mult), w_ready)
                wait_empty(eng, f"{kind}sp{h}")
                eng.dma_start(cp_out[h] if kind == "a" else rp_out[h], pout[:, sl, 0:w]).then_inc(pout_out[sl], 16)
                last = AH if kind == "a" else AH + CH
                for x in range(2):
                    n = 2 * hg + x
                    wait_empty(eng, f"{kind}ss{h}.{4 * x + 3}")
                    dst, _ = state_dram(n, True)
                    eng.dma_start(dst, st[:, n % 3, :, 0:w]).then_inc(st_out[n % 3], 16)
                    if n + 3 < 2 * last:
                        load(n + 3)

            def ffn(l):
                for i in range(2 * KF + 3):
                    n = XB + 2 * KF * l + i
                    if i < 2 * KF:
                        if l == 1 and i == 0:
                            eng.wait_ge(fout_out, 16)
                        fill(n, pad[:, n % 4, 1:], fst[:, l, i, :, :], W2)
                    if i >= 3:
                        m = i - 3
                        keep_rows(n - 3, pad[:, (n - 3) % 4, 1:], fout[:, m, :], W2, START[f"up{l}"] + m)
                eng.wait_ge(tail_done, XB + 2 * KF * (l + 1))
                eng.dma_start(f_out[l], fout[:]).then_inc(fout_out, 16)

            eng.wait_ge(sst_in, 16)
            eng.wait_ge(fst_in, 16)
            eng.wait_ge(const_in, 16)
            for i in range(XB + 3):
                if i < XB:
                    if i >= 4:
                        pass
                    fill(i, pad[:, i % 4, :], sst[:, i], W1)
                if i >= 3:
                    keep_rows(i - 3, pad[:, (i - 3) % 4, :], sout[:, i - 3, :], W1, XBC0 + i - 3)
            eng.wait_ge(slab_ready, 1)
            eng.dma_start(m_out, rsm[0:AH, 1, 0:NB + 1]).then_inc(small_out, 16)
            eng.wait_ge(tail_done, XB)
            eng.dma_start(sconv_out, sout[:]).then_inc(small_out, 16)
            wait_empty(eng, "sdec")
            zero_attention()
            for n in range(3):
                load(n)
            for h in range(AH):
                head("a", h, h, qT[:, h, :], AV + 1)
            eng.wait_ge(ylo_ready, 8)
            for i in range(3):
                eng.wait_ge(st_out[i], 16 * len(range(i, 2 * AH, 3)))
            for i in range(2):
                eng.wait_ge(pout_out[i], 16 * (AH // 2))
            for b in range(NB):
                eng.dma_start(sts[:, b, :], h_in[b][:, 0:GW]).then_inc(sts_in[b], 16)
            eng.wait_ge(silu_done, XB)
            for g in range(BG):
                do(tt(cm[:, g], bc(xbcT[:, 10 + g, TP:T], 1, NB), own, ALU.mult), scratch_free)
            for g in range(BG):
                wait_empty(eng, f"bn{g}")
                do(tt(bm[0:NS, :, g, :], bc(bnat[0:NS, 2, g, :], 1, NB), bc(mine[0:NS], 2, P), ALU.mult), bm_ready)
            for g in range(BG):
                wait_job(eng, f"si{g}")
                for b in range(NB):
                    x = sts[:, b, :].rearrange("p (h e) -> p h e", h=HG)
                    do(tt(x, x, bc(sdec[:, b, g * HG:(g + 1) * HG], 2, BP), ALU.mult), dec_ready)
                wait_empty(eng, f"sp{g}")
                eng.dma_start(hp_out[:, g * GW:(g + 1) * GW], pst[:, g, :]).then_inc(pst_out, 16)
                for b in range(NB):
                    wait_empty(eng, f"su{g}.{b}")
                    eng.dma_start(h_out[b][:, g * GW:(g + 1) * GW], sts[:, b, :]).then_inc(sts_out[b], 16)
                if g + 1 < BG:
                    for b in range(NB):
                        eng.wait_ge(sts_out[b], 16 * (g + 1))
                        eng.dma_start(sts[:, b, :], h_in[b][:, (g + 1) * GW:(g + 2) * GW]).then_inc(sts_in[b], 16)
            eng.wait_ge(pst_out, 16 * BG)
            eng.wait_ge(ylo_ready, 16)
            do(nc.gpsimd.memset(pad[:], 0.0), zeroed)
            settle()
            ffn(0)
            for j in range(2 * CH):
                i = j % CH
                wait_tile_empty(eng, START["odd"] + j)
                do(tt((rqT if j < CH else rkT)[:, i, :], E[:, j % 2, 0:T], Sp[:, j % 2, 0:T], ALU.add), rope_ready)
            zero_attention()
            for n in range(2 * AH, 2 * AH + 3):
                load(n)
            for h in range(CH):
                head("r", h, AH + h, rqT[:, h, :], CV)
            for i in range(3):
                eng.wait_ge(st_out[i], 16 * len(range(i, 2 * (AH + CH), 3)))
            for i in range(2):
                eng.wait_ge(pout_out[i], 16 * ((AH + CH) // 2))
            eng.wait_ge(ylo_ready, 32)
            do(nc.gpsimd.memset(pad[:], 0.0), zeroed)
            settle()
            ffn(1)
            eng.wait_ge(fout_out, 32)
            eng.wait_ge(small_out, 32)
            for b in range(NB):
                eng.wait_ge(sts_out[b], 16 * BG)


def constants():
    c = np.zeros((P, CONST_W), np.float32)

    def put(name, a):
        at, w = CONSTS[name]
        c[:a.shape[0], at:at + w] = a.reshape(a.shape[0], -1)

    key, query = np.arange(P)[:, None], np.arange(TP)[None, :]
    ns = np.arange(NS)
    put("ident", np.eye(P))
    put("ones", np.ones((P, P)))
    gap = np.full((P, BLK), -1.0)
    gap[:, 0:TP] = query - key
    gap[:, TP:TP + P] = query[:, :P] - key
    same = ns[:, None] // TS == ns[None, :] // TS
    gap[:NS, TP + P:] = np.where(same, ns[None, :] - ns[:, None], -1)
    put("mask", (gap >= 0).astype(np.float32))
    put("dist", np.where(gap >= 0, gap, 1e9))
    put("own", np.broadcast_to(np.arange(NB)[:, None] == ns[None, :] // TS, (P, NB, NS)))
    put("mine", ns[:, None] // TS == np.arange(NB)[None, :])
    inv = (np.float32(10000.0) ** (-np.arange(64, dtype=np.float32) / np.float32(64))).astype(np.float32)
    pos = np.concatenate([np.arange(TP), 2048 + ns % TS]).astype(np.float32)
    angle = (pos[None, :] * inv[:, None]).astype(np.float32).astype(np.float64)
    put("cos", np.concatenate([np.cos(angle)] * 2))
    put("sin", np.concatenate([np.sin(angle), -np.sin(angle)]))
    lg = np.array(LOG_GAMMA)[None, :]
    rk = np.zeros((P, 3, CH))
    for g in range(2):
        rk[:, g] = np.exp(lg * (TP - 1 - g * P - np.arange(P))[:, None])
    rk[:NS, 2] = np.exp(lg * (TS - 1 - ns % TS)[:, None])
    put("retk", rk * KSCALE)
    put("retq", np.exp(lg * (ns % TS + 1)[:, None]))
    return c


def starts():
    first = np.zeros(T)
    first[0] = 1
    first[TP::TS] = 1
    drop = -1e30 * first
    drop[0] = 0
    return np.broadcast_to(np.stack([1 - first, drop]).astype(np.float32), (BH, 2, T))


def kernel(**inputs):
    import concourse.bacc as bacc
    from concourse.bass_utils import run_bass_kernel_spmd

    a = {k: np.asarray(x) for k, x in inputs.items()}

    def tiled(x):
        return np.moveaxis(x.reshape(*x.shape[:-1], -1, P), -1, 0)

    def paired(x):
        n = x.shape[:-1]
        return np.swapaxes(x.reshape(*n, 2, KF, P), -3, -2).reshape(*n, 2 * KF * P)

    tokens = np.concatenate([a["x_prompt"].reshape(TP, D), a["x_sample"].reshape(NS, D)])
    xin = np.ascontiguousarray(np.swapaxes(tiled(tokens), 1, 2))

    def weight_tiles(w):
        k, n = w.shape
        return w.reshape(k // P, P, n // P, P).transpose(2, 0, 1, 3).reshape(-1, P, P)

    w = a["even_w_in"][0]
    gates = np.zeros((D, P), np.float32)
    gates[:, 0:AH] = w[:, 2048:2052]
    gates[:, 32:32 + AH] = w[:, 2052:2056]
    gates[:, 64:64 + BH] = w[:, 5640:5656]
    w_even = np.concatenate([w[:, :2048], gates, w[:, 2056:5640]], axis=1)
    streams = [weight_tiles(w_even), weight_tiles(a["even_w_out"][0]),
               weight_tiles(paired(a["ffn_w_up"][0])), weight_tiles(a["ffn_w_down"][0]),
               weight_tiles(a["odd_w_in"][0]), weight_tiles(a["odd_w_out"][0]),
               weight_tiles(paired(a["ffn_w_up"][1])), weight_tiles(a["ffn_w_down"][1])]
    wts = np.concatenate(streams).reshape(CHUNKS, CHUNK, P, P).transpose(0, 2, 1, 3).reshape(CHUNKS, P, CHUNK * P)

    vecs = np.zeros((P, VEC_W), np.float32)

    def put(name, x):
        at, n = VECS[name]
        vecs[:x.shape[0], at:at + n] = x.reshape(x.shape[0], -1)

    for i, g in enumerate((a["norm_mix_g"][0], a["norm_ffn_g"][0], a["norm_mix_g"][1], a["norm_ffn_g"][1],
                           a["norm_final_g"])):
        put(f"norm{i}", tiled(g))
    put("ag", tiled(a["mlstm_norm_g"][0]))
    put("scw", np.swapaxes(tiled(a["ssd_conv_w"][0]), 1, 2))
    put("scb", tiled(a["ssd_conv_b"][0]))
    put("D", tiled(np.repeat(a["ssd_D"][0], BP)))
    put("sg", tiled(a["ssd_norm_g"][0]))
    put("rg", tiled(a["ret_norm_g"][0]))
    put("fcw", np.swapaxes(tiled(paired(a["ffn_conv_w"])), 2, 3))
    put("fcb", tiled(paired(a["ffn_conv_b"])))
    for name, x in (("igb", a["mlstm_igate_b"]), ("fgb", a["mlstm_fgate_b"]), ("dtb", a["ssd_dt_bias"]),
                    ("alog", a["ssd_A_log"])):
        put(name, x[0][:, None])
    put("m0", a["state_mlstm_m"][0].T)
    vecs[:, VECS["eps"][0]] = EPS

    sconv = np.ascontiguousarray(tiled(a["state_ssd_conv"][0]).transpose(0, 3, 1, 2))
    fconv = np.ascontiguousarray(tiled(paired(a["state_ffn_conv"])).transpose(0, 1, 4, 2, 3))
    c_in = np.concatenate([a["state_mlstm_C"][0], a["state_mlstm_n"][0][..., None]], axis=-1).transpose(1, 2, 0, 3)
    r_in = a["state_ret_S"][0].transpose(1, 2, 0, 3)
    h_in = a["state_ssd_h"][0].reshape(NB, BH * BP, P).transpose(0, 2, 1)
    ins = {"xin": xin, "wts": wts, "consts": constants(), "starts": starts(), "vecs": vecs, "sconv": sconv, "fconv": fconv,
           "c_in": c_in, "r_in": r_in, "h_in": h_in}
    outs = {"y_out": (P, KD, T), "c_out": (AH, P, NB, AV + 1), "cp_out": (AH, P, AV + 1), "m_out": (AH, NB + 1),
            "sconv_out": (P, XB, 27), "h_out": (NB, P, D), "hp_out": (P, D), "r_out": (CH, P, NB, CV),
            "rp_out": (CH, P, CV), "f_out": (2, P, 2 * KF, 18)}
    ins = {k: np.ascontiguousarray(x) for k, x in ins.items()}
    nc = bacc.Bacc("TRN2", target_bir_lowering=False, num_devices=1)
    args = [nc.dram_tensor(k, x.shape, F32, kind="ExternalInput").ap() for k, x in ins.items()]
    args += [nc.dram_tensor(k, s, F32, kind="ExternalOutput").ap() for k, s in outs.items()]
    build(nc, *args)
    r = run_bass_kernel_spmd(nc, [ins], core_ids=[0]).results[0]

    def untiled(x):
        return np.moveaxis(x, 0, -1).reshape(*x.shape[1:-1], -1)

    def unpaired(x):
        return np.swapaxes(x.reshape(*x.shape[:-1], KF, 2, P), -3, -2).reshape(x.shape)

    y = untiled(np.swapaxes(r["y_out"], 1, 2))
    c = r["c_out"].transpose(2, 0, 1, 3)
    cp = r["cp_out"]
    m = r["m_out"]
    sc = untiled(np.swapaxes(r["sconv_out"], 1, 2))
    fc = unpaired(untiled(r["f_out"].transpose(1, 0, 3, 2)))
    h = r["h_out"].transpose(0, 2, 1).reshape(NB, BH, BP, P)
    hp = r["hp_out"].T.reshape(1, BH, BP, P)
    return (y[:TP].reshape(1, TP, D), y[TP:].reshape(NB, TS, D),
            cp[None, None, ..., :AV], cp[None, None, ..., AV], m[:, 0][None, None],
            sc[:W1][None, None], hp[None], r["rp_out"][None, None], fc[:, :W2][:, None],
            c[None, ..., :AV], c[None, ..., AV], m[:, 1:].T[None],
            sc[W1:].reshape(1, NB, W1, -1), h[None], r["r_out"].transpose(2, 0, 1, 3)[None],
            fc[:, W2:].reshape(2, NB, W2, -1))
```

```python
import math
from contextlib import ExitStack

import numpy as np

import concourse.bass as bass
from concourse import mybir

F32 = mybir.dt.float32
F32R = mybir.dt.float32r
ALU = mybir.AluOpType
ACT = mybir.ActivationFunctionType

P = 128
D = 1024
KD = D // P
TP, NB, TS = 256, 8, 4
NS = NB * TS
T = TP + NS
EPS = 1e-6
AH, AV = 4, 256
CH, CV = 8, 256
BH, BP, BG = 16, 64, 2
HG = BH // BG
GW = HG * BP
KSCALE = P ** -0.5
FF = 2816
KF = FF // P
XB = 12
W1, W2 = 3, 2
CHUNK = 8
RING = 4
SLOTS = 5
SSLOTS = 11
BLK = 2 * P + P + NS
LOG_GAMMA = [math.log1p(-2.0 ** (-5.0 - h)) for h in range(CH)]

EVEN = [("q", i) for i in range(AH)] + [("k", i) for i in range(AH)] + [("v", i) for i in range(8)] \
    + [("gates", 0)] + [("og", i) for i in range(8)] + [("z", i) for i in range(8)] \
    + [("xbc", i) for i in range(XB)]
ODD = [("rq", i) for i in range(CH)] + [("rk", i) for i in range(CH)] + [("rv", i) for i in range(16)] \
    + [("rg", i) for i in range(16)]
UP = [("up", i) for i in range(2 * KF)]
OUT = [("out", i) for i in range(KD)]
PHASES = [("even", EVEN, KD), ("even_out", OUT, 16), ("up0", UP, KD), ("down0", OUT, KF),
          ("odd", ODD, KD), ("odd_out", OUT, 16), ("up1", UP, KD), ("down1", OUT, KF)]


def plan_tiles():
    tiles, start, at = [], {}, 0
    for phase, kinds, k in PHASES:
        start[phase] = len(tiles)
        for kind, i in kinds:
            tiles.append((phase, kind, i, k, at))
            at += k
    assert at % CHUNK == 0
    return tiles, start, at // CHUNK


TILES, START, CHUNKS = plan_tiles()
BY_DVE = ("gates", "out", "rq", "rk")


def last_chunk(t):
    return (TILES[t][4] + TILES[t][3] - 1) // CHUNK


def emptied_by(t):
    return "dve" if TILES[t][1] in BY_DVE else "act"


EMPTIED = []
for _t in range(len(TILES)):
    EMPTIED.append(1 + sum(emptied_by(u) == emptied_by(_t) for u in range(_t)))

JOBS = []


def _jobs():
    def job(name, by):
        JOBS.append((name, by))

    def front(kind, h):
        job(f"{kind}sc{h}", "dve")
        job(f"{kind}kn{h}", "dve")

    def heads(kind, n, tail=()):
        if kind == "a":
            job("abc0", "act")
            job("abc1", "act")
        front(kind, 0)
        for h in range(n):
            if kind == "a" and h + 2 < n:
                job(f"abc{h + 2}", "act")
            if h + 1 < n:
                front(kind, h + 1)
            job(f"{kind}o0{h}", "act")
            job(f"{kind}o1{h}", "act")
            job(f"{kind}sp{h}", "act")
            if h:
                turned_back(kind, h - 1)
            job(f"{kind}oi{h}", "dve")
            job(f"{kind}os{h}", "dve")
            for b in range(NB):
                job(f"{kind}ss{h}.{b}", "dve")
        for name in tail:
            job(name, "dve")
        turned_back(kind, n - 1)

    def turned_back(kind, h):
        for i in range(2):
            job(f"{kind}yt{2 * h + i}", "dve")

    job("norm0", "act")
    for i in range(8):
        job(f"v{i}", "dve")
    for name in ("col0", "col1", "adec", "sdec"):
        job(name, "dve")
    heads("a", AH, [f"xn{i}" for i in range(8)])
    for g in range(BG):
        job(f"bn{g}", "act")
    for g in range(BG):
        job(f"cb{g}", "dve")
    job("sbc0", "act")
    job("sbc1", "act")
    for h in range(BH):
        if h + 2 < BH:
            job(f"sbc{h + 2}", "act")
        job(f"say{h}", "dve")
    job("si0", "dve")
    job("sp0", "act")
    job("sp1", "act")
    for b in range(NB):
        job(f"su0.{b}", "dve")
    job("si1", "dve")
    for b in range(NB):
        job(f"su1.{b}", "dve")
    for i in range(8):
        job(f"sy{i}", "dve")
    for g in range(BG):
        job(f"sn{g}", "act")
    job("norm1", "act")
    job("norm2", "act")
    for i in range(16):
        job(f"rv{i}", "dve")
    heads("r", CH)
    job("norm3", "act")
    job("norm4", "act")


_jobs()
JOB = {name: n for n, (name, _) in enumerate(JOBS)}
JOB_EMPTIED = [1 + sum(by == JOBS[n][1] for _, by in JOBS[:n]) for n in range(len(JOBS))]

CONSTS = {}
_at = 0
for _name, _w in (("ident", P), ("ones", P), ("drop", BLK), ("dist", BLK), ("own", NB * NS), ("mine", NB),
                  ("cos", T), ("sin", T), ("retk", 3 * CH), ("retq", CH)):
    CONSTS[_name] = (_at, _w)
    _at += _w
CONST_W = _at
VECS = {}
_at = 0
for _name, _w in (("norm0", 8), ("norm1", 8), ("norm2", 8), ("norm3", 8), ("norm4", 8), ("ag", 8),
                  ("scw", XB * 4), ("scb", XB), ("D", 8), ("sg", 8), ("rg", 16), ("fcw", 2 * 44 * 3),
                  ("fcb", 2 * 44), ("igb", 1), ("fgb", 1), ("dtb", 1), ("alog", 1), ("m0", NB), ("eps", 1)):
    VECS[_name] = (_at, _w)
    _at += _w
VEC_W = _at


CHUNK_READ = []
_mid = 0
for _c in range(CHUNKS):
    _end = (_c + 1) * CHUNK
    _t = next(t for t in range(len(TILES)) if TILES[t][4] + TILES[t][3] >= _end)
    if TILES[_t][4] + TILES[_t][3] == _end:
        CHUNK_READ.append(("tile", _t + 1))
    else:
        _mid += 1
        CHUNK_READ.append(("mid", _mid))


def build(nc, xin, wts, consts, starts, vecs, sconv, fconv, c_in, r_in, h_in,
          y_out, c_out, cp_out, m_out, sconv_out, h_out, hp_out, r_out, rp_out, f_out):
    ctx = ExitStack()
    with ctx:
        words = nc.sbuf_bytes_remaining // 4 - 32
        at0 = nc.sbuf_base
        ctx.enter_context(nc.sbuf_tensor("arena", [P, words], F32))
        top = at0 + 4 * words

        class Area:

            def __init__(self, at):
                self.at = (at + 31) // 32 * 32

            def take(self, name, shape, dt=F32):
                t = nc.alloc_sbuf_tensor_at(name, shape, dt, offset=self.at)
                self.at += (int(np.prod(shape[1:])) * 4 + 31) // 32 * 32
                assert self.at <= top, name
                return t

        keep = Area(at0)
        xT = keep.take("xT", [P, KD, T])
        hH = keep.take("hH", [P, KD, T], F32R)
        hL = keep.take("hL", [P, KD, T], F32R)
        hF = keep.take("hF", [P, KD, T])
        raw = keep.take("raw", [P, RING, CHUNK * P])
        wh = keep.take("wh", [P, RING, CHUNK * P], F32R)
        wl = keep.take("wl", [P, RING, CHUNK * P], F32R)
        cst = keep.take("cst", [P, CONST_W])
        vec = keep.take("vec", [P, VEC_W])
        sst = keep.take("sst", [P, XB, NB, W1])
        fst = keep.take("fst", [P, 2, 2 * KF, NB, W2])
        fout = keep.take("fout", [P, 2 * KF, (NB + 1) * W2])
        sout = keep.take("sout", [P, XB, (NB + 1) * W1])
        rstd = keep.take("rstd", [P, T])

        conv = Area(keep.at)
        pad = conv.take("pad", [P, 4, 320])
        cy = conv.take("cy", [P, 4, 312])
        ffn = Area(conv.at)
        sgate = ffn.take("sgate", [P, 2, 312])
        hidF = ffn.take("hidF", [P, 3, T])
        HH = ffn.take("HH", [P, KF, T], F32R)
        HL = ffn.take("HL", [P, KF, T], F32R)

        att = Area(conv.at)
        E = att.take("E", [P, 2, BLK])
        Sp = att.take("Sp", [P, 2, BLK])
        qTm = att.take("qTm", [P, 2, NB, NS])
        kg = att.take("kg", [P, 2, 2, P])
        kgm = att.take("kgm", [P, NB, P])
        at_num = att.at
        num = att.take("num", [P, 2, 3, AV + 1])
        at_pout = att.at
        pout = att.take("pout", [P, 2, AV + 1])
        vT = nc.alloc_sbuf_tensor_at("vT", [P, 2, T], F32, offset=att.at)
        yF = att.take("yF", [P, 2, T])
        kgs = att.take("kgs", [P, P])
        stats = att.take("stats", [P, 3, 6])
        mv = att.take("mv", [P, 3, 2])
        sm = att.take("sm", [P, 8, 3])
        st = [att.take(f"st{i}", [P, 4, AV + 1]) for i in range(3)]
        early = Area(keep.at)
        st_a = st + [early.take(f"st{i}", [P, 4, AV + 1]) for i in (3, 4)]
        assert early.at <= conv.at

        ml = Area(att.at)
        qT = ml.take("qT", [P, AH, T])
        kT = ml.take("kT", [P, AH, T])
        vA = ml.take("vA", [P, 3, AH, AV + 1])
        y2 = Area(att.at)
        YH = y2.take("YH", [P, 8, T], F32R)
        YL = y2.take("YL", [P, 8, T], F32R)
        even = Area(max(ml.at, y2.at))
        xbcT = even.take("xbcT", [P, XB, T])
        zT = even.take("zT", [P, 8, T])
        cols = even.take("cols", [P, 3, 2 * P])
        adec = even.take("adec", [P, AH, NB])
        sdec = even.take("sdec", [P, NB, BH])
        nM = even.take("nM", [P, T])
        drop = even.take("drop", [P, BLK], F32R)
        identR = even.take("identR", [P, P], F32R)
        ac = even.take("ac", [P, T])
        rsm = even.take("rsm", [P, 6, 16])

        rw = Area(conv.at)
        slab = rw.take("slab", [P, 2, T])
        rows = rw.take("rows", [P, 9, T])
        dg = rw.take("dg", [P, NB, BH])
        resets = rw.take("resets", [P, 2, T])
        assert rw.at <= at_pout

        sd = Area(keep.at)
        cm = sd.take("cm", [P, BG, NB, NS])
        bnat = sd.take("bnat", [P, 3, BG, P])
        ty = sd.take("ty", [P, 2, T])
        itmp = sd.take("itmp", [P, GW])
        assert sd.at <= conv.at
        sd = Area(conv.at)
        xdt = sd.take("xdt", [P, 3, D])
        rst2 = sd.take("rst2", [P, BG, T])
        assert sd.at <= at_num
        sd = Area(at_num)
        bm = sd.take("bm", [P, NB, BG, P])
        sts = [sd.take(f"sts{i}", [P, GW])[:] for i in range(SSLOTS - 4)]
        sts += [hF[:, 2 * i:2 * i + 2, :].rearrange("p a t -> p (a t)")[:, 0:GW] for i in range(4)]
        assert sd.at <= att.at
        sd = Area(att.at)
        pst = nc.alloc_sbuf_tensor_at("pst", [P, 2, GW], F32, offset=sd.at)
        E2 = sd.take("E2", [P, 3, BLK])
        cbm = sd.take("cbm", [P, BG, BLK])
        yn = sd.take("yn", [P, 3, D])
        assert sd.at <= ml.at

        odd = Area(att.at)
        rqT = odd.take("rqT", [P, CH, T])
        rkT = odd.take("rkT", [P, CH, T])
        rvA = odd.take("rvA", [P, 3, CH, CV])
        st_r = st + [odd.take(f"st{i}r", [P, 4, AV + 1]) for i in (3, 4)]
        gT = nc.alloc_sbuf_tensor_at("gT", [P, 8, T], F32, offset=keep.at)
        y3 = Area(att.at)
        RH = y3.take("RH", [P, 8, T], F32R)
        RL = y3.take("RL", [P, 8, T], F32R)

        def const(name):
            at, w = CONSTS[name]
            return cst[:, at:at + w]

        def v(name, i=0, p=P):
            return vec[0:p, VECS[name][0] + i:VECS[name][0] + i + 1]

        ident, ones, dist = (const(n) for n in ("ident", "ones", "dist"))
        own = const("own").rearrange("p (b l) -> p b l", b=NB)
        mine = const("mine")
        m0 = vec[0:AH, VECS["m0"][0]:VECS["m0"][0] + NB]

        bank = [ctx.enter_context(nc.psum_tensor(f"gemm{i}", [P, 512], F32)) for i in range(4)]
        mixb = [ctx.enter_context(nc.psum_tensor(f"mix{i}", [P, 512], F32)) for i in range(4)]

        def mb(name):
            return mixb[JOB[name] % 4]

        def sem(name):
            return ctx.enter_context(nc.semaphore(name))

        resets_in, kgm_ready, cm_ready = sem("resets_in"), sem("kgm_ready"), sem("cm_ready")
        x_in, const_in, vec_in, sst_in, fst_in = (sem(n) for n in ("x_in", "const_in", "vec_in", "sst_in", "fst_in"))
        raw_in = [sem(f"raw_in{i}") for i in range(RING)]
        st_in = [sem(f"st_in{i}") for i in range(SLOTS)]
        st_out = [sem(f"st_out{i}") for i in range(SLOTS)]
        sts_in = [sem(f"sts_in{i}") for i in range(SSLOTS)]
        sts_out = [sem(f"sts_out{i}") for i in range(SSLOTS)]
        pout_out = [sem(f"pout_out{i}") for i in range(2)]
        pst_out, fout_out, small_out, y_stored = (sem(n) for n in ("pst_out", "fout_out", "small_out", "y_stored"))
        act_step, dve_step, pool_step = sem("act_step"), sem("dve_step"), sem("pool_step")
        hi_ready, lo_ready, mid_read = sem("hi_ready"), sem("lo_ready"), sem("mid_read")
        gemm_done, mix_done = sem("gemm_done"), sem("mix_done")
        gemm_act, gemm_dve = sem("gemm_act"), sem("gemm_dve")
        mix_act, mix_dve = sem("mix_act"), sem("mix_dve")
        x_ready, sq_ready, rstd_ready = sem("x_ready"), sem("sq_ready"), sem("rstd_ready")
        h_ready, xhi_ready, xlo_ready = sem("h_ready"), sem("xhi_ready"), sem("xlo_ready")
        zeroed, fill_done, tail_done, conv_done = (sem(n) for n in ("zeroed", "fill_done", "tail_done", "conv_done"))
        silu_done, hid_ready, hidhi_ready, hidlo_ready = (sem(n) for n in ("silu_done", "hid_ready", "hidhi_ready", "hidlo_ready"))
        row_dve, row_act, slab_ready = sem("row_dve"), sem("row_act"), sem("slab_ready")
        exp_ready, drop_ready, qm_ready = sem("exp_ready"), sem("drop_ready"), sem("qm_ready")
        var_ready, inv_ready, yn_ready = sem("var_ready"), sem("inv_ready"), sem("yn_ready")
        yhi_ready, ylo_ready = sem("yhi_ready"), sem("ylo_ready")
        bm_ready, exp2_ready, e_ready, xw_ready = (sem(n) for n in ("bm_ready", "exp2_ready", "e_ready", "xw_ready"))
        dec_ready, ynat_ready = sem("dec_ready"), sem("ynat_ready")
        zq_ready, sq2_ready, srs_ready, yg_ready = (sem(n) for n in ("zq_ready", "sq2_ready", "srs_ready", "yg_ready"))
        rope_ready, y_ready = sem("rope_ready"), sem("y_ready")

        class Steps:

            def __init__(self, eng, own_sem):
                self.eng, self.own, self.count, self.last = eng, own_sem, {}, None

            def do(self, ins, s=None):
                s = self.own if s is None else s
                self.count[s.name] = self.count.get(s.name, 0) + 1
                ins.then_inc(s, 1)
                self.last = (s, self.count[s.name])

            def settle(self):
                self.eng.wait_ge(*self.last)

        def wait_tile(eng, t):
            eng.wait_ge(gemm_done, t + 1)

        def wait_tile_empty(eng, t):
            eng.wait_ge(gemm_act if emptied_by(t) == "act" else gemm_dve, EMPTIED[t])

        def wait_job(eng, name):
            eng.wait_ge(mix_done, JOB[name] + 1)

        def wait_empty(eng, name):
            n = JOB[name]
            eng.wait_ge(mix_act if JOBS[n][1] == "act" else mix_dve, JOB_EMPTIED[n])

        def wait_read(eng, c):
            kind, n = CHUNK_READ[c]
            eng.wait_ge(gemm_done if kind == "tile" else mid_read, n)

        def smp(ap):
            return ap[:, TP:T].rearrange("p (b t) -> p b t", b=NB)

        def padded(ap, w, at=0):
            s = at + w + TP
            return ap[:, s:s + NB * (w + TS)].rearrange("p (b t) -> p b t", b=NB)

        def bc(ap, axis, n):
            a = ap.unsqueeze(axis)
            return a.broadcast_to([*a.shape[:axis], n, *a.shape[axis + 1:]])

        YA = ((hH, hL), (YH, YL))
        YR = ((hH, hL), (RH, RL))
        T0 = START["even"]
        XBC0 = T0 + 33

        HEADS = [("a", h, h) for h in range(AH)] + [("r", h, AH + h) for h in range(CH)]

        def state_dram(n, out):
            hg, x = divmod(n, 2)
            kind, h, _ = HEADS[hg]
            t = (c_out if out else c_in) if kind == "a" else (r_out if out else r_in)
            w = AV + 1 if kind == "a" else CV
            return t[h][:, 4 * x:4 * x + 4, :], w

        def state(n):
            return (st_a if HEADS[n // 2][0] == "a" else st_r)[n % SLOTS]

        block = ctx.enter_context(nc.Block())

        @block.sync
        def _(sp):
            sp.dma_start(xT[:], xin).then_inc(x_in, 16)
            sp.dma_start(vec[:], vecs).then_inc(vec_in, 16)
            sp.dma_start(cst[:], consts).then_inc(const_in, 16)
            sp.dma_start(resets[0:BH], starts).then_inc(resets_in, 16)
            for c in range(CHUNKS):
                if c >= RING:
                    sp.wait_ge(lo_ready, c - RING + 1)
                sp.dma_start(raw[:, c % RING, :], wts[c]).then_inc(raw_in[c % RING], 16)
            sp.wait_ge(y_ready, KD)
            sp.dma_start(y_out, hF[:]).then_inc(y_stored, 16)
            sp.wait_ge(y_stored, 16)

        @block.tensor
        def _(pe):
            mm = nc.tensor.matmul

            def tile(t, rhs, operand=None):
                _, kind, _, K, w0 = TILES[t]
                if t >= 4:
                    wait_tile_empty(pe, t - 4)
                out = bank[t % 4][:, 0:T]
                for k in range(K):
                    c, pos = divmod(w0 + k, CHUNK)
                    if k == 0 or pos == 0:
                        pe.wait_ge(lo_ready, c + 1)
                    if operand is not None:
                        pe.wait_ge(operand[0], operand[1] + k + 1)
                    xh, xl = rhs(k)
                    h = wh[:, c % RING, pos * P:(pos + 1) * P]
                    lo = wl[:, c % RING, pos * P:(pos + 1) * P]
                    mm(out, h, xh, start=(k == 0), stop=False)
                    mm(out, h, xl, start=False, stop=False)
                    last = mm(out, lo, xh, start=False, stop=(k == K - 1))
                    if pos == CHUNK - 1 and k < K - 1:
                        last.then_inc(mid_read, 1)
                last.then_inc(gemm_done, 1)

            turn_of = [0]

            def free_bank(name):
                n = JOB[name]
                assert n == turn_of[0], name
                turn_of[0] += 1
                if n >= 4:
                    wait_empty(pe, JOBS[n - 4][0])
                return mb(name)

            def norm(n):
                out = free_bank(f"norm{n}")[:, 0:T]
                for i in range(KD):
                    pe.wait_ge(sq_ready, KD * n + i + 1)
                    last = mm(out, ones, hF[:, i, :], start=(i == 0), stop=(i == KD - 1))
                last.then_inc(mix_done, 1)

            def normed(k):
                return hH[:, k, :], hL[:, k, :]

            def turn(name, src):
                out = free_bank(name)
                for g, (a, n) in enumerate(((0, P), (P, P), (TP, NS))):
                    last = nc.tensor.transpose(out[0:n, g * P:(g + 1) * P], src[:, a:a + n], ident)
                last.then_inc(mix_done, 1)

            def turn_back(name, src):
                out = free_bank(name)
                for g, (a, n) in enumerate(((0, P), (P, P), (TP, NS))):
                    last = nc.tensor.transpose(out[:, a:a + n], src(g)[0:n], ident[0:n, 0:n])
                last.then_inc(mix_done, 1)

            def scores(out, k, q):
                mm(out[:, 0:TP], k[:, 0:P], q[:, 0:TP], start=True, stop=True)
                mm(out[:, TP:TP + P], k[:, P:TP], q[:, P:TP], start=True, stop=True)
                return mm(out[0:NS, TP + P:BLK], k[:, TP:T], q[:, TP:T], start=True, stop=True)

            def log_rows(name, rows, n, h):
                out = free_bank(name)
                one = ident[0:n, h:h + 1].broadcast_to([n, P])
                mm(out[:, 0:BLK], identR[:], drop[:], start=True, stop=False)
                mm(out[:, 0:TP], one, rows[0:n, 0:TP], start=False, stop=False)
                mm(out[:, TP:BLK], one, rows[0:n, P:T], start=False, stop=True).then_inc(mix_done, 1)

            def row_max(h):
                log_rows(f"abc{h}", nM, AH, h)

            def front(kind, h, qk):
                q, k = qk(h)
                if kind == "r":
                    pe.wait_ge(rope_ready, CH + h + 1)
                out = free_bank(f"{kind}sc{h}")
                scores(out, k, q).then_inc(mix_done, 1)
                turn(f"{kind}kn{h}", k)

            def middle(kind, h, hg, va, w):
                s = Sp[:, hg % 2, :]
                wait_empty(pe, f"{kind}kn{h}")
                out = free_bank(f"{kind}o0{h}")
                mm(out[:, 0:w], s[:, 0:P], va(0), start=True, stop=True).then_inc(mix_done, 1)
                out = free_bank(f"{kind}o1{h}")
                mm(out[:, 0:w], s[:, P:TP], va(0), start=True, stop=False)
                mm(out[:, 0:w], s[:, TP:TP + P], va(1), start=False, stop=True).then_inc(mix_done, 1)
                out = free_bank(f"{kind}sp{h}")
                mm(out[:, 0:w], kg[:, hg % 2, 0, :], va(0), start=True, stop=False)
                mm(out[:, 0:w], kg[:, hg % 2, 1, :], va(1), start=False, stop=True).then_inc(mix_done, 1)
                if h:
                    back(kind, h - 1, hg - 1)
                out = free_bank(f"{kind}oi{h}")
                pe.wait_ge(qm_ready, hg + 1)
                for b in range(NB):
                    n = 2 * hg + b // 4
                    pe.wait_ge(st_in[n % SLOTS], 16 * (n // SLOTS + 1))
                    last = mm(out[0:NS, 0:w], qTm[:, hg % 2, b, :], state(n)[:, b % 4, 0:w],
                              start=(b == 0), stop=(b == NB - 1))
                last.then_inc(mix_done, 1)
                out = free_bank(f"{kind}os{h}")
                mm(out[0:NS, 0:w], s[0:NS, TP + P:BLK], va(2)[0:NS], start=True, stop=True).then_inc(mix_done, 1)
                pe.wait_ge(kgm_ready, hg + 1)
                for b in range(NB):
                    out = free_bank(f"{kind}ss{h}.{b}")
                    mm(out[:, 0:w], kgm[0:NS, b, :], va(2)[0:NS], start=True, stop=True).then_inc(mix_done, 1)

            def back(kind, h, hg):
                pe.wait_ge(yn_ready, hg + 1)
                for i in range(2):
                    turn_back(f"{kind}yt{2 * h + i}", lambda g: num[:, hg % 2, g, i * P:(i + 1) * P])

            def heads(kind, n, first, qk, va, w):
                if kind == "a":
                    pe.wait_ge(drop_ready, 1)
                    row_max(0)
                    row_max(1)
                front(kind, 0, qk)
                for h in range(n):
                    if kind == "a" and h + 2 < n:
                        row_max(h + 2)
                    if h + 1 < n:
                        front(kind, h + 1, qk)
                    middle(kind, h, first + h, lambda g: va(g, h), w)

            def ffn(l):
                norm(2 * l + 1)
                for i in range(2 * KF):
                    tile(START[f"up{l}"] + i, normed, (xlo_ready, KD * (2 * l + 1)) if i == 0 else None)
                for i in range(KD):
                    tile(START[f"down{l}"] + i, lambda k: (HH[:, k, :], HL[:, k, :]),
                         (hidlo_ready, KF * l) if i == 0 else None)

            pe.wait_ge(const_in, 16)
            norm(0)
            for t in range(T0, START["even_out"]):
                tile(t, normed, (xlo_ready, 0) if t == T0 else None)
                if 9 <= t <= 16:
                    wait_tile_empty(pe, t - 1)
                    turn(f"v{t - 9}", vT[:, (t - 9) % 2, :])
            pe.wait_ge(slab_ready, 1)
            for s in range(2):
                turn(f"col{s}", slab[:, s, :])
            out = free_bank("adec")
            for h in range(AH):
                last = mm(out[:, h * NB:(h + 1) * NB], ident[0:AH, h:h + 1].broadcast_to([AH, P]),
                          rsm[0:AH, 2, 0:NB], start=True, stop=True)
            last.then_inc(mix_done, 1)
            out = free_bank("sdec")
            mm(out[:, 0:NB * BH], ones[0:BH, :], dg[0:BH, :, :].rearrange("p b h -> p (b h)"),
               start=True, stop=True).then_inc(mix_done, 1)
            heads("a", AH, 0, lambda h: (qT[:, h, :], kT[:, h, :]), lambda g, h: vA[:, g, h, :], AV + 1)
            pe.wait_ge(silu_done, XB)
            for i in range(8):
                turn(f"xn{i}", xbcT[:, i, :])
            back("a", AH - 1, AH - 1)
            for g in range(BG):
                turn(f"bn{g}", xbcT[:, 8 + g, :])
            for g in range(BG):
                out = free_bank(f"cb{g}")
                scores(out, xbcT[:, 8 + g, :], xbcT[:, 10 + g, :]).then_inc(mix_done, 1)

            def say(h):
                out = free_bank(f"say{h}")
                pe.wait_ge(e_ready, h + 1)
                e = E2[:, h % 3, :]
                x = xdt[:, :, h * BP:(h + 1) * BP]
                mm(out[:, 0:BP], e[:, 0:P], x[:, 0, :], start=True, stop=True)
                mm(out[:, BP:2 * BP], e[:, P:TP], x[:, 0, :], start=True, stop=False)
                mm(out[:, BP:2 * BP], e[:, TP:TP + P], x[:, 1, :], start=False, stop=True)
                mm(out[0:NS, 2 * BP:3 * BP], e[0:NS, TP + P:BLK], x[0:NS, 2, :], start=True, stop=True)\
                    .then_inc(mix_done, 1)

            def sbc(h):
                log_rows(f"sbc{h}", ac, BH, h)

            sbc(0)
            sbc(1)
            for h in range(BH):
                if h + 2 < BH:
                    sbc(h + 2)
                say(h)

            def si(g):
                out = free_bank(f"si{g}")
                pe.wait_ge(cm_ready, 1)
                for b in range(NB):
                    n = g * NB + b
                    pe.wait_ge(sts_in[n % SSLOTS], 16 * (n // SSLOTS + 1))
                    last = mm(out[0:NS, :], cm[:, g, b, :], sts[n % SSLOTS], start=(b == 0), stop=(b == NB - 1))
                last.then_inc(mix_done, 1)

            def sp_(g):
                sl = slice(g * GW, (g + 1) * GW)
                out = free_bank(f"sp{g}")
                mm(out[:, :], bnat[:, 0, g, :], xdt[:, 0, sl], start=True, stop=False)
                mm(out[:, :], bnat[:, 1, g, :], xdt[:, 1, sl], start=False, stop=True).then_inc(mix_done, 1)

            def su(g):
                sl = slice(g * GW, (g + 1) * GW)
                for b in range(NB):
                    out = free_bank(f"su{g}.{b}")
                    mm(out[:, :], bm[0:NS, b, g, :], xdt[0:NS, 2, sl], start=True, stop=True).then_inc(mix_done, 1)

            si(0)
            pe.wait_ge(xw_ready, 1)
            sp_(0)
            sp_(1)
            pe.wait_ge(bm_ready, BG)
            su(0)
            si(1)
            su(1)
            pe.wait_ge(ynat_ready, BG)
            for i in range(8):
                turn_back(f"sy{i}", lambda g: yn[:, g, i * P:(i + 1) * P])
            for g in range(BG):
                out = free_bank(f"sn{g}")
                for i in range(4):
                    pe.wait_ge(sq2_ready, 4 * g + i + 1)
                    last = mm(out[:, 0:T], ones, xbcT[:, 4 * g + i, :], start=(i == 0), stop=(i == 3))
                last.then_inc(mix_done, 1)
            for i in range(KD):
                tile(START["even_out"] + i,
                     lambda k: (hH[:, k, :], hL[:, k, :]) if k < 8 else (YH[:, k - 8, :], YL[:, k - 8, :]),
                     (ylo_ready, 0) if i == 0 else None)
            ffn(0)
            norm(2)
            for i in range(len(ODD)):
                t = START["odd"] + i
                tile(t, normed, (xlo_ready, 2 * KD) if i == 0 else None)
                if 17 <= i <= 32:
                    wait_tile_empty(pe, t - 1)
                    turn(f"rv{i - 17}", vT[:, (i - 17) % 2, :])
            heads("r", CH, AH, lambda h: (rqT[:, h, :], rkT[:, h, :]), lambda g, h: rvA[:, g, h, :], CV)
            back("r", CH - 1, AH + CH - 1)
            for i in range(KD):
                tile(START["odd_out"] + i,
                     lambda k: (hH[:, k, :], hL[:, k, :]) if k < 8 else (RH[:, k - 8, :], RL[:, k - 8, :]),
                     (ylo_ready, 16) if i == 0 else None)
            ffn(1)
            norm(4)

        @block.scalar
        def _(eng):
            s = Steps(eng, act_step)
            act = nc.scalar.activation
            at = [0]

            def split(upto):
                while at[0] <= min(upto, CHUNKS - 1):
                    c = at[0]
                    eng.wait_ge(raw_in[c % RING], 16 * (c // RING + 1))
                    if c >= RING:
                        wait_read(eng, c - RING)
                    s.do(act(wh[:, c % RING, :], raw[:, c % RING, :], ACT.Copy), hi_ready)
                    at[0] += 1

            def rsqrt(dst, src, n, ready):
                s.do(act(dst, src, ACT.Ln, scale=1.0 / n, bias=eps[0:dst.shape[0]]))
                s.settle()
                s.do(act(dst, dst, ACT.Exp, scale=-0.5), ready)

            eps = vec[:, VEC_W - 1:VEC_W]

            def norm(n):
                if n == 0:
                    eng.wait_ge(x_in, 16)
                    eng.wait_ge(vec_in, 16)
                else:
                    eng.wait_ge(xlo_ready, KD * n)
                if n in (1, 3):
                    eng.wait_ge(ylo_ready, 16 if n == 1 else 32)
                if n == 1:
                    for i in range(SSLOTS - 4, SSLOTS):
                        eng.wait_ge(sts_out[i], 16 * len(range(i, BG * NB, SSLOTS)))
                for i in range(KD):
                    if n:
                        eng.wait_ge(x_ready, KD * (n - 1) + i + 1)
                    s.do(act(hF[:, i, :], xT[:, i, :], ACT.Square), sq_ready)
                wait_job(eng, f"norm{n}")
                s.do(act(rstd[:], mb(f"norm{n}")[:, 0:T], ACT.Ln, scale=1.0 / D, bias=eps), mix_act)
                s.settle()
                s.do(act(rstd[:], rstd[:], ACT.Exp, scale=-0.5), rstd_ready)
                if n == 4:
                    return
                for i in range(KD):
                    eng.wait_ge(h_ready, KD * n + i + 1)
                    s.do(act(hH[:, i, :], hF[:, i, :], ACT.Copy), xhi_ready)

            def y_high(n, dst, src):
                s.do(act(dst, src, ACT.Copy), yhi_ready)

            def weights(kind, h, hg):
                sl = hg % 2
                if h >= 2:
                    wait_empty(eng, f"{kind}sc{h - 2}")
                if kind == "a":
                    wait_job(eng, f"abc{h}")
                    b = mb(f"abc{h}")
                    s.do(act(E[:, sl, 0:TP], b[:, 0:TP], ACT.Exp, bias=cols[:, 0, h:h + 1]))
                    s.do(act(E[:, sl, TP:TP + P], b[:, TP:TP + P], ACT.Exp, bias=cols[:, 1, h:h + 1]))
                    s.do(act(E[0:NS, sl, TP + P:BLK], b[0:NS, TP + P:BLK], ACT.Exp, bias=cols[0:NS, 2, h:h + 1]), mix_act)
                else:
                    s.do(act(E[:, sl, :], dist, ACT.Exp, scale=LOG_GAMMA[h]), exp_ready)

            def back(kind, h, Y):
                for i in range(2):
                    n = 2 * h + i
                    wait_empty(eng, f"{kind}yt{n}")
                    y_high(n, Y[n // 8][0][:, n % 8, :], yF[:, n % 2, :])

            def heads(kind, count, first, Y, w):
                if kind == "r":
                    eng.wait_ge(rope_ready, 2 * CH)
                else:
                    wait_empty(eng, "sdec")
                weights(kind, 0, first)
                weights(kind, 1, first + 1)
                eng.wait_ge(zeroed, 3 if kind == "a" else 5)
                for h in range(count):
                    hg = first + h
                    if h + 2 < count:
                        weights(kind, h + 2, hg + 2)
                    for g in range(2):
                        wait_job(eng, f"{kind}o{g}{h}")
                        s.do(act(num[:, hg % 2, g, 0:w], mb(f"{kind}o{g}{h}")[:, 0:w], ACT.Copy), mix_act)
                    if hg >= 2:
                        eng.wait_ge(pout_out[hg % 2], 16 * (hg // 2))
                    wait_job(eng, f"{kind}sp{h}")
                    s.do(act(pout[:, hg % 2, 0:w], mb(f"{kind}sp{h}")[:, 0:w], ACT.Copy), mix_act)
                    if h:
                        back(kind, h - 1, Y)
                    eng.wait_ge(var_ready, hg + 1)
                    s.do(act(sm[:, 5, :], sm[:, 4, :], ACT.Ln, bias=eps))
                    s.settle()
                    s.do(act(sm[:, 6, :], sm[:, 5, :], ACT.Exp, scale=-0.5), inv_ready)
                back(kind, count - 1, Y)

            def ffn(l):
                norm(2 * l + 1)
                t0 = START[f"up{l}"]

                eng.wait_ge(zeroed, 4 + 2 * l)

                def silu(j):
                    eng.wait_ge(conv_done, XB + 2 * KF * l + 2 * j + 1)
                    if j >= 2:
                        eng.wait_ge(hid_ready, KF * l + j - 1)
                    s.do(act(sgate[:, j % 2, 0:304], cy[:, 2 * (j % 2), 0:304], ACT.Silu), silu_done)

                def high(j):
                    eng.wait_ge(hid_ready, KF * l + j + 1)
                    s.do(act(HH[:, j, :], hidF[:, j % 3, :], ACT.Copy), hidhi_ready)

                for j in range(KF + 2):
                    if j < KF:
                        for x in range(2):
                            i = 2 * j + x
                            split(last_chunk(t0 + i) + 3)
                            wait_tile(eng, t0 + i)
                            n = XB + 2 * KF * l + i
                            if n >= 4:
                                eng.wait_ge(conv_done, n - 3)
                                eng.wait_ge(tail_done, n - 3)
                            b = bank[(t0 + i) % 4]
                            p = pad[:, n % 4, 1:]
                            s.do(act(p[:, W2:W2 + TP], b[:, 0:TP], ACT.Copy))
                            s.do(act(padded(p, W2)[:, :, W2:], smp(b), ACT.Copy), gemm_act)
                    if 1 <= j <= KF:
                        silu(j - 1)
                    if j >= 2:
                        high(j - 2)
                for i in range(KD):
                    split(last_chunk(START[f"down{l}"] + i) + 3)

            def silu_x(i):
                eng.wait_ge(conv_done, i + 1)
                s.do(act(xbcT[:, i, 0:TP], cy[:, i % 4, 0:TP], ACT.Silu))
                s.do(act(smp(xbcT[:, i, :]), padded(cy[:, i % 4, :], W1, -W1)[:, :, W1:], ACT.Silu), silu_done)

            split(2)
            norm(0)
            eng.wait_ge(const_in, 16)
            s.do(act(drop[:], const("drop"), ACT.Copy))
            s.do(act(identR[:], ident, ACT.Copy), drop_ready)
            eng.wait_ge(zeroed, 1)
            for t in range(T0, START["even_out"]):
                kind, i = TILES[t][1:3]
                split(last_chunk(t) + 3)
                if kind != "gates":
                    wait_tile(eng, t)
                b = bank[t % 4]
                if kind in ("q", "k"):
                    s.do(act((qT if kind == "q" else kT)[:, i, :], b[:, 0:T], ACT.Copy), gemm_act)
                elif kind == "v":
                    if i >= 2:
                        wait_job(eng, f"v{i - 2}")
                    s.do(act(vT[:, i % 2, :], b[:, 0:T], ACT.Copy), gemm_act)
                elif kind == "gates":
                    eng.wait_ge(row_dve, 1)
                    s.do(act(rows[0:AH, 3, :], rows[0:AH, 3, :], ACT.Exp))
                    s.do(act(rows[0:BH, 4, :], rows[0:BH, 4, :], ACT.Exp))
                    s.do(act(rsm[0:BH, 5, 0:1], v("alog", p=BH), ACT.Exp))
                    s.settle()
                    s.do(act(rows[0:AH, 3, :], rows[0:AH, 3, :], ACT.Ln, bias=1.0))
                    s.do(act(rows[0:BH, 4, :], rows[0:BH, 4, :], ACT.Ln, bias=1.0), row_act)
                    eng.wait_ge(row_dve, 2)
                    s.do(act(slab[64:64 + AH, 0, :], rows[0:AH, 3, :], ACT.Exp, scale=-1.0))
                    s.do(act(slab[32:32 + AH, 0, TP:T], rows[0:AH, 4, TP:T], ACT.Exp))
                    s.do(act(rows[0:AH, 5, :], rows[0:AH, 5, :], ACT.Exp))
                    s.do(act(rsm[0:AH, 2, 0:NB], rsm[0:AH, 2, 0:NB], ACT.Exp))
                    s.do(act(slab[96:96 + BH, 1, :], rows[0:BH, 2, :], ACT.Exp, scale=-1.0))
                    s.do(act(slab[64:64 + BH, 1, :], ac[0:BH, :], ACT.Exp))
                    s.do(act(rsm[0:BH, 3, 0:NB], smp(ac[0:BH, :])[:, :, TS - 1], ACT.Exp), row_act)
                elif kind == "og":
                    if i == 0:
                        eng.wait_ge(xlo_ready, KD)
                    s.do(act(hF[:, i, :], b[:, 0:T], ACT.Sigmoid), gemm_act)
                elif kind == "z":
                    s.do(act(zT[:, i, :], b[:, 0:T], ACT.Silu), gemm_act)
                elif kind == "xbc":
                    if i >= 4:
                        eng.wait_ge(conv_done, i - 3)
                        eng.wait_ge(tail_done, i - 3)
                    p = pad[:, i % 4, :]
                    s.do(act(p[:, W1:W1 + TP], b[:, 0:TP], ACT.Copy))
                    s.do(act(padded(p, W1)[:, :, W1:], smp(b), ACT.Copy), gemm_act)
                    if i >= 1:
                        silu_x(i - 1)
            silu_x(XB - 1)
            heads("a", AH, 0, YA, AV + 1)
            for i in (3, 4):
                eng.wait_ge(st_out[i], 16)
            for g in range(BG):
                wait_job(eng, f"bn{g}")
                b = mb(f"bn{g}")
                s.do(act(bnat[:, 0:2, g, :], b[:, 0:TP].rearrange("p (g n) -> p g n", g=2), ACT.Copy))
                s.do(act(bnat[0:NS, 2, g, :], b[0:NS, TP:TP + P], ACT.Copy), mix_act)
            for h in range(BH):
                wait_job(eng, f"sbc{h}")
                if h >= 3:
                    wait_job(eng, f"say{h - 3}")
                b, x = mb(f"sbc{h}"), E2[:, h % 3, :]
                c = P + h
                s.do(act(x[:, 0:TP], b[:, 0:TP], ACT.Exp, bias=cols[:, 0, c:c + 1]))
                s.do(act(x[:, TP:TP + P], b[:, TP:TP + P], ACT.Exp, bias=cols[:, 1, c:c + 1]))
                s.do(act(x[0:NS, TP + P:BLK], b[0:NS, TP + P:BLK], ACT.Exp, bias=cols[0:NS, 2, c:c + 1]), mix_act)
            for g in range(BG):
                wait_job(eng, f"sp{g}")
                s.do(act(pst[:, g, :], mb(f"sp{g}")[:, :], ACT.Copy), mix_act)
            for i in range(8):
                eng.wait_ge(zq_ready, i + 1)
                s.do(act(xbcT[:, i, :], zT[:, i, :], ACT.Square), sq2_ready)
            for g in range(BG):
                wait_job(eng, f"sn{g}")
                s.do(act(rst2[:, g, :], mb(f"sn{g}")[:, 0:T], ACT.Ln, scale=1.0 / GW, bias=eps), mix_act)
                s.settle()
                s.do(act(rst2[:, g, :], rst2[:, g, :], ACT.Exp, scale=-0.5), srs_ready)
            eng.wait_ge(pst_out, 16 * BG)
            for i in range(8):
                eng.wait_ge(yg_ready, i + 1)
                y_high(8 + i, YH[:, i, :], zT[:, i, :])
            for i in range(KD):
                split(last_chunk(START["even_out"] + i) + 3)
            ffn(0)
            norm(2)
            for j in range(len(ODD)):
                t = START["odd"] + j
                kind, i = TILES[t][1:3]
                split(last_chunk(t) + 3)
                b = bank[t % 4]
                if kind == "rv":
                    wait_tile(eng, t)
                    if i >= 2:
                        wait_job(eng, f"rv{i - 2}")
                    s.do(act(vT[:, i % 2, :], b[:, 0:T], ACT.Copy), gemm_act)
                elif kind == "rg":
                    wait_tile(eng, t)
                    if i == 8:
                        eng.wait_ge(xlo_ready, 3 * KD)
                    s.do(act(gT[:, i, :] if i < 8 else hF[:, i - 8, :], b[:, 0:T], ACT.Silu), gemm_act)
            heads("r", CH, AH, YR, CV)
            for i in range(KD):
                split(last_chunk(START["odd_out"] + i) + 3)
            ffn(1)
            norm(4)

        @block.vector
        def _(eng):
            s = Steps(eng, dve_step)
            do, settle = s.do, s.settle
            ts, tt, stt = nc.vector.tensor_scalar, nc.vector.tensor_tensor, nc.vector.scalar_tensor_tensor
            copy = nc.vector.tensor_copy
            at = [0]

            def split(upto):
                while at[0] <= min(upto, CHUNKS - 1):
                    c = at[0]
                    eng.wait_ge(hi_ready, c + 1)
                    if c >= RING:
                        wait_read(eng, c - RING)
                    do(tt(wl[:, c % RING, :], raw[:, c % RING, :], wh[:, c % RING, :].bitcast(F32), ALU.subtract), lo_ready)
                    at[0] += 1

            def norm(n):
                if n == 0:
                    eng.wait_ge(vec_in, 16)
                eng.wait_ge(rstd_ready, n + 1)
                for i in range(KD):
                    do(stt(out=hF[:, i, :], in0=xT[:, i, :], scalar=v(f"norm{n}", i), in1=rstd[:],
                           op0=ALU.mult, op1=ALU.mult), h_ready if n < 4 else y_ready)
                if n == 4:
                    return
                for i in range(KD):
                    eng.wait_ge(xhi_ready, KD * n + i + 1)
                    do(tt(hL[:, i, :], hF[:, i, :], hH[:, i, :].bitcast(F32), ALU.subtract), xlo_ready)

            def out_tiles(phase, n):
                for i in range(KD):
                    t = START[phase] + i
                    split(last_chunk(t) + 3)
                    wait_tile(eng, t)
                    do(tt(xT[:, i, :], bank[t % 4][:, 0:T], xT[:, i, :], ALU.add), gemm_dve)
                    settle()
                    eng.sem_inc(x_ready, 1)

            def turned(name, dst):
                wait_job(eng, name)
                b = mb(name)
                do(copy(dst(slice(0, 2), P), b[:, 0:TP].rearrange("p (g n) -> p g n", g=2)))
                do(copy(dst(2, NS), b[0:NS, TP:TP + P]), mix_dve)

            def column(s_, i, g):
                n = NS if g == 2 else P
                return cols[0:n, g, P * s_ + i:P * s_ + i + 1]

            def front(kind, h, hg):
                sl = hg % 2
                if kind == "a":
                    wait_empty(eng, f"abc{h}")
                else:
                    eng.wait_ge(exp_ready, h + 1)
                wait_job(eng, f"{kind}sc{h}")
                b = mb(f"{kind}sc{h}")
                do(stt(out=Sp[:, sl, 0:TP + P], in0=b[:, 0:TP + P], scalar=KSCALE, in1=E[:, sl, 0:TP + P],
                       op0=ALU.mult, op1=ALU.mult))
                do(stt(out=Sp[0:NS, sl, TP + P:BLK], in0=b[0:NS, TP + P:BLK], scalar=KSCALE,
                       in1=E[0:NS, sl, TP + P:BLK], op0=ALU.mult, op1=ALU.mult), mix_dve)
                wait_job(eng, f"{kind}kn{h}")
                b = mb(f"{kind}kn{h}")
                if kind == "a":
                    wk = [column(0, 96 + h, g) for g in range(3)]
                else:
                    rk = const("retk")
                    wk = [rk[0:NS if g == 2 else P, g * CH + h:g * CH + h + 1] for g in range(3)]
                for g in range(2):
                    do(ts(kg[:, sl, g, :], b[:, g * P:(g + 1) * P], wk[g], None, ALU.mult))
                if hg:
                    eng.wait_ge(kgm_ready, hg)
                do(ts(kgs[0:NS], b[0:NS, TP:TP + P], wk[2], None, ALU.mult), mix_dve)

            def middle(kind, h, hg, w):
                sl = hg % 2
                wait_job(eng, f"{kind}oi{h}")
                wq = column(0, 32 + h, 2) if kind == "a" else const("retq")[0:NS, h:h + 1]
                y = num[0:NS, sl, 2, 0:w]
                do(ts(y, mb(f"{kind}oi{h}")[0:NS, 0:w], wq, None, ALU.mult), mix_dve)
                wait_job(eng, f"{kind}os{h}")
                settle()
                do(tt(y, mb(f"{kind}os{h}")[0:NS, 0:w], y, ALU.add), mix_dve)
                for b_ in range(NB):
                    n = 2 * hg + b_ // 4
                    wait_job(eng, f"{kind}ss{h}.{b_}")
                    dec = adec[:, h, b_:b_ + 1] if kind == "a" else math.exp(LOG_GAMMA[h] * TS)
                    x = state(n)[:, b_ % 4, 0:w]
                    do(stt(out=x, in0=x, scalar=dec, in1=mb(f"{kind}ss{h}.{b_}")[:, 0:w],
                           op0=ALU.mult, op1=ALU.add), mix_dve)

            def head_norm(kind, h, hg):
                sl = hg % 2
                settle()
                wait_empty(eng, f"{kind}o1{h}")
                for g in range(3):
                    do(nc.vector.bn_stats(out=stats[0:NS if g == 2 else P, g, :], in_=num[0:NS if g == 2 else P, sl, g, 0:CV]))
                if kind == "a":
                    den = num[:, sl, :, AV]
                    do(stt(out=sm[:, 0, :], in0=den, scalar=-1.0, in1=den, op0=ALU.mult, op1=ALU.max))
                settle()
                for g in range(3):
                    do(nc.vector.bn_aggr(out=mv[0:NS if g == 2 else P, g, :], in_=stats[0:NS if g == 2 else P, g, :]))
                if kind == "a":
                    do(tt(sm[:, 1, :], sm[:, 0, :], cols[:, :, 64 + h], ALU.max))
                    settle()
                    do(nc.vector.reciprocal(sm[:, 2, :], sm[:, 1, :]))
                    settle()
                    do(tt(sm[:, 3, :], mv[:, :, 1], sm[:, 2, :], ALU.mult))
                    settle()
                    do(tt(sm[:, 4, :], sm[:, 3, :], sm[:, 2, :], ALU.mult), var_ready)
                    eng.wait_ge(inv_ready, hg + 1)
                    do(tt(sm[:, 7, :], sm[:, 6, :], sm[:, 2, :], ALU.mult))
                else:
                    settle()
                    do(copy(sm[:, 4, :], mv[:, :, 1]), var_ready)
                    eng.wait_ge(inv_ready, hg + 1)
                    do(copy(sm[:, 7, :], sm[:, 6, :]))
                settle()
                for g in range(3):
                    n = NS if g == 2 else P
                    do(ts(num[0:n, sl, g, 0:CV], num[0:n, sl, g, 0:CV], mv[0:n, g, 0:1], sm[0:n, 7, g:g + 1],
                          ALU.subtract, ALU.mult), yn_ready if g == 2 else None)

            def back(kind, h):
                for i in range(2):
                    n = 2 * h + i
                    wait_job(eng, f"{kind}yt{n}")
                    if n >= 2:
                        eng.wait_ge(ylo_ready, (16 if kind == "r" else 0) + n - 1)
                    if kind == "a":
                        gate, gain = hF[:, n, :], v("ag", n)
                    else:
                        gate, gain = (gT[:, n, :] if n < 8 else hF[:, n - 8, :]), v("rg", n)
                    do(stt(out=yF[:, n % 2, :], in0=mb(f"{kind}yt{n}")[:, 0:T], scalar=gain, in1=gate,
                           op0=ALU.mult, op1=ALU.mult), mix_dve)

            def heads(kind, count, first, w):
                front(kind, 0, first)
                for h in range(count):
                    if h + 1 < count:
                        front(kind, h + 1, first + h + 1)
                    if h:
                        back(kind, h - 1)
                    middle(kind, h, first + h, w)
                    head_norm(kind, h, first + h)

            def convolve(n, x, width, taps, bias):
                eng.wait_ge(fill_done, n + 1)
                y = cy[:, n % 4, 0:width]
                do(ts(y, x[:, 0:width], taps[0], bias, ALU.mult, ALU.add))
                for j in range(1, len(taps)):
                    settle()
                    do(stt(out=y, in0=x[:, j:j + width], scalar=taps[j], in1=y, op0=ALU.mult, op1=ALU.add),
                       conv_done if j == len(taps) - 1 else None)

            def ffn(l):
                norm(2 * l + 1)
                t0 = START[f"up{l}"]
                for j in range(KF + 2):
                    if j < KF:
                        for x in range(2):
                            i = 2 * j + x
                            n = XB + 2 * KF * l + i
                            split(last_chunk(t0 + i) + 3)
                            wait_tile_empty(eng, t0 + i)
                            if x == 0 and j >= 2:
                                eng.wait_ge(silu_done, XB + KF * l + j - 1)
                            convolve(n, pad[:, n % 4, 1:], 304,
                                     [v("fcw", (2 * KF * l + i) * 3 + d) for d in range(3)],
                                     v("fcb", 2 * KF * l + i))
                    if 1 <= j <= KF:
                        p, sl = j - 1, (j - 1) % 2
                        eng.wait_ge(silu_done, XB + KF * l + p + 1)
                        eng.wait_ge(conv_done, XB + 2 * KF * l + 2 * p + 2)
                        if p >= 3:
                            eng.wait_ge(hidlo_ready, KF * l + p - 2)
                        g, u, o = sgate[:, sl, :], cy[:, 2 * sl + 1, :], hidF[:, p % 3, :]
                        do(tt(o[:, 0:TP], g[:, 0:TP], u[:, 0:TP], ALU.mult))
                        do(tt(smp(o), padded(g, W2, -W2)[:, :, W2:], padded(u, W2, -W2)[:, :, W2:],
                              ALU.mult), hid_ready)
                    if j >= 2:
                        p = j - 2
                        eng.wait_ge(hidhi_ready, KF * l + p + 1)
                        do(tt(HL[:, p, :], hidF[:, p % 3, :], HH[:, p, :].bitcast(F32), ALU.subtract), hidlo_ready)
                out_tiles(f"down{l}", 2 * l + 1)

            def gate_rows(t):
                b = bank[t % 4]
                a4, b16 = slice(0, AH), slice(0, BH)
                li, fx, dx, f3, d4, lf, dt = (rows[a4, 0, :], rows[a4, 1, :], rows[b16, 2, :], rows[a4, 3, :],
                                              rows[b16, 4, :], rows[a4, 5, :], rows[b16, 6, :])
                wait_tile(eng, t)
                eng.wait_ge(const_in, 16)
                do(ts(li, b[0:AH, 0:T], v("igb", p=AH), None, ALU.add))
                do(ts(fx, b[32:32 + AH, 0:T], v("fgb", p=AH), None, ALU.add))
                do(ts(dx, b[64:64 + BH, 0:T], v("dtb", p=BH), None, ALU.add), gemm_dve)
                settle()
                do(stt(out=f3, in0=fx, scalar=-1.0, in1=fx, op0=ALU.mult, op1=ALU.min))
                do(stt(out=d4, in0=dx, scalar=-1.0, in1=dx, op0=ALU.mult, op1=ALU.min), row_dve)
                eng.wait_ge(row_act, 1)
                do(stt(out=lf, in0=fx, scalar=0.0, in1=f3, op0=ALU.min, op1=ALU.subtract))
                do(stt(out=dt, in0=dx, scalar=0.0, in1=d4, op0=ALU.max, op1=ALU.add))
                settle()
                do(copy(slab[32:32 + BH, 1, :], dt))
                do(ts(rows[b16, 7, :], dt, rsm[b16, 5, 0:1], -1.0, ALU.mult, ALU.mult))
                settle()
                kp, dp = resets[:, 0, :], resets[:, 1, :]
                eng.wait_ge(resets_in, 16)
                scan = nc.vector.tensor_tensor_scan
                cum = rows[a4, 8, :]
                do(scan(out=cum, data0=kp[a4], data1=lf, initial=0.0, op0=ALU.mult, op1=ALU.add))
                do(scan(out=ac[b16, :], data0=kp[b16], data1=rows[b16, 7, :], initial=0.0, op0=ALU.mult, op1=ALU.add))
                settle()
                do(ts(slab[b16, 1, :], ac[b16, :], -1.0, None, ALU.mult))
                a = slab[a4, 0, :]
                do(tt(a, li, cum, ALU.subtract))
                settle()
                do(copy(li, a))
                settle()
                first = smp(li)[:, :, 0]
                do(tt(first, first, m0, ALU.max))
                settle()
                M = rows[a4, 1, :]
                do(scan(out=M, data0=dp[a4], data1=li, initial=0.0, op0=ALU.add, op1=ALU.max))
                settle()
                ends = rsm[a4, 0, 0:NB + 1]
                do(copy(ends[:, 0:1], M[:, TP - 1:TP]))
                do(copy(ends[:, 1:NB + 1], smp(M)[:, :, TS - 1]))
                do(ts(nM[a4, :], M, -1.0, None, ALU.mult))
                do(tt(rows[a4, 3, :], cum, M, ALU.add))
                settle()
                do(copy(rsm[a4, 1, 0:1], rows[a4, 3, TP - 1:TP]))
                do(copy(rsm[a4, 1, 1:NB + 1], smp(rows[a4, 3, :])[:, :, TS - 1]))
                do(tt(smp(rows[a4, 4, :]), bc(m0, 2, TS), smp(M), ALU.subtract))
                do(ts(rows[a4, 5, 0:TP], a[:, 0:TP], ends[:, 0:1], None, ALU.subtract))
                do(tt(smp(rows[a4, 5, :]), smp(a), bc(ends[:, 1:NB + 1], 2, TS), ALU.subtract))
                do(tt(rsm[a4, 2, 0:NB], m0, ends[:, 1:NB + 1], ALU.subtract))
                do(ts(rows[b16, 2, 0:TP], ac[b16, 0:TP], ac[b16, TP - 1:TP], None, ALU.subtract))
                do(tt(smp(rows[b16, 2, :]), smp(ac[b16, :]), bc(smp(ac[b16, :])[:, :, TS - 1], 2, TS), ALU.subtract), row_dve)
                eng.wait_ge(row_act, 2)
                do(ts(slab[96:96 + AH, 0, :], rows[a4, 5, :], KSCALE, None, ALU.mult))
                do(tt(dg[b16], bc(rsm[b16, 3, 0:NB], 2, BH), bc(ident[b16, 0:BH], 1, NB), ALU.mult), slab_ready)

            split(2)
            norm(0)
            for t in range(T0, START["even_out"]):
                kind, i = TILES[t][1:3]
                split(last_chunk(t) + 3)
                if kind == "gates":
                    eng.wait_ge(zeroed, 2)
                    gate_rows(t)
                if 10 <= t <= 17:
                    n = t - 10
                    if n == 0:
                        eng.wait_ge(zeroed, 2)
                    turned(f"v{n}", lambda g, p: vA[0:p, g, n // 2, (n % 2) * P:(n % 2) * P + P])
                if kind == "xbc" and i >= 1 or t == START["even_out"] - 1:
                    for m in ([i - 1] if t < START["even_out"] - 1 else [i - 1, i]):
                        wait_tile_empty(eng, XBC0 + m)
                        if m >= 4:
                            eng.wait_ge(silu_done, m - 3)
                        convolve(m, pad[:, m % 4, :], 312, [v("scw", m * 4 + d) for d in range(4)], v("scb", m))
            for c in range(2):
                turned(f"col{c}", lambda g, p: cols[0:p, g, c * P:(c + 1) * P])
            wait_job(eng, "adec")
            do(copy(adec[:], mb("adec")[:, 0:AH * NB].rearrange("p (h b) -> p h b", h=AH)), mix_dve)
            wait_job(eng, "sdec")
            do(copy(sdec[:], mb("sdec")[:, 0:NB * BH].rearrange("p (b h) -> p b h", b=NB)), mix_dve)
            settle()
            heads("a", AH, 0, AV + 1)
            for i in range(8):
                wait_job(eng, f"xn{i}")
                b = mb(f"xn{i}")
                dtc = cols[:, :, P + 32 + 2 * i:P + 32 + 2 * i + 2]
                for g in range(3):
                    n = NS if g == 2 else P
                    do(tt(xdt[0:n, g, i * P:(i + 1) * P].rearrange("p (h e) -> p h e", h=2),
                          b[0:n, g * P:(g + 1) * P].rearrange("p (h e) -> p h e", h=2),
                          bc(dtc[0:n, g, :], 2, BP), ALU.mult), mix_dve if g == 2 else None)
            back("a", AH - 1)
            for g in range(BG):
                wait_job(eng, f"cb{g}")
                b = mb(f"cb{g}")
                do(copy(cbm[:, g, 0:TP + P], b[:, 0:TP + P]))
                do(copy(cbm[0:NS, g, TP + P:BLK], b[0:NS, TP + P:BLK]), mix_dve)
            settle()
            for h in range(BH + 1):
                if h < BH:
                    wait_empty(eng, f"sbc{h}")
                    x, c = E2[:, h % 3, :], cbm[:, h // HG, :]
                    for part in ((slice(0, P), slice(0, TP + P)), (slice(0, NS), slice(TP + P, BLK))):
                        do(tt(x[part], x[part], c[part], ALU.mult),
                           e_ready if part[0].stop == NS else None)
                if h:
                    wait_job(eng, f"say{h - 1}")
                    b = mb(f"say{h - 1}")
                    sl = slice((h - 1) * BP, h * BP)
                    do(copy(yn[:, 0:2, sl], b[:, 0:2 * BP].rearrange("p (g n) -> p g n", g=2)))
                    do(copy(yn[0:NS, 2, sl], b[0:NS, 2 * BP:3 * BP]), mix_dve)
            for g in range(3):
                n = NS if g == 2 else P
                x = xdt[0:n, g, :].rearrange("p (h e) -> p h e", h=BH)
                do(tt(x, x, bc(cols[0:n, g, P + 96:P + 96 + BH], 2, BP), ALU.mult), xw_ready if g == 2 else None)
            for g in range(BG):
                wait_job(eng, f"si{g}")
                r3 = lambda a: a.rearrange("p (h e) -> p h e", h=HG)
                do(tt(r3(itmp[0:NS, :]), r3(mb(f"si{g}")[0:NS, :]),
                      bc(cols[0:NS, 2, P + 64 + g * HG:P + 64 + (g + 1) * HG], 2, BP), ALU.mult), mix_dve)
                settle()
                y = yn[0:NS, 2, g * GW:(g + 1) * GW]
                do(tt(y, y, itmp[0:NS, :], ALU.add), ynat_ready)
                for b_ in range(NB):
                    x = sts[(g * NB + b_) % SSLOTS]
                    wait_job(eng, f"su{g}.{b_}")
                    eng.wait_ge(dec_ready, g * NB + b_ + 1)
                    do(tt(x, mb(f"su{g}.{b_}")[:, :], x, ALU.add), mix_dve)
            for i in range(8):
                wait_job(eng, f"sy{i}")
                do(stt(out=ty[:, i % 2, :], in0=xbcT[:, i, :], scalar=v("D", i), in1=mb(f"sy{i}")[:, 0:T],
                       op0=ALU.mult, op1=ALU.add), mix_dve)
                settle()
                do(tt(zT[:, i, :], zT[:, i, :], ty[:, i % 2, :], ALU.mult), zq_ready)
            for i in range(8):
                eng.wait_ge(srs_ready, i // 4 + 1)
                do(stt(out=zT[:, i, :], in0=zT[:, i, :], scalar=v("sg", i), in1=rst2[:, i // 4, :],
                       op0=ALU.mult, op1=ALU.mult), yg_ready)
            for i in range(8):
                eng.wait_ge(yhi_ready, 8 + i + 1)
                do(tt(YL[:, i, :], zT[:, i, :], YH[:, i, :].bitcast(F32), ALU.subtract), ylo_ready)
            out_tiles("even_out", 0)
            ffn(0)
            norm(2)
            cos, sin = const("cos"), const("sin")
            for j in range(len(ODD)):
                t = START["odd"] + j
                kind, i = TILES[t][1:3]
                split(last_chunk(t) + 3)
                b = bank[t % 4]
                if kind in ("rq", "rk"):
                    wait_tile(eng, t)
                    if j >= 2:
                        eng.wait_ge(rope_ready, j - 1)
                    do(tt(E[:, j % 2, 0:T], b[:, 0:T], cos, ALU.mult))
                    do(tt(Sp[0:64, j % 2, 0:T], b[64:P, 0:T], sin[64:P], ALU.mult))
                    do(tt(Sp[64:P, j % 2, 0:T], b[0:64, 0:T], sin[0:64], ALU.mult), gemm_dve)
                if 18 <= j <= 33:
                    n = j - 18
                    turned(f"rv{n}", lambda g, p: rvA[0:p, g, n // 2, (n % 2) * P:(n % 2) * P + P])
            heads("r", CH, AH, CV)
            back("r", CH - 1)
            out_tiles("odd_out", 2)
            ffn(1)
            norm(4)

        @block.gpsimd
        def _(eng):
            s = Steps(eng, pool_step)
            do, settle = s.do, s.settle
            tt, copy = nc.gpsimd.tensor_tensor, nc.gpsimd.tensor_copy

            eng.dma_start(sst[:], sconv).then_inc(sst_in, 16)
            eng.dma_start(fst[:], fconv).then_inc(fst_in, 16)
            do(nc.gpsimd.memset(pad[:], 0.0), zeroed)
            do(nc.gpsimd.memset(slab[:], 0.0))
            do(nc.gpsimd.memset(cols[:], 1.0))
            do(nc.gpsimd.memset(vA[:, :, :, AV:AV + 1], 1.0), zeroed)
            settle()

            def load(n):
                if n >= SLOTS:
                    eng.wait_ge(st_out[n % SLOTS], 16 * (n // SLOTS))
                src, w = state_dram(n, False)
                eng.dma_start(state(n)[:, :, 0:w], src).then_inc(st_in[n % SLOTS], 16)

            def zero_attention():
                do(nc.gpsimd.memset(num[:], 0.0))
                do(nc.gpsimd.memset(mv[:], 0.0), zeroed)

            def fill(n, x, kept, w):
                if n >= 4:
                    eng.wait_ge(conv_done, n - 3)
                do(copy(padded(x, w)[:, :, 0:w], kept), fill_done)

            def keep_rows(n, x, dst, w, t):
                wait_tile_empty(eng, t)
                do(copy(dst[:, 0:w], x[:, TP:TP + w]))
                do(copy(dst[:, w:(NB + 1) * w].rearrange("p (b r) -> p b r", b=NB), padded(x, w)[:, :, TS:TS + w]), tail_done)

            def queries(kind, h, hg, q):
                if hg >= 2:
                    kk, hh, _ = HEADS[hg - 2]
                    wait_job(eng, f"{kk}oi{hh}")
                if kind == "r":
                    eng.wait_ge(rope_ready, h + 1)
                do(tt(qTm[:, hg % 2], bc(q[:, TP:T], 1, NB), own, ALU.mult), qm_ready)

            def back(kind, h, Y):
                for i in range(2):
                    n = 2 * h + i
                    eng.wait_ge(yhi_ready, (16 if kind == "r" else 0) + n + 1)
                    hi, lo = Y[n // 8]
                    do(tt(lo[:, n % 8, :], yF[:, n % 2, :], hi[:, n % 8, :].bitcast(F32), ALU.subtract), ylo_ready)

            def heads(kind, count, first, q, Y, w):
                queries(kind, 0, first, q(0))
                for h in range(count):
                    hg = first + h
                    wait_empty(eng, f"{kind}kn{h}")
                    if h:
                        wait_job(eng, f"{kind}ss{h - 1}.{NB - 1}")
                    do(tt(kgm[0:NS], bc(kgs[0:NS], 1, NB), bc(mine[0:NS], 2, P), ALU.mult), kgm_ready)
                    if h + 1 < count:
                        queries(kind, h + 1, hg + 1, q(h + 1))
                    wait_empty(eng, f"{kind}sp{h}")
                    eng.dma_start(cp_out[h] if kind == "a" else rp_out[h], pout[:, hg % 2, 0:w]).then_inc(pout_out[hg % 2], 16)
                    if h:
                        back(kind, h - 1, Y)
                    for x in range(2):
                        n = 2 * hg + x
                        wait_empty(eng, f"{kind}ss{h}.{4 * x + 3}")
                        dst, _ = state_dram(n, True)
                        eng.dma_start(dst, state(n)[:, :, 0:w]).then_inc(st_out[n % SLOTS], 16)
                    for n in range(2 * hg + SLOTS - 1, 2 * hg + SLOTS + 1):
                        if 2 * first + SLOTS <= n < 2 * (first + count):
                            load(n)
                back(kind, count - 1, Y)

            def ffn(l):
                for i in range(2 * KF + 3):
                    n = XB + 2 * KF * l + i
                    if i < 2 * KF:
                        if l == 1 and i == 0:
                            eng.wait_ge(fout_out, 16)
                        fill(n, pad[:, n % 4, 1:], fst[:, l, i, :, :], W2)
                    if i >= 3:
                        m = i - 3
                        keep_rows(n - 3, pad[:, (n - 3) % 4, 1:], fout[:, m, :], W2, START[f"up{l}"] + m)
                eng.wait_ge(tail_done, XB + 2 * KF * (l + 1))
                eng.dma_start(f_out[l], fout[:]).then_inc(fout_out, 16)

            for n in range(3):
                load(n)
            eng.wait_ge(sst_in, 16)
            eng.wait_ge(fst_in, 16)
            eng.wait_ge(const_in, 16)
            for i in range(XB + 3):
                if i < XB:
                    if i >= 4:
                        pass
                    fill(i, pad[:, i % 4, :], sst[:, i], W1)
                if i >= 3:
                    keep_rows(i - 3, pad[:, (i - 3) % 4, :], sout[:, i - 3, :], W1, XBC0 + i - 3)
            eng.wait_ge(slab_ready, 1)
            eng.dma_start(m_out, rsm[0:AH, 1, 0:NB + 1]).then_inc(small_out, 16)
            eng.wait_ge(tail_done, XB)
            eng.dma_start(sconv_out, sout[:]).then_inc(small_out, 16)
            eng.wait_ge(silu_done, XB)
            for n in (3, 4):
                load(n)
            wait_empty(eng, "sdec")
            zero_attention()
            heads("a", AH, 0, lambda h: qT[:, h, :], YA, AV + 1)
            settle()
            for i in range(SLOTS):
                eng.wait_ge(st_out[i], 16 * len(range(i, 2 * AH, SLOTS)))
            for i in range(2):
                eng.wait_ge(pout_out[i], 16 * (AH // 2))

            def load_ssd(n):
                g, b = divmod(n, NB)
                eng.dma_start(sts[n % SSLOTS], h_in[b][:, g * GW:(g + 1) * GW]).then_inc(sts_in[n % SSLOTS], 16)

            for n in range(SSLOTS):
                load_ssd(n)
            for g in range(BG):
                do(tt(cm[:, g], bc(xbcT[:, 10 + g, TP:T], 1, NB), own, ALU.mult), cm_ready if g else None)
            for g in range(BG):
                wait_empty(eng, f"bn{g}")
                do(tt(bm[0:NS, :, g, :], bc(bnat[0:NS, 2, g, :], 1, NB), bc(mine[0:NS], 2, P), ALU.mult), bm_ready)
            for g in range(BG):
                wait_job(eng, f"si{g}")
                for b in range(NB):
                    x = sts[(g * NB + b) % SSLOTS].rearrange("p (h e) -> p h e", h=HG)
                    do(tt(x, x, bc(sdec[:, b, g * HG:(g + 1) * HG], 2, BP), ALU.mult), dec_ready)
                if g == 0:
                    for i in range(BG):
                        wait_empty(eng, f"sp{i}")
                        eng.dma_start(hp_out[:, i * GW:(i + 1) * GW], pst[:, i, :]).then_inc(pst_out, 16)
                for b in range(NB):
                    n = g * NB + b
                    wait_empty(eng, f"su{g}.{b}")
                    eng.dma_start(h_out[b][:, g * GW:(g + 1) * GW], sts[n % SSLOTS]).then_inc(sts_out[n % SSLOTS], 16)
                for n in range(SSLOTS, BG * NB) if g == 0 else ():
                    eng.wait_ge(sts_out[n % SSLOTS], 16)
                    load_ssd(n)
            for i in range(SSLOTS):
                eng.wait_ge(sts_out[i], 16 * len(range(i, BG * NB, SSLOTS)))
            eng.wait_ge(pst_out, 16 * BG)
            eng.wait_ge(ylo_ready, 16)
            do(nc.gpsimd.memset(pad[:], 0.0), zeroed)
            settle()
            ffn(0)
            for j in range(2 * CH):
                i = j % CH
                wait_tile_empty(eng, START["odd"] + j)
                do(tt((rqT if j < CH else rkT)[:, i, :], E[:, j % 2, 0:T], Sp[:, j % 2, 0:T], ALU.add), rope_ready)
            zero_attention()
            for n in range(2 * AH, 2 * AH + SLOTS):
                load(n)
            heads("r", CH, AH, lambda h: rqT[:, h, :], YR, CV)
            for i in range(SLOTS):
                eng.wait_ge(st_out[i], 16 * len(range(i, 2 * (AH + CH), SLOTS)))
            for i in range(2):
                eng.wait_ge(pout_out[i], 16 * ((AH + CH) // 2))
            eng.wait_ge(ylo_ready, 32)
            do(nc.gpsimd.memset(pad[:], 0.0), zeroed)
            settle()
            ffn(1)
            eng.wait_ge(fout_out, 32)
            eng.wait_ge(small_out, 32)


def constants():
    c = np.zeros((P, CONST_W), np.float32)

    def put(name, a):
        at, w = CONSTS[name]
        c[:a.shape[0], at:at + w] = a.reshape(a.shape[0], -1)

    key, query = np.arange(P)[:, None], np.arange(TP)[None, :]
    ns = np.arange(NS)
    put("ident", np.eye(P))
    put("ones", np.ones((P, P)))
    gap = np.full((P, BLK), -1.0)
    gap[:, 0:TP] = query - key
    gap[:, TP:TP + P] = query[:, :P] - key
    same = ns[:, None] // TS == ns[None, :] // TS
    gap[:NS, TP + P:] = np.where(same, ns[None, :] - ns[:, None], -1)
    put("drop", np.where(gap >= 0, 0, -1e30))
    put("dist", np.where(gap >= 0, gap, 1e9))
    put("own", np.broadcast_to(np.arange(NB)[:, None] == ns[None, :] // TS, (P, NB, NS)))
    put("mine", ns[:, None] // TS == np.arange(NB)[None, :])
    inv = (np.float32(10000.0) ** (-np.arange(64, dtype=np.float32) / np.float32(64))).astype(np.float32)
    pos = np.concatenate([np.arange(TP), 2048 + ns % TS]).astype(np.float32)
    angle = (pos[None, :] * inv[:, None]).astype(np.float32).astype(np.float64)
    put("cos", np.concatenate([np.cos(angle)] * 2))
    put("sin", np.concatenate([np.sin(angle), -np.sin(angle)]))
    lg = np.array(LOG_GAMMA)[None, :]
    rk = np.zeros((P, 3, CH))
    for g in range(2):
        rk[:, g] = np.exp(lg * (TP - 1 - g * P - np.arange(P))[:, None])
    rk[:NS, 2] = np.exp(lg * (TS - 1 - ns % TS)[:, None])
    put("retk", rk * KSCALE)
    put("retq", np.exp(lg * (ns % TS + 1)[:, None]))
    return c


def starts():
    first = np.zeros(T)
    first[0] = 1
    first[TP::TS] = 1
    drop = -1e30 * first
    drop[0] = 0
    return np.broadcast_to(np.stack([1 - first, drop]).astype(np.float32), (BH, 2, T))


def kernel(**inputs):
    import concourse.bacc as bacc
    from concourse.bass_utils import run_bass_kernel_spmd

    a = {k: np.asarray(x) for k, x in inputs.items()}

    def tiled(x):
        return np.moveaxis(x.reshape(*x.shape[:-1], -1, P), -1, 0)

    def paired(x):
        n = x.shape[:-1]
        return np.swapaxes(x.reshape(*n, 2, KF, P), -3, -2).reshape(*n, 2 * KF * P)

    tokens = np.concatenate([a["x_prompt"].reshape(TP, D), a["x_sample"].reshape(NS, D)])
    xin = np.ascontiguousarray(np.swapaxes(tiled(tokens), 1, 2))

    def weight_tiles(w):
        k, n = w.shape
        return w.reshape(k // P, P, n // P, P).transpose(2, 0, 1, 3).reshape(-1, P, P)

    w = a["even_w_in"][0]
    gates = np.zeros((D, P), np.float32)
    gates[:, 0:AH] = w[:, 2048:2052]
    gates[:, 32:32 + AH] = w[:, 2052:2056]
    gates[:, 64:64 + BH] = w[:, 5640:5656]
    w_even = np.concatenate([w[:, :2048], gates, w[:, 2056:5640]], axis=1)
    streams = [weight_tiles(w_even), weight_tiles(a["even_w_out"][0]),
               weight_tiles(paired(a["ffn_w_up"][0])), weight_tiles(a["ffn_w_down"][0]),
               weight_tiles(a["odd_w_in"][0]), weight_tiles(a["odd_w_out"][0]),
               weight_tiles(paired(a["ffn_w_up"][1])), weight_tiles(a["ffn_w_down"][1])]
    wts = np.concatenate(streams).reshape(CHUNKS, CHUNK, P, P).transpose(0, 2, 1, 3).reshape(CHUNKS, P, CHUNK * P)

    vecs = np.zeros((P, VEC_W), np.float32)

    def put(name, x):
        at, n = VECS[name]
        vecs[:x.shape[0], at:at + n] = x.reshape(x.shape[0], -1)

    for i, g in enumerate((a["norm_mix_g"][0], a["norm_ffn_g"][0], a["norm_mix_g"][1], a["norm_ffn_g"][1],
                           a["norm_final_g"])):
        put(f"norm{i}", tiled(g))
    put("ag", tiled(a["mlstm_norm_g"][0]))
    put("scw", np.swapaxes(tiled(a["ssd_conv_w"][0]), 1, 2))
    put("scb", tiled(a["ssd_conv_b"][0]))
    put("D", tiled(np.repeat(a["ssd_D"][0], BP)))
    put("sg", tiled(a["ssd_norm_g"][0]))
    put("rg", tiled(a["ret_norm_g"][0]))
    put("fcw", np.swapaxes(tiled(paired(a["ffn_conv_w"])), 2, 3))
    put("fcb", tiled(paired(a["ffn_conv_b"])))
    for name, x in (("igb", a["mlstm_igate_b"]), ("fgb", a["mlstm_fgate_b"]), ("dtb", a["ssd_dt_bias"]),
                    ("alog", a["ssd_A_log"])):
        put(name, x[0][:, None])
    put("m0", a["state_mlstm_m"][0].T)
    vecs[:, VECS["eps"][0]] = EPS

    sconv = np.ascontiguousarray(tiled(a["state_ssd_conv"][0]).transpose(0, 3, 1, 2))
    fconv = np.ascontiguousarray(tiled(paired(a["state_ffn_conv"])).transpose(0, 1, 4, 2, 3))
    c_in = np.concatenate([a["state_mlstm_C"][0], a["state_mlstm_n"][0][..., None]], axis=-1).transpose(1, 2, 0, 3)
    r_in = a["state_ret_S"][0].transpose(1, 2, 0, 3)
    h_in = a["state_ssd_h"][0].reshape(NB, BH * BP, P).transpose(0, 2, 1)
    ins = {"xin": xin, "wts": wts, "consts": constants(), "starts": starts(), "vecs": vecs, "sconv": sconv, "fconv": fconv,
           "c_in": c_in, "r_in": r_in, "h_in": h_in}
    outs = {"y_out": (P, KD, T), "c_out": (AH, P, NB, AV + 1), "cp_out": (AH, P, AV + 1), "m_out": (AH, NB + 1),
            "sconv_out": (P, XB, 27), "h_out": (NB, P, D), "hp_out": (P, D), "r_out": (CH, P, NB, CV),
            "rp_out": (CH, P, CV), "f_out": (2, P, 2 * KF, 18)}
    ins = {k: np.ascontiguousarray(x) for k, x in ins.items()}
    nc = bacc.Bacc("TRN2", target_bir_lowering=False, num_devices=1)
    args = [nc.dram_tensor(k, x.shape, F32, kind="ExternalInput").ap() for k, x in ins.items()]
    args += [nc.dram_tensor(k, s, F32, kind="ExternalOutput").ap() for k, s in outs.items()]
    build(nc, *args)
    r = run_bass_kernel_spmd(nc, [ins], core_ids=[0]).results[0]

    def untiled(x):
        return np.moveaxis(x, 0, -1).reshape(*x.shape[1:-1], -1)

    def unpaired(x):
        return np.swapaxes(x.reshape(*x.shape[:-1], KF, 2, P), -3, -2).reshape(x.shape)

    y = untiled(np.swapaxes(r["y_out"], 1, 2))
    c = r["c_out"].transpose(2, 0, 1, 3)
    cp = r["cp_out"]
    m = r["m_out"]
    sc = untiled(np.swapaxes(r["sconv_out"], 1, 2))
    fc = unpaired(untiled(r["f_out"].transpose(1, 0, 3, 2)))
    h = r["h_out"].transpose(0, 2, 1).reshape(NB, BH, BP, P)
    hp = r["hp_out"].T.reshape(1, BH, BP, P)
    return (y[:TP].reshape(1, TP, D), y[TP:].reshape(NB, TS, D),
            cp[None, None, ..., :AV], cp[None, None, ..., AV], m[:, 0][None, None],
            sc[:W1][None, None], hp[None], r["rp_out"][None, None], fc[:, :W2][:, None],
            c[None, ..., :AV], c[None, ..., AV], m[:, 1:].T[None],
            sc[W1:].reshape(1, NB, W1, -1), h[None], r["r_out"].transpose(2, 0, 1, 3)[None],
            fc[:, W2:].reshape(2, NB, W2, -1))
```

```python
import math
from contextlib import ExitStack

import numpy as np

import concourse.bass as bass
from concourse import mybir

F32 = mybir.dt.float32
F32R = mybir.dt.float32r
ALU = mybir.AluOpType
ACT = mybir.ActivationFunctionType

P = 128
D = 1024
KD = D // P
TP, NB, TS = 256, 8, 4
NS = NB * TS
T = TP + NS
EPS = 1e-6
AH, AV = 4, 256
CH, CV = 8, 256
BH, BP, BG = 16, 64, 2
HG = BH // BG
GW = HG * BP
KSCALE = P ** -0.5
FF = 2816
KF = FF // P
XB = 12
W1, W2 = 3, 2
CHUNK = 8
RING = 4
SI0, SU0 = 6, BH - NB
TOGETHER = {"a": 1, "r": 2}
DECAY_DVE = (1, 4)
SLOTS = 5
SSLOTS = 11
BLK = 2 * P + P + NS
LOG_GAMMA = [math.log1p(-2.0 ** (-5.0 - h)) for h in range(CH)]

EVEN = [("q", i) for i in range(AH)] + [("k", i) for i in range(AH)] + [("v", i) for i in range(8)] \
    + [("gates", 0)] + [("og", i) for i in range(8)] + [("z", i) for i in range(8)] \
    + [("xbc", i) for i in range(XB)]
ODD = [("rq", i) for i in range(CH)] + [("rk", i) for i in range(CH)] + [("rv", i) for i in range(16)] \
    + [("rg", i) for i in range(16)]
UP = [("up", i) for i in range(2 * KF)]
OUT = [("out", i) for i in range(KD)]
PHASES = [("even", EVEN, KD), ("even_out", OUT, 16), ("up0", UP, KD), ("down0", OUT, KF),
          ("odd", ODD, KD), ("odd_out", OUT, 16), ("up1", UP, KD), ("down1", OUT, KF)]


def plan_tiles():
    tiles, start, at = [], {}, 0
    for phase, kinds, k in PHASES:
        start[phase] = len(tiles)
        for n, (kind, i) in enumerate(kinds):
            first = at + n * k
            if k == 2 * CHUNK:
                first = at + (n // 4) * 4 * k + (n % 4) * CHUNK
            tiles.append((phase, kind, i, k, first))
        at += len(kinds) * k
    assert at % CHUNK == 0
    return tiles, start, at // CHUNK


TILES, START, CHUNKS = plan_tiles()
BY_DVE = ("gates", "out", "rq", "rk")


def place(t, k):
    K, first = TILES[t][3:]
    if K == 2 * CHUNK:
        return first // CHUNK + 4 * (k // CHUNK), k % CHUNK
    return divmod(first + k, CHUNK)


def last_chunk(t):
    return place(t, TILES[t][3] - 1)[0]


def parts():
    t = 0
    while t < len(TILES):
        K = TILES[t][3]
        if K == 2 * CHUNK:
            for half in range(2):
                for u in range(t, t + 4):
                    yield u, half * CHUNK, (half + 1) * CHUNK
            t += 4
        else:
            yield t, 0, K
            t += 1


def emptied_by(t):
    return "dve" if TILES[t][1] in BY_DVE else "act"


EMPTIED = []
for _t in range(len(TILES)):
    EMPTIED.append(1 + sum(emptied_by(u) == emptied_by(_t) for u in range(_t)))

JOBS = []


def _jobs():
    def job(name, by):
        JOBS.append((name, by))

    def front(kind, h):
        job(f"{kind}sc{h}", "dve")
        job(f"{kind}kn{h}", "act")

    def heads(kind, n, tail=()):
        if kind == "a":
            job("abc0", "act")
            job("abc1", "act")
        front(kind, 0)
        if kind == "a":
            job("abc2", "act")
        for h in range(n):
            if kind == "a" and 2 < h + 2 < n:
                job(f"abc{h + 2}", "act")
            job(f"{kind}o0{h}", "act")
            job(f"{kind}o1{h}", "act")
            job(f"{kind}sp{h}", "act")
            if h + 1 < n:
                front(kind, h + 1)
            job(f"{kind}oi{h}", "act")
            job(f"{kind}os{h}", "dve")
            for b in range(TOGETHER[kind] - 1, NB, TOGETHER[kind]):
                job(f"{kind}ss{h}.{b}", "dve")
            if h:
                turned_back(kind, h - 1)
        for name, by in tail:
            job(name, by)
        turned_back(kind, n - 1)

    def turned_back(kind, h):
        for i in range(2):
            job(f"{kind}yt{2 * h + i}", "dve")

    job("norm0", "act")
    for i in range(8):
        job(f"v{i}", "dve")
    for name in ("col0", "col1", "adec", "sdec"):
        job(name, "dve")
    heads("a", AH, [(name, "act") for name in ("cb0", "cb1", "bn0", "bn1", "sbc0", "sbc1")] + [("xn0", "dve"), ("xn1", "dve")])
    for h in range(BH):
        if h + 2 < BH:
            job(f"sbc{h + 2}", "act")
        if h < 6:
            job(f"xn{h + 2}", "dve")
        job(f"say{h}", "act" if h >= SU0 else "dve")
        if h == SI0:
            job("si0", "dve")
        if h >= SU0:
            job(f"su0.{h - SU0}", "dve")
    job("si1", "dve")
    job("sp0", "act")
    job("sp1", "act")
    for b in range(NB):
        job(f"su1.{b}", "dve")
    for i in range(8):
        job(f"sy{i}", "dve")
    for g in range(BG):
        job(f"sn{g}", "act")
    job("norm1", "act")
    job("norm2", "act")
    for i in range(16):
        job(f"rv{i}", "dve")
    heads("r", CH)
    job("norm3", "act")
    job("norm4", "act")


_jobs()
JOB = {name: n for n, (name, _) in enumerate(JOBS)}
JOB_EMPTIED = [1 + sum(by == JOBS[n][1] for _, by in JOBS[:n]) for n in range(len(JOBS))]

BEFORE, BANK, SSD_LAST = {}, {}, {}
_turns = {"mix": [], "gemm": []}
for _name, _ in JOBS:
    _ring = "gemm" if _name.startswith(("xn", "say")) else "mix"
    _n = len(_turns[_ring])
    BANK[_name] = (_ring, _n % 4)
    BEFORE[_name] = _turns[_ring][_n - 4] if _n >= 4 else None
    _turns[_ring].append(_name)
    if _ring == "gemm":
        SSD_LAST[_n % 4] = _name

CONSTS = {}
_at = 0
for _name, _w in (("ident", P), ("ones", P), ("drop", BLK), ("dist", BLK), ("own", NB * NS), ("mine", NB),
                  ("cos", T), ("sin", T), ("retk", 3 * CH), ("retq", CH)):
    CONSTS[_name] = (_at, _w)
    _at += _w
CONST_W = _at
VECS = {}
_at = 0
for _name, _w in (("norm0", 8), ("norm1", 8), ("norm2", 8), ("norm3", 8), ("norm4", 8), ("ag", 8),
                  ("scw", XB * 4), ("scb", XB), ("D", 8), ("sg", 8), ("rg", 16), ("fcw", 2 * 44 * 3),
                  ("fcb", 2 * 44), ("igb", 1), ("fgb", 1), ("dtb", 1), ("alog", 1), ("m0", NB), ("eps", 1)):
    VECS[_name] = (_at, _w)
    _at += _w
VEC_W = _at


CHUNK_READ = {}
_mid = 0
for _t, _k0, _k1 in parts():
    for _k in range(_k0, _k1):
        _c, _pos = place(_t, _k)
        if _pos == CHUNK - 1:
            _last = _k == TILES[_t][3] - 1
            _mid += not _last
            CHUNK_READ[_c] = ("tile", _t + 1) if _last else ("mid", _mid)
E_OUT, R_IN, R_OUT = (place(START[_p], 0)[0] for _p in ("even_out", "odd", "odd_out"))


def build(nc, xin, wts, consts, starts, vecs, sconv, fconv, c_in, r_in, h_in,
          y_out, c_out, cp_out, m_out, sconv_out, h_out, hp_out, r_out, rp_out, f_out):
    ctx = ExitStack()
    with ctx:
        words = nc.sbuf_bytes_remaining // 4 - 32
        at0 = nc.sbuf_base
        ctx.enter_context(nc.sbuf_tensor("arena", [P, words], F32))
        top = at0 + 4 * words

        class Area:

            def __init__(self, at):
                self.at = (at + 31) // 32 * 32

            def take(self, name, shape, dt=F32):
                t = nc.alloc_sbuf_tensor_at(name, shape, dt, offset=self.at)
                self.at += (int(np.prod(shape[1:])) * 4 + 31) // 32 * 32
                assert self.at <= top, name
                return t

        keep = Area(at0)
        xT = keep.take("xT", [P, KD, T])
        hH = keep.take("hH", [P, KD, T], F32R)
        hL = keep.take("hL", [P, KD, T], F32R)
        hF = keep.take("hF", [P, KD, T])
        raw = keep.take("raw", [P, RING, CHUNK * P])
        wh = keep.take("wh", [P, RING, CHUNK * P], F32R)
        wl = keep.take("wl", [P, RING, CHUNK * P], F32R)
        cst = keep.take("cst", [P, CONST_W])
        vec = keep.take("vec", [P, VEC_W])
        sst = keep.take("sst", [P, XB, NB, W1])
        fst = keep.take("fst", [P, 2, 2 * KF, NB, W2])
        at_fout = keep.at
        fout = keep.take("fout", [P, 2 * KF, (NB + 1) * W2])
        sout = keep.take("sout", [P, XB, (NB + 1) * W1])
        xt = nc.alloc_sbuf_tensor_at("xt", [P, D], F32, offset=at_fout)
        rstd = keep.take("rstd", [P, T])

        conv = Area(keep.at)
        pad = conv.take("pad", [P, 4, 320])
        cy = conv.take("cy", [P, 4, 312])
        ffn = Area(conv.at)
        sgate = ffn.take("sgate", [P, 2, 312])
        hidF = ffn.take("hidF", [P, 3, T])
        HH = ffn.take("HH", [P, KF, T], F32R)
        HL = ffn.take("HL", [P, KF, T], F32R)

        att = Area(conv.at)
        E = att.take("E", [P, 2, BLK])
        Sp = att.take("Sp", [P, 2, BLK])
        qTm = att.take("qTm", [P, 2, NB, NS])
        kg = att.take("kg", [P, 2, 2, P])
        kgm = att.take("kgm", [P, NB, P], F32R)
        at_num = att.at
        num = att.take("num", [P, 2, 3, AV + 1])
        at_pout = att.at
        pout = att.take("pout", [P, 2, AV + 1])
        vT = nc.alloc_sbuf_tensor_at("vT", [P, 2, T], F32, offset=att.at)
        yF = att.take("yF", [P, 2, T])
        kgs = att.take("kgs", [P, P])
        kst = att.take("kst", [P, P], F32R)
        vst = att.take("vst", [P, AV + 2], F32R)
        stats = att.take("stats", [P, 3, 6])
        mv = att.take("mv", [P, 3, 2])
        sm = att.take("sm", [P, 8, 3])
        st = [att.take(f"st{i}", [P, 4, AV + 1]) for i in range(3)]
        early = Area(keep.at)
        st_a = st + [early.take(f"st{i}", [P, 4, AV + 1]) for i in (3, 4)]
        assert early.at <= conv.at

        ml = Area(att.at)
        qT = ml.take("qT", [P, AH, T])
        kT = ml.take("kT", [P, AH, T])
        vA = ml.take("vA", [P, 3, AH, AV + 1])
        y2 = Area(att.at)
        YH = y2.take("YH", [P, 8, T], F32R)
        YL = y2.take("YL", [P, 8, T], F32R)
        even = Area(max(ml.at, y2.at))
        xbcT = even.take("xbcT", [P, XB, T])
        zT = even.take("zT", [P, 8, T])
        cols = even.take("cols", [P, 3, 2 * P])
        adec = even.take("adec", [P, AH, NB])
        sdec = even.take("sdec", [P, NB, BH])
        nM = even.take("nM", [P, T])
        drop = even.take("drop", [P, BLK], F32R)
        identR = even.take("identR", [P, P], F32R)
        ac = even.take("ac", [P, T])
        rsm = even.take("rsm", [P, 6, 16])

        rw = Area(conv.at)
        slab = rw.take("slab", [P, 2, T])
        rows = rw.take("rows", [P, 9, T])
        dg = rw.take("dg", [P, NB, BH])
        resets = rw.take("resets", [P, 2, T])
        assert rw.at <= at_pout

        sd = Area(keep.at)
        cm = sd.take("cm", [P, BG, NB, NS])
        bnat = sd.take("bnat", [P, 3, BG, P])
        itmp = sd.take("itmp", [P, GW])
        xws = sd.take("xws", [P, D], F32R)
        bst = sd.take("bst", [P, BG, P], F32R)
        sd.at = max(sd.at, conv.at)
        xdt = sd.take("xdt", [P, 3, D])
        assert sd.at <= at_num
        sd = Area(at_num)
        bm = sd.take("bm", [P, NB, BG, P], F32R)
        sts = [sd.take(f"sts{i}", [P, GW])[:] for i in range(SSLOTS - 4)]
        sts += [hF[:, 2 * i:2 * i + 2, :].rearrange("p a t -> p (a t)")[:, 0:GW] for i in range(4)]
        assert sd.at <= att.at
        sd = Area(at_num)
        rst2 = sd.take("rst2", [P, BG, T])
        ty = sd.take("ty", [P, 2, T])
        sd = Area(att.at)
        pst = nc.alloc_sbuf_tensor_at("pst", [P, 2, GW], F32, offset=sd.at)
        E2 = sd.take("E2", [P, 3, BLK])
        cbm = sd.take("cbm", [P, BG, BLK])
        yn = sd.take("yn", [P, 3, D])
        assert sd.at <= ml.at

        odd = Area(att.at)
        rqT = odd.take("rqT", [P, CH, T])
        rkT = odd.take("rkT", [P, CH, T])
        rvA = odd.take("rvA", [P, 3, CH, CV])
        st_r = st + [odd.take(f"st{i}r", [P, 4, AV + 1]) for i in (3, 4)]
        gT = nc.alloc_sbuf_tensor_at("gT", [P, 8, T], F32, offset=keep.at)
        y3 = Area(att.at)
        RH = y3.take("RH", [P, 8, T], F32R)
        RL = y3.take("RL", [P, 8, T], F32R)

        def const(name):
            at, w = CONSTS[name]
            return cst[:, at:at + w]

        def v(name, i=0, p=P):
            return vec[0:p, VECS[name][0] + i:VECS[name][0] + i + 1]

        ident, ones, dist = (const(n) for n in ("ident", "ones", "dist"))
        own = const("own").rearrange("p (b l) -> p b l", b=NB)
        mine = const("mine")
        m0 = vec[0:AH, VECS["m0"][0]:VECS["m0"][0] + NB]

        bank = [ctx.enter_context(nc.psum_tensor(f"gemm{i}", [P, 512], F32)) for i in range(4)]
        mixb = [ctx.enter_context(nc.psum_tensor(f"mix{i}", [P, 512], F32)) for i in range(4)]

        def mb(name):
            ring, i = BANK[name]
            return (mixb if ring == "mix" else bank)[i]

        def sem(name):
            return ctx.enter_context(nc.semaphore(name))

        resets_in, kgm_ready, cm_ready = sem("resets_in"), sem("kgm_ready"), sem("cm_ready")
        x_in = [sem(f"x_in{i}") for i in range(2)]
        const_in, table_in, vec_in = sem("const_in"), sem("table_in"), sem("vec_in")
        sst_in, fst_in = sem("sst_in"), sem("fst_in")
        raw_in = [sem(f"raw_in{i}") for i in range(RING)]
        st_in = [sem(f"st_in{i}") for i in range(SLOTS)]
        st_out = [sem(f"st_out{i}") for i in range(SLOTS)]
        sts_in = [sem(f"sts_in{i}") for i in range(SSLOTS)]
        sts_out = [sem(f"sts_out{i}") for i in range(SSLOTS)]
        pout_out = [sem(f"pout_out{i}") for i in range(2)]
        pst_out, fout_out, small_out, y_stored = (sem(n) for n in ("pst_out", "fout_out", "small_out", "y_stored"))
        act_step, dve_step, pool_step = sem("act_step"), sem("dve_step"), sem("pool_step")
        hi_ready, lo_ready, mid_read = sem("hi_ready"), sem("lo_ready"), sem("mid_read")
        gemm_done, mix_done = sem("gemm_done"), sem("mix_done")
        gemm_act, gemm_dve = sem("gemm_act"), sem("gemm_dve")
        mix_act, mix_dve = sem("mix_act"), sem("mix_dve")
        x_ready, sq_ready, rstd_ready = sem("x_ready"), sem("sq_ready"), sem("rstd_ready")
        h_ready, xhi_ready, xlo_ready = sem("h_ready"), sem("xhi_ready"), sem("xlo_ready")
        zeroed, fill_done, tail_done, conv_done = (sem(n) for n in ("zeroed", "fill_done", "tail_done", "conv_done"))
        silu_done, hid_ready, hidhi_ready, hidlo_ready = (sem(n) for n in ("silu_done", "hid_ready", "hidhi_ready", "hidlo_ready"))
        row_dve, row_act, slab_ready = sem("row_dve"), sem("row_act"), sem("slab_ready")
        exp_ready, drop_ready, qm_ready = sem("exp_ready"), sem("drop_ready"), sem("qm_ready")
        var_ready, inv_ready, yn_ready = sem("var_ready"), sem("inv_ready"), sem("yn_ready")
        yhi_ready, ylo_ready = sem("yhi_ready"), sem("ylo_ready")
        xws_ready, exp2_ready, e_ready, xw_ready = (sem(n) for n in ("xws_ready", "exp2_ready", "e_ready", "xw_ready"))
        dec_ready, ynat_ready, bm_ready = sem("dec_ready"), sem("ynat_ready"), sem("bm_ready")
        zq_ready, sq2_ready, srs_ready, yg_ready = (sem(n) for n in ("zq_ready", "sq2_ready", "srs_ready", "yg_ready"))
        rope_ready, y_ready = sem("rope_ready"), sem("y_ready")

        ROW = [slice(i * NS, (i + 1) * NS) for i in range(3)]
        STACK = slice(0, 3 * NS)
        kst_hi, klo_ready = sem("kst_hi"), sem("klo_ready")
        vst_hi, vst_ready = sem("vst_hi"), sem("vst_ready")
        xt_ready, xst_hi, bst_hi = sem("xt_ready"), sem("xst_hi"), sem("bst_hi")

        class Steps:

            def __init__(self, eng, own_sem):
                self.eng, self.own, self.count, self.last = eng, own_sem, {}, None

            def do(self, ins, s=None):
                s = self.own if s is None else s
                self.count[s.name] = self.count.get(s.name, 0) + 1
                ins.then_inc(s, 1)
                self.last = (s, self.count[s.name])

            def settle(self):
                self.eng.wait_ge(*self.last)

        def wait_tile(eng, t):
            eng.wait_ge(gemm_done, t + 1)

        def wait_tile_empty(eng, t):
            eng.wait_ge(gemm_act if emptied_by(t) == "act" else gemm_dve, EMPTIED[t])

        def wait_job(eng, name):
            eng.wait_ge(mix_done, JOB[name] + 1)

        def wait_empty(eng, name):
            n = JOB[name]
            eng.wait_ge(mix_act if JOBS[n][1] == "act" else mix_dve, JOB_EMPTIED[n])

        def wait_read(eng, c):
            kind, n = CHUNK_READ[c]
            eng.wait_ge(gemm_done if kind == "tile" else mid_read, n)

        def smp(ap):
            return ap[:, TP:T].rearrange("p (b t) -> p b t", b=NB)

        def padded(ap, w, at=0):
            s = at + w + TP
            return ap[:, s:s + NB * (w + TS)].rearrange("p (b t) -> p b t", b=NB)

        def bc(ap, axis, n):
            a = ap.unsqueeze(axis)
            return a.broadcast_to([*a.shape[:axis], n, *a.shape[axis + 1:]])

        YA = ((hH, hL), (YH, YL))
        YR = ((hH, hL), (RH, RL))
        T0 = START["even"]
        XBC0 = T0 + 33
        COLS = T0 + 27
        FRONT = T0 + 30

        HEADS = [("a", h, h) for h in range(AH)] + [("r", h, AH + h) for h in range(CH)]

        def state_dram(n, out):
            hg, x = divmod(n, 2)
            kind, h, _ = HEADS[hg]
            t = (c_out if out else c_in) if kind == "a" else (r_out if out else r_in)
            w = AV + 1 if kind == "a" else CV
            return t[h][:, 4 * x:4 * x + 4, :], w

        def state(n):
            return (st_a if HEADS[n // 2][0] == "a" else st_r)[n % SLOTS]

        block = ctx.enter_context(nc.Block())

        @block.sync
        def _(sp):
            at = [0]

            def stream(end):
                while at[0] < end:
                    c = at[0]
                    if c >= RING:
                        sp.wait_ge(lo_ready, c - RING + 1)
                    sp.dma_start(raw[:, c % RING, :], wts[c]).then_inc(raw_in[c % RING], 16)
                    at[0] += 1

            def load(n):
                if n >= SLOTS:
                    sp.wait_ge(st_out[n % SLOTS], 16 * (n // SLOTS))
                src, w = state_dram(n, False)
                sp.dma_start(state(n)[:, :, 0:w], src).then_inc(st_in[n % SLOTS], 16)

            def heads(kind, count, first, w):
                for h in range(count):
                    hg = first + h
                    wait_empty(sp, f"{kind}sp{h}")
                    sp.dma_start(cp_out[h] if kind == "a" else rp_out[h], pout[:, hg % 2, 0:w]).then_inc(pout_out[hg % 2], 16)
                    for x in range(2):
                        n = 2 * hg + x
                        wait_empty(sp, f"{kind}ss{h}.{4 * x + 3}")
                        dst, _ = state_dram(n, True)
                        sp.dma_start(dst, state(n)[:, :, 0:w]).then_inc(st_out[n % SLOTS], 16)
                    for n in range(2 * hg + SLOTS - 1, 2 * hg + SLOTS + 1):
                        if 2 * first + SLOTS <= n < 2 * (first + count):
                            load(n)

            def load_ssd(n):
                g, b = divmod(n, NB)
                sp.dma_start(sts[n % SSLOTS], h_in[b][:, g * GW:(g + 1) * GW]).then_inc(sts_in[n % SSLOTS], 16)

            for i in range(2):
                half = slice(i * KD // 2, (i + 1) * KD // 2)
                sp.dma_start(xT[:, half, :], xin[:, half, :]).then_inc(x_in[i], 16)
                if i == 0:
                    sp.dma_start(cst[:, 0:2 * P], consts[:, 0:2 * P]).then_inc(const_in, 16)
            stream(2)
            sp.dma_start(vec[:], vecs).then_inc(vec_in, 16)
            stream(RING)
            sp.dma_start(cst[:, 2 * P:], consts[:, 2 * P:]).then_inc(table_in, 16)
            sp.dma_start(resets[0:BH], starts).then_inc(resets_in, 16)
            stream(16)
            for n in range(3):
                load(n)
            stream(E_OUT + 2 * RING)
            sp.wait_ge(silu_done, XB)
            sp.wait_ge(tail_done, XB)
            for n in (3, 4):
                load(n)
            heads("a", AH, 0, AV + 1)
            sp.wait_ge(ylo_ready, 8)
            for i in range(SLOTS):
                sp.wait_ge(st_out[i], 16 * len(range(i, 2 * AH, SLOTS)))
            for i in range(2):
                sp.wait_ge(pout_out[i], 16 * (AH // 2))
            for n in range(SSLOTS):
                load_ssd(n)
            for n in range(BG * NB):
                g, b = divmod(n, NB)
                if n == NB:
                    for i in range(BG):
                        wait_empty(sp, f"sp{i}")
                        sp.dma_start(hp_out[:, i * GW:(i + 1) * GW], pst[:, i, :]).then_inc(pst_out, 16)
                wait_empty(sp, f"su{g}.{b}")
                sp.dma_start(h_out[b][:, g * GW:(g + 1) * GW], sts[n % SSLOTS]).then_inc(sts_out[n % SSLOTS], 16)
                m = n + SSLOTS - 2
                if SSLOTS <= m < BG * NB:
                    sp.wait_ge(sts_out[m % SSLOTS], 16)
                    load_ssd(m)
                if n == NB - 1:
                    for m in range(n + SSLOTS - 1, BG * NB):
                        sp.wait_ge(sts_out[m % SSLOTS], 16)
                        load_ssd(m)
            stream(R_IN + 16)
            for n in range(2 * AH, 2 * AH + SLOTS):
                load(n)
            stream(R_OUT + 2 * RING)
            heads("r", CH, AH, CV)
            stream(CHUNKS)
            for i in range(0, KD, 2):
                sp.wait_ge(y_ready, i + 2)
                sp.dma_start(y_out[:, i:i + 2, :], hF[:, i:i + 2, :]).then_inc(y_stored, 16)
            sp.wait_ge(y_stored, 16 * KD // 2)

        @block.tensor
        def _(pe):
            mm = nc.tensor.matmul

            def tiles(ts, rhs, operand=None, k0=0, k1=None):
                K = TILES[ts[0]][3]
                k1 = K if k1 is None else k1
                for t in ts:
                    if t >= 4 and k0 == 0:
                        wait_tile_empty(pe, t - 4)
                    if 0 <= t - START["even_out"] < 4 and k0 == 0:
                        wait_empty(pe, SSD_LAST[t % 4])
                for k in range(k0, k1):
                    if operand is not None:
                        pe.wait_ge(operand[0], operand[1] + k + 1)
                    for t in ts:
                        out = bank[t % 4][:, 0:T]
                        c, pos = place(t, k)
                        if k == k0 or pos == 0:
                            pe.wait_ge(lo_ready, c + 1)
                        xh, xl = rhs(k)
                        h = wh[:, c % RING, pos * P:(pos + 1) * P]
                        lo = wl[:, c % RING, pos * P:(pos + 1) * P]
                        mm(out, h, xh, start=(k == 0), stop=False)
                        mm(out, h, xl, start=False, stop=False)
                        last = mm(out, lo, xh, start=False, stop=(k == K - 1))
                        if k == K - 1:
                            last.then_inc(gemm_done, 1)
                        elif pos == CHUNK - 1:
                            last.then_inc(mid_read, 1)

            def out_part(phase, half, which, rhs, operand=None):
                for n, i in enumerate(which):
                    tiles([START[phase] + i], rhs, operand if n == 0 else None, half * CHUNK, (half + 1) * CHUNK)

            def out_rest(phase, rhs, operand):
                t = START[phase]
                tiles([t, t + 1], rhs, operand, CHUNK, 2 * CHUNK)
                out_part(phase, 1, range(2, 4), rhs)
                for half in range(2):
                    out_part(phase, half, range(4, KD), rhs)

            turn_of = [0]

            def free_bank(name):
                n = JOB[name]
                assert n == turn_of[0], name
                turn_of[0] += 1
                if BEFORE[name] is not None:
                    wait_empty(pe, BEFORE[name])
                elif BANK[name][0] == "gemm":
                    t = START["even_out"] - 4
                    wait_tile_empty(pe, t + (BANK[name][1] - t) % 4)
                return mb(name)

            def norm(n):
                out = free_bank(f"norm{n}")[:, 0:T]
                for i in range(KD):
                    pe.wait_ge(sq_ready, KD * n + i + 1)
                    last = mm(out, ones, hF[:, i, :], start=(i == 0), stop=(i == KD - 1))
                last.then_inc(mix_done, 1)

            def normed(k):
                return hH[:, k, :], hL[:, k, :]

            def turn(name, src):
                out = free_bank(name)
                for g, (a, n) in enumerate(((0, P), (P, P), (TP, NS))):
                    last = nc.tensor.transpose(out[0:n, g * P:(g + 1) * P], src[:, a:a + n], ident)
                last.then_inc(mix_done, 1)

            def turn_back(name, src):
                out = free_bank(name)
                for g, (a, n) in enumerate(((0, P), (P, P), (TP, NS))):
                    last = nc.tensor.transpose(out[:, a:a + n], src(g)[0:n], ident[0:n, 0:n])
                last.then_inc(mix_done, 1)

            def scores(out, k, q):
                mm(out[:, 0:TP], k[:, 0:P], q[:, 0:TP], start=True, stop=True)
                mm(out[:, TP:TP + P], k[:, P:TP], q[:, P:TP], start=True, stop=True)
                return mm(out[0:NS, TP + P:BLK], k[:, TP:T], q[:, TP:T], start=True, stop=True)

            def log_rows(name, rows, n, h):
                out = free_bank(name)
                one = ident[0:n, h:h + 1].broadcast_to([n, P])
                mm(out[:, 0:BLK], identR[:], drop[:], start=True, stop=False)
                mm(out[:, 0:TP], one, rows[0:n, 0:TP], start=False, stop=False)
                mm(out[:, TP:BLK], one, rows[0:n, P:T], start=False, stop=True).then_inc(mix_done, 1)

            def row_max(h):
                log_rows(f"abc{h}", nM, AH, h)

            def front(kind, h, qk):
                q, k = qk(h)
                if kind == "r":
                    pe.wait_ge(rope_ready, CH + h + 1)
                out = free_bank(f"{kind}sc{h}")
                scores(out, k, q).then_inc(mix_done, 1)
                turn(f"{kind}kn{h}", k)

            def middle(kind, h, hg, va, w, ahead):
                s = Sp[:, hg % 2, :]
                wait_empty(pe, f"{kind}sc{h}")
                out = free_bank(f"{kind}o0{h}")
                mm(out[:, 0:w], s[:, 0:P], va(0), start=True, stop=True).then_inc(mix_done, 1)
                out = free_bank(f"{kind}o1{h}")
                mm(out[:, 0:w], s[:, P:TP], va(0), start=True, stop=False)
                mm(out[:, 0:w], s[:, TP:TP + P], va(1), start=False, stop=True).then_inc(mix_done, 1)
                out = free_bank(f"{kind}sp{h}")
                wait_empty(pe, f"{kind}kn{h}")
                mm(out[:, 0:w], kg[:, hg % 2, 0, :], va(0), start=True, stop=False)
                mm(out[:, 0:w], kg[:, hg % 2, 1, :], va(1), start=False, stop=True).then_inc(mix_done, 1)
                if ahead is not None:
                    ahead()
                out = free_bank(f"{kind}oi{h}")
                pe.wait_ge(qm_ready, hg + 1)
                for b in range(NB):
                    n = 2 * hg + b // 4
                    pe.wait_ge(st_in[n % SLOTS], 16 * (n // SLOTS + 1))
                    last = mm(out[0:NS, 0:w], qTm[:, hg % 2, b, :], state(n)[:, b % 4, 0:w],
                              start=(b == 0), stop=(b == NB - 1))
                last.then_inc(mix_done, 1)
                out = free_bank(f"{kind}os{h}")
                mm(out[0:NS, 0:w], s[0:NS, TP + P:BLK], va(2)[0:NS], start=True, stop=True).then_inc(mix_done, 1)
                pe.wait_ge(kgm_ready, hg + 1)
                pe.wait_ge(vst_ready, hg + 1)
                even, m = w + w % 2, TOGETHER[kind]
                for b in range(m - 1, NB, m):
                    out = free_bank(f"{kind}ss{h}.{b}")
                    for i in range(m):
                        last = mm(out[:, i * even:(i + 1) * even], kgm[STACK, b - m + 1 + i, :], vst[STACK, 0:even],
                                  start=True, stop=True)
                    last.then_inc(mix_done, 1)
                if h:
                    back(kind, h - 1, hg - 1)

            def back(kind, h, hg):
                pe.wait_ge(yn_ready, hg + 1)
                for i in range(2):
                    turn_back(f"{kind}yt{2 * h + i}", lambda g: num[:, hg % 2, g, i * P:(i + 1) * P])

            def heads(kind, n, first, qk, va, w):
                for h in range(n):
                    if kind == "a" and 2 < h + 2 < n:
                        row_max(h + 2)
                    middle(kind, h, first + h, lambda g: va(g, h), w, (lambda: front(kind, h + 1, qk)) if h + 1 < n else None)

            def ffn(l):
                norm(2 * l + 1)
                t0 = START[f"up{l}"]
                tiles([t0, t0 + 1], normed, (xlo_ready, KD * (2 * l + 1)))
                for i in range(2, 2 * KF):
                    tiles([t0 + i], normed)
                for i in range(KD):
                    tiles([START[f"down{l}"] + i], lambda k: (HH[:, k, :], HL[:, k, :]),
                          (hidlo_ready, KF * l) if i == 0 else None)

            def qk_a(h):
                return qT[:, h, :], kT[:, h, :]

            def gate_columns():
                pe.wait_ge(slab_ready, 1)
                for s in range(2):
                    turn(f"col{s}", slab[:, s, :])
                out = free_bank("adec")
                for h in range(AH):
                    last = mm(out[:, h * NB:(h + 1) * NB], ident[0:AH, h:h + 1].broadcast_to([AH, P]),
                              rsm[0:AH, 2, 0:NB], start=True, stop=True)
                last.then_inc(mix_done, 1)
                out = free_bank("sdec")
                mm(out[:, 0:NB * BH], ones[0:BH, :], dg[0:BH, :, :].rearrange("p b h -> p (b h)"),
                   start=True, stop=True).then_inc(mix_done, 1)

            pe.wait_ge(const_in, 16)
            norm(0)
            tiles([T0, T0 + 1], normed, (xlo_ready, 0))
            for t in range(T0 + 2, START["even_out"]):
                if t == COLS:
                    gate_columns()
                if t == FRONT:
                    pe.wait_ge(drop_ready, 1)
                    row_max(0)
                    row_max(1)
                    front("a", 0, qk_a)
                    row_max(2)
                tiles([t], normed)
                if 9 <= t <= 16:
                    wait_tile_empty(pe, t - 1)
                    turn(f"v{t - 9}", vT[:, (t - 9) % 2, :])
            heads("a", AH, 0, qk_a, lambda g, h: vA[:, g, h, :], AV + 1)
            pe.wait_ge(silu_done, XB)
            for g in range(BG):
                out = free_bank(f"cb{g}")
                scores(out, xbcT[:, 8 + g, :], xbcT[:, 10 + g, :]).then_inc(mix_done, 1)
            for g in range(BG):
                turn(f"bn{g}", xbcT[:, 8 + g, :])

            def sbc(h):
                log_rows(f"sbc{h}", ac, BH, h)

            sbc(0)
            sbc(1)
            for i in range(2):
                turn(f"xn{i}", xbcT[:, i, :])
            back("a", AH - 1, AH - 1)

            def say(h):
                out = free_bank(f"say{h}")
                pe.wait_ge(e_ready, h + 1)
                e = E2[:, h % 3, :]
                x = xdt[:, :, h * BP:(h + 1) * BP]
                mm(out[:, 0:BP], e[:, 0:P], x[:, 0, :], start=True, stop=True)
                mm(out[:, BP:2 * BP], e[:, P:TP], x[:, 0, :], start=True, stop=False)
                mm(out[:, BP:2 * BP], e[:, TP:TP + P], x[:, 1, :], start=False, stop=True)
                mm(out[0:NS, 2 * BP:3 * BP], e[0:NS, TP + P:BLK], x[0:NS, 2, :], start=True, stop=True)\
                    .then_inc(mix_done, 1)

            def si(g):
                out = free_bank(f"si{g}")
                pe.wait_ge(cm_ready, 1)
                for b in range(NB):
                    n = g * NB + b
                    pe.wait_ge(sts_in[n % SSLOTS], 16 * (n // SSLOTS + 1))
                    last = mm(out[0:NS, :], cm[:, g, b, :], sts[n % SSLOTS], start=(b == 0), stop=(b == NB - 1))
                last.then_inc(mix_done, 1)

            def sp_(g):
                sl = slice(g * GW, (g + 1) * GW)
                out = free_bank(f"sp{g}")
                mm(out[:, :], bnat[:, 0, g, :], xdt[:, 0, sl], start=True, stop=False)
                mm(out[:, :], bnat[:, 1, g, :], xdt[:, 1, sl], start=False, stop=True).then_inc(mix_done, 1)

            def su(g, b):
                sl = slice(g * GW, (g + 1) * GW)
                out = free_bank(f"su{g}.{b}")
                mm(out[:, :], bm[STACK, b, g, :], xws[STACK, sl], start=True, stop=True).then_inc(mix_done, 1)

            for h in range(BH):
                if h + 2 < BH:
                    sbc(h + 2)
                if h < 6:
                    turn(f"xn{h + 2}", xbcT[:, h + 2, :])
                say(h)
                if h == SI0:
                    si(0)
                if h == SU0:
                    pe.wait_ge(bm_ready, BG)
                    pe.wait_ge(xws_ready, 1)
                    pe.wait_ge(xst_hi, 2)
                if h >= SU0:
                    su(0, h - SU0)
            si(1)
            pe.wait_ge(xw_ready, 1)
            sp_(0)
            sp_(1)
            y_a = lambda k: (hH[:, k, :], hL[:, k, :]) if k < 8 else (YH[:, k - 8, :], YL[:, k - 8, :])
            for b in range(NB):
                su(1, b)
                if b == 3:
                    out_part("even_out", 0, (0,), y_a, (ylo_ready, 0))
            pe.wait_ge(ynat_ready, BG)
            for i in range(8):
                turn_back(f"sy{i}", lambda g: yn[:, g, i * P:(i + 1) * P])
            out_part("even_out", 0, (1,), y_a)
            for g in range(BG):
                out = free_bank(f"sn{g}")
                for i in range(4):
                    pe.wait_ge(sq2_ready, 4 * g + i + 1)
                    last = mm(out[:, 0:T], ones, xbcT[:, 4 * g + i, :], start=(i == 0), stop=(i == 3))
                last.then_inc(mix_done, 1)
            out_part("even_out", 0, (2, 3), y_a)
            out_rest("even_out", y_a, (ylo_ready, 0))
            ffn(0)
            norm(2)
            qk_r = lambda h: (rqT[:, h, :], rkT[:, h, :])
            for i in range(1, len(ODD)):
                t = START["odd"] + i
                if i == len(ODD) - 2:
                    front("r", 0, qk_r)
                tiles([t - 1, t] if i == 1 else [t], normed, (xlo_ready, 2 * KD) if i == 1 else None)
                if 17 <= i <= 32:
                    wait_tile_empty(pe, t - 1)
                    turn(f"rv{i - 17}", vT[:, (i - 17) % 2, :])
            heads("r", CH, AH, qk_r, lambda g, h: rvA[:, g, h, :], CV)
            y_r = lambda k: (hH[:, k, :], hL[:, k, :]) if k < 8 else (RH[:, k - 8, :], RL[:, k - 8, :])
            out_part("odd_out", 0, (0, 1), y_r, (ylo_ready, 16))
            back("r", CH - 1, AH + CH - 1)
            out_part("odd_out", 0, (2, 3), y_r)
            out_rest("odd_out", y_r, (ylo_ready, 16))
            ffn(1)
            norm(4)

        @block.scalar
        def _(eng):
            s = Steps(eng, act_step)
            act = nc.scalar.activation
            at = [0]

            def split(upto):
                while at[0] <= min(upto, CHUNKS - 1):
                    c = at[0]
                    eng.wait_ge(raw_in[c % RING], 16 * (c // RING + 1))
                    if c >= RING:
                        wait_read(eng, c - RING)
                    s.do(act(wh[:, c % RING, :], raw[:, c % RING, :], ACT.Copy), hi_ready)
                    at[0] += 1

            def rsqrt(dst, src, n, ready):
                s.do(act(dst, src, ACT.Ln, scale=1.0 / n, bias=eps[0:dst.shape[0]]))
                s.settle()
                s.do(act(dst, dst, ACT.Exp, scale=-0.5), ready)

            eps = vec[:, VEC_W - 1:VEC_W]

            def log_and_exp():
                nc.scalar.preload_act_table_set("natural_log_exp_and_others")

            def norm(n):
                log_and_exp()
                if n:
                    eng.wait_ge(xlo_ready, KD * n)
                if n in (1, 3):
                    eng.wait_ge(ylo_ready, 16 if n == 1 else 32)
                if n == 1:
                    for i in range(SSLOTS - 4, SSLOTS):
                        eng.wait_ge(sts_out[i], 16 * len(range(i, BG * NB, SSLOTS)))
                for i in range(KD):
                    if n:
                        eng.wait_ge(x_ready, KD * (n - 1) + i + 1)
                    elif i % (KD // 2) == 0:
                        eng.wait_ge(x_in[i // (KD // 2)], 16)
                    s.do(act(hF[:, i, :], xT[:, i, :], ACT.Square), sq_ready)
                if n == 0:
                    split(1)
                    eng.wait_ge(vec_in, 16)
                wait_job(eng, f"norm{n}")
                s.do(act(rstd[:], mb(f"norm{n}")[:, 0:T], ACT.Ln, scale=1.0 / D, bias=eps), mix_act)
                s.settle()
                s.do(act(rstd[:], rstd[:], ACT.Exp, scale=-0.5), rstd_ready)
                if n == 4:
                    return
                for i in range(KD):
                    eng.wait_ge(h_ready, KD * n + i + 1)
                    s.do(act(hH[:, i, :], hF[:, i, :], ACT.Copy), xhi_ready)

            def y_high(n, dst, src):
                s.do(act(dst, src, ACT.Copy), yhi_ready)

            def weights(kind, h, hg):
                sl = hg % 2
                if h >= 2:
                    wait_empty(eng, f"{kind}sc{h - 2}")
                if kind == "a":
                    wait_job(eng, f"abc{h}")
                    b = mb(f"abc{h}")
                    s.do(act(E[:, sl, 0:TP], b[:, 0:TP], ACT.Exp, bias=cols[:, 0, h:h + 1]))
                    s.do(act(E[:, sl, TP:TP + P], b[:, TP:TP + P], ACT.Exp, bias=cols[:, 1, h:h + 1]))
                    s.do(act(E[0:NS, sl, TP + P:BLK], b[0:NS, TP + P:BLK], ACT.Exp, bias=cols[0:NS, 2, h:h + 1]), mix_act)
                else:
                    s.do(act(E[:, sl, :], dist, ACT.Exp, scale=LOG_GAMMA[h]), exp_ready)

            def back(kind, h, Y):
                for i in range(2):
                    n = 2 * h + i
                    wait_empty(eng, f"{kind}yt{n}")
                    y_high(n, Y[n // 8][0][:, n % 8, :], yF[:, n % 2, :])

            def keys(kind, h, hg):
                wait_job(eng, f"{kind}kn{h}")
                b = mb(f"{kind}kn{h}")

                def wk(g, n):
                    if kind == "a":
                        return cols[0:n, g, 96 + h:97 + h]
                    return const("retk")[0:n, g * CH + h:g * CH + h + 1]

                for g in range(2):
                    s.do(act(kg[:, hg % 2, g, :], b[:, g * P:(g + 1) * P], ACT.Copy, scale=wk(g, P)))
                if hg:
                    eng.wait_ge(kgm_ready, hg)
                for dst in (kst[ROW[0]], kst[ROW[2]], kgs[0:NS]):
                    s.do(act(dst, b[0:NS, TP:TP + P], ACT.Copy, scale=wk(2, NS)), mix_act if dst.dtype == F32 else kst_hi)

            def inverse(hg):
                eng.wait_ge(var_ready, hg + 1)
                s.do(act(sm[:, 5, :], sm[:, 4, :], ACT.Ln, bias=eps))
                s.settle()
                s.do(act(sm[:, 6, :], sm[:, 5, :], ACT.Exp, scale=-0.5), inv_ready)

            def heads(kind, count, first, Y, w, values):
                if kind == "r":
                    log_and_exp()
                eng.wait_ge(zeroed, 3 if kind == "a" else 5)
                if kind == "a":
                    s.do(act(vst[STACK, AV + 1:AV + 2], ones[STACK, 0:1], ACT.Copy, scale=0.0))
                for h in range(count):
                    hg = first + h
                    if h + 2 < count and hg:
                        weights(kind, h + 2, hg + 2)
                    for g in range(2):
                        wait_job(eng, f"{kind}o{g}{h}")
                        s.do(act(num[:, hg % 2, g, 0:w], mb(f"{kind}o{g}{h}")[:, 0:w], ACT.Copy), mix_act)
                    if h:
                        inverse(hg - 1)
                    if hg >= 2:
                        eng.wait_ge(pout_out[hg % 2], 16 * (hg // 2))
                    wait_job(eng, f"{kind}sp{h}")
                    s.do(act(pout[:, hg % 2, 0:w], mb(f"{kind}sp{h}")[:, 0:w], ACT.Copy), mix_act)
                    if h + 1 < count:
                        keys(kind, h + 1, hg + 1)
                    if h:
                        wait_job(eng, f"{kind}ss{h - 1}.{NB - 1}")
                    for row in ROW[0:2]:
                        s.do(act(vst[row, 0:w], values(h), ACT.Copy), vst_hi)
                    if hg == 0:
                        silu_x(XB - 2)
                        silu_x(XB - 1)
                    wait_job(eng, f"{kind}oi{h}")
                    wq = cols[0:NS, 2, 32 + h:33 + h] if kind == "a" else const("retq")[0:NS, h:h + 1]
                    s.do(act(num[0:NS, hg % 2, 2, 0:w], mb(f"{kind}oi{h}")[0:NS, 0:w], ACT.Copy, scale=wq), mix_act)
                    if hg == 0:
                        log_and_exp()
                        split(E_OUT + RING - 1)
                    if h:
                        back(kind, h - 1, Y)
                if kind == "r":
                    inverse(first + count - 1)
                    back(kind, count - 1, Y)

            def ffn(l):
                norm(2 * l + 1)
                t0 = START[f"up{l}"]

                eng.wait_ge(zeroed, 4 + 2 * l)

                def silu(j):
                    eng.wait_ge(conv_done, XB + 2 * KF * l + 2 * j + 1)
                    if j >= 2:
                        eng.wait_ge(hid_ready, KF * l + j - 1)
                    s.do(act(sgate[:, j % 2, 0:304], cy[:, 2 * (j % 2), 0:304], ACT.Silu), silu_done)

                def high(j):
                    eng.wait_ge(hid_ready, KF * l + j + 1)
                    s.do(act(HH[:, j, :], hidF[:, j % 3, :], ACT.Copy), hidhi_ready)

                for j in range(KF + 2):
                    if j < KF:
                        for x in range(2):
                            i = 2 * j + x
                            split(last_chunk(t0 + i) + 3)
                            wait_tile(eng, t0 + i)
                            n = XB + 2 * KF * l + i
                            if n >= 4:
                                eng.wait_ge(conv_done, n - 3)
                                eng.wait_ge(tail_done, n - 3)
                            b = bank[(t0 + i) % 4]
                            p = pad[:, n % 4, 1:]
                            s.do(act(p[:, W2:W2 + TP], b[:, 0:TP], ACT.Copy))
                            s.do(act(padded(p, W2)[:, :, W2:], smp(b), ACT.Copy), gemm_act)
                    if 1 <= j <= KF:
                        silu(j - 1)
                    if j >= 2:
                        high(j - 2)
                for i in range(KD):
                    split(last_chunk(START[f"down{l}"] + i) + 3)

            def silu_x(i):
                eng.wait_ge(conv_done, i + 1)
                s.do(act(xbcT[:, i, 0:TP], cy[:, i % 4, 0:TP], ACT.Silu))
                s.do(act(smp(xbcT[:, i, :]), padded(cy[:, i % 4, :], W1, -W1)[:, :, W1:], ACT.Silu), silu_done)

            norm(0)
            split(2)
            eng.wait_ge(table_in, 16)
            s.do(act(drop[:], const("drop"), ACT.Copy))
            s.do(act(identR[:], ident, ACT.Copy), drop_ready)
            eng.wait_ge(zeroed, 1)
            for t in range(T0, START["even_out"]):
                kind, i = TILES[t][1:3]
                split(last_chunk(t) + 3)
                if kind != "gates":
                    wait_tile(eng, t)
                b = bank[t % 4]
                if kind in ("q", "k"):
                    s.do(act((qT if kind == "q" else kT)[:, i, :], b[:, 0:T], ACT.Copy), gemm_act)
                elif kind == "v":
                    if i >= 2:
                        wait_job(eng, f"v{i - 2}")
                    s.do(act(vT[:, i % 2, :], b[:, 0:T], ACT.Copy), gemm_act)
                elif kind == "gates":
                    log_and_exp()
                    eng.wait_ge(row_dve, 1)
                    s.do(act(rows[0:AH, 3, :], rows[0:AH, 3, :], ACT.Exp))
                    s.do(act(rows[0:BH, 4, :], rows[0:BH, 4, :], ACT.Exp))
                    s.do(act(rsm[0:BH, 5, 0:1], v("alog", p=BH), ACT.Exp))
                    s.settle()
                    s.do(act(rows[0:AH, 3, :], rows[0:AH, 3, :], ACT.Ln, bias=1.0))
                    s.do(act(rows[0:BH, 4, :], rows[0:BH, 4, :], ACT.Ln, bias=1.0), row_act)
                    split(last_chunk(t) + 5)
                    eng.wait_ge(row_dve, 2)
                    s.do(act(slab[64:64 + AH, 0, :], rows[0:AH, 3, :], ACT.Exp, scale=-1.0))
                    s.do(act(slab[32:32 + AH, 0, TP:T], rows[0:AH, 4, TP:T], ACT.Exp))
                    s.do(act(rows[0:AH, 5, :], rows[0:AH, 5, :], ACT.Exp))
                    s.do(act(rsm[0:AH, 2, 0:NB], rsm[0:AH, 2, 0:NB], ACT.Exp))
                    s.do(act(slab[96:96 + BH, 1, :], rows[0:BH, 2, :], ACT.Exp, scale=-1.0))
                    s.do(act(slab[64:64 + BH, 1, :], ac[0:BH, :], ACT.Exp))
                    s.do(act(rsm[0:BH, 3, 0:NB], smp(ac[0:BH, :])[:, :, TS - 1], ACT.Exp), row_act)
                elif kind == "og":
                    if i == 0:
                        eng.wait_ge(xlo_ready, KD)
                    s.do(act(hF[:, i, :], b[:, 0:T], ACT.Sigmoid), gemm_act)
                elif kind == "z":
                    s.do(act(zT[:, i, :], b[:, 0:T], ACT.Silu), gemm_act)
                elif kind == "xbc":
                    if i >= 4:
                        eng.wait_ge(conv_done, i - 3)
                        eng.wait_ge(tail_done, i - 3)
                    p = pad[:, i % 4, :]
                    s.do(act(p[:, W1:W1 + TP], b[:, 0:TP], ACT.Copy))
                    s.do(act(padded(p, W1)[:, :, W1:], smp(b), ACT.Copy), gemm_act)
                    if i >= 2:
                        silu_x(i - 2)
                if t == FRONT - 1:
                    log_and_exp()
                    wait_empty(eng, "sdec")
                    weights("a", 0, 0)
                    weights("a", 1, 1)
                    keys("a", 0, 0)
                if t == FRONT + 1:
                    weights("a", 2, 2)
            heads("a", AH, 0, YA, AV + 1, lambda h: vA[0:NS, 2, h, :])
            for g in range(BG):
                wait_job(eng, f"cb{g}")
                b = mb(f"cb{g}")
                s.do(act(cbm[:, g, 0:TP + P], b[:, 0:TP + P], ACT.Copy))
                s.do(act(cbm[0:NS, g, TP + P:BLK], b[0:NS, TP + P:BLK], ACT.Copy), mix_act)
            inverse(AH - 1)
            for i in (3, 4):
                eng.wait_ge(st_out[i], 16)
            for g in range(BG):
                wait_job(eng, f"bn{g}")
                b = mb(f"bn{g}")
                s.do(act(bnat[:, 0:2, g, :], b[:, 0:TP].rearrange("p (g n) -> p g n", g=2), ACT.Copy))
                s.do(act(bst[ROW[0], g, :], b[0:NS, TP:TP + P], ACT.Copy), bst_hi)
                s.do(act(bst[ROW[2], g, :], b[0:NS, TP:TP + P], ACT.Copy), bst_hi)
                s.do(act(bnat[0:NS, 2, g, :], b[0:NS, TP:TP + P], ACT.Copy), mix_act)

            def empty_say(h):
                wait_job(eng, f"say{h}")
                b, sl = mb(f"say{h}"), slice(h * BP, (h + 1) * BP)
                s.do(act(yn[:, 0:2, sl], b[:, 0:2 * BP].rearrange("p (g n) -> p g n", g=2), ACT.Copy))
                s.do(act(yn[0:NS, 2, sl], b[0:NS, 2 * BP:3 * BP], ACT.Copy), mix_act)

            for h in range(BH):
                wait_job(eng, f"sbc{h}")
                if h >= 3:
                    wait_job(eng, f"say{h - 3}")
                b, x = mb(f"sbc{h}"), E2[:, h % 3, :]
                c = P + h
                s.do(act(x[:, 0:TP], b[:, 0:TP], ACT.Exp, bias=cols[:, 0, c:c + 1]))
                s.do(act(x[:, TP:TP + P], b[:, TP:TP + P], ACT.Exp, bias=cols[:, 1, c:c + 1]))
                s.do(act(x[0:NS, TP + P:BLK], b[0:NS, TP + P:BLK], ACT.Exp, bias=cols[0:NS, 2, c:c + 1]), mix_act)
                if h == 1:
                    back("a", AH - 1, YA)
                if h in (SU0 - 2, SU0 - 1):
                    eng.wait_ge(xt_ready, 1)
                    s.do(act(xws[ROW[h - SU0 + 2], :], xt[0:NS, :], ACT.Copy), xst_hi)
                if h - 2 >= SU0:
                    empty_say(h - 2)
            for h in (BH - 2, BH - 1):
                empty_say(h)
            for g in range(BG):
                wait_job(eng, f"sp{g}")
                s.do(act(pst[:, g, :], mb(f"sp{g}")[:, :], ACT.Copy), mix_act)
            log_and_exp()
            for i in range(8):
                eng.wait_ge(zq_ready, i + 1)
                s.do(act(xbcT[:, i, :], zT[:, i, :], ACT.Square), sq2_ready)
            split(E_OUT + RING)
            for g in range(BG):
                wait_job(eng, f"sn{g}")
                s.do(act(rst2[:, g, :], mb(f"sn{g}")[:, 0:T], ACT.Ln, scale=1.0 / GW, bias=eps), mix_act)
                s.settle()
                s.do(act(rst2[:, g, :], rst2[:, g, :], ACT.Exp, scale=-0.5), srs_ready)
            split(E_OUT + RING + 1)
            eng.wait_ge(pst_out, 16 * BG)
            for i in range(8):
                eng.wait_ge(yg_ready, i + 1)
                y_high(8 + i, YH[:, i, :], zT[:, i, :])
            for i in range(KD):
                split(last_chunk(START["even_out"] + i) + 3)
            ffn(0)
            norm(2)
            for j in range(len(ODD)):
                t = START["odd"] + j
                kind, i = TILES[t][1:3]
                split(last_chunk(t) + 3)
                b = bank[t % 4]
                if kind == "rg" and i == 0:
                    log_and_exp()
                    eng.wait_ge(rope_ready, 2 * CH)
                    weights("r", 0, AH)
                    weights("r", 1, AH + 1)
                if j == len(ODD) - 2:
                    keys("r", 0, AH)
                if kind == "rv":
                    wait_tile(eng, t)
                    if i >= 2:
                        wait_job(eng, f"rv{i - 2}")
                    s.do(act(vT[:, i % 2, :], b[:, 0:T], ACT.Copy), gemm_act)
                elif kind == "rg":
                    wait_tile(eng, t)
                    if i == 8:
                        eng.wait_ge(xlo_ready, 3 * KD)
                    s.do(act(gT[:, i, :] if i < 8 else hF[:, i - 8, :], b[:, 0:T], ACT.Silu), gemm_act)
            split(R_OUT + RING - 1)
            heads("r", CH, AH, YR, CV, lambda h: rvA[0:NS, 2, h, :])
            for i in range(KD):
                split(last_chunk(START["odd_out"] + i) + 3)
            ffn(1)
            norm(4)

        @block.vector
        def _(eng):
            s = Steps(eng, dve_step)
            do, settle = s.do, s.settle
            ts, tt, stt = nc.vector.tensor_scalar, nc.vector.tensor_tensor, nc.vector.scalar_tensor_tensor
            copy = nc.vector.tensor_copy
            at = [0]

            def split(upto):
                while at[0] <= min(upto, CHUNKS - 1):
                    c = at[0]
                    eng.wait_ge(hi_ready, c + 1)
                    if c >= RING:
                        wait_read(eng, c - RING)
                    do(tt(wl[:, c % RING, :], raw[:, c % RING, :], wh[:, c % RING, :].bitcast(F32), ALU.subtract), lo_ready)
                    at[0] += 1

            def norm(n):
                if n == 0:
                    eng.wait_ge(vec_in, 16)
                    split(1)
                eng.wait_ge(rstd_ready, n + 1)
                for i in range(KD + 1):
                    if i < KD:
                        do(stt(out=hF[:, i, :], in0=xT[:, i, :], scalar=v(f"norm{n}", i), in1=rstd[:],
                               op0=ALU.mult, op1=ALU.mult), h_ready if n < 4 else y_ready)
                    if i and n < 4:
                        eng.wait_ge(xhi_ready, KD * n + i)
                        do(tt(hL[:, i - 1, :], hF[:, i - 1, :], hH[:, i - 1, :].bitcast(F32), ALU.subtract), xlo_ready)

            def out_tiles(phase, n):
                for i in range(KD):
                    t = START[phase] + i
                    split(last_chunk(t) + 3)
                    wait_tile(eng, t)
                    do(tt(xT[:, i, :], bank[t % 4][:, 0:T], xT[:, i, :], ALU.add), gemm_dve)
                    settle()
                    eng.sem_inc(x_ready, 1)

            def turned(name, dst):
                wait_job(eng, name)
                b = mb(name)
                do(copy(dst(slice(0, 2), P), b[:, 0:TP].rearrange("p (g n) -> p g n", g=2)))
                do(copy(dst(2, NS), b[0:NS, TP:TP + P]), mix_dve)

            def column(s_, i, g):
                n = NS if g == 2 else P
                return cols[0:n, g, P * s_ + i:P * s_ + i + 1]

            def front(kind, h, hg):
                sl = hg % 2
                if kind == "a":
                    wait_empty(eng, f"abc{h}")
                else:
                    eng.wait_ge(exp_ready, h + 1)
                wait_job(eng, f"{kind}sc{h}")
                b = mb(f"{kind}sc{h}")
                do(stt(out=Sp[:, sl, 0:TP + P], in0=b[:, 0:TP + P], scalar=KSCALE, in1=E[:, sl, 0:TP + P],
                       op0=ALU.mult, op1=ALU.mult))
                do(stt(out=Sp[0:NS, sl, TP + P:BLK], in0=b[0:NS, TP + P:BLK], scalar=KSCALE,
                       in1=E[0:NS, sl, TP + P:BLK], op0=ALU.mult, op1=ALU.mult), mix_dve)

            def middle(kind, h, hg, w):
                sl = hg % 2
                y = num[0:NS, sl, 2, 0:w]
                wait_empty(eng, f"{kind}oi{h}")
                wait_job(eng, f"{kind}os{h}")
                do(tt(y, mb(f"{kind}os{h}")[0:NS, 0:w], y, ALU.add), mix_dve)
                m = TOGETHER[kind]
                for b_ in range(m - 1, NB, m):
                    n = 2 * hg + b_ // 4
                    wait_job(eng, f"{kind}ss{h}.{b_}")
                    dec = adec[:, h, b_:b_ + 1] if kind == "a" else math.exp(LOG_GAMMA[h] * TS)
                    x = state(n)[:, b_ % 4 - m + 1:b_ % 4 + 1, 0:w]
                    do(stt(out=x, in0=x, scalar=dec, in1=mb(f"{kind}ss{h}.{b_}")[:, 0:m * w].rearrange("p (m w) -> p m w", m=m),
                           op0=ALU.mult, op1=ALU.add), mix_dve)

            def statistics(kind, h, hg):
                sl = hg % 2
                settle()
                wait_empty(eng, f"{kind}o1{h}")
                for g in range(3):
                    do(nc.vector.bn_stats(out=stats[0:NS if g == 2 else P, g, :], in_=num[0:NS if g == 2 else P, sl, g, 0:CV]))
                if kind == "a":
                    den = num[:, sl, :, AV]
                    do(stt(out=sm[:, 0, :], in0=den, scalar=-1.0, in1=den, op0=ALU.mult, op1=ALU.max))
                settle()
                for g in range(3):
                    do(nc.vector.bn_aggr(out=mv[0:NS if g == 2 else P, g, :], in_=stats[0:NS if g == 2 else P, g, :]))
                if kind == "a":
                    do(tt(sm[:, 1, :], sm[:, 0, :], cols[:, :, 64 + h], ALU.max))
                    settle()
                    do(nc.vector.reciprocal(sm[:, 2, :], sm[:, 1, :]))
                    settle()
                    do(tt(sm[:, 3, :], mv[:, :, 1], sm[:, 2, :], ALU.mult))
                    settle()
                    do(tt(sm[:, 4, :], sm[:, 3, :], sm[:, 2, :], ALU.mult), var_ready)
                else:
                    settle()
                    do(copy(sm[:, 4, :], mv[:, :, 1]), var_ready)

            def normalise(kind, h, hg):
                sl = hg % 2
                eng.wait_ge(inv_ready, hg + 1)
                if kind == "a":
                    do(tt(sm[:, 7, :], sm[:, 6, :], sm[:, 2, :], ALU.mult))
                else:
                    do(copy(sm[:, 7, :], sm[:, 6, :]))
                settle()
                for g in range(3):
                    n = NS if g == 2 else P
                    do(ts(num[0:n, sl, g, 0:CV], num[0:n, sl, g, 0:CV], mv[0:n, g, 0:1], sm[0:n, 7, g:g + 1],
                          ALU.subtract, ALU.mult), yn_ready if g == 2 else None)

            def back(kind, h):
                for i in range(2):
                    n = 2 * h + i
                    wait_job(eng, f"{kind}yt{n}")
                    if n >= 2:
                        eng.wait_ge(ylo_ready, (16 if kind == "r" else 0) + n - 1)
                    if kind == "a":
                        gate, gain = hF[:, n, :], v("ag", n)
                    else:
                        gate, gain = (gT[:, n, :] if n < 8 else hF[:, n - 8, :]), v("rg", n)
                    do(stt(out=yF[:, n % 2, :], in0=mb(f"{kind}yt{n}")[:, 0:T], scalar=gain, in1=gate,
                           op0=ALU.mult, op1=ALU.mult), mix_dve)

            def heads(kind, count, first, w):
                for h in range(count):
                    hg = first + h
                    if h:
                        statistics(kind, h - 1, hg - 1)
                        normalise(kind, h - 1, hg - 1)
                    if h + 1 < count:
                        front(kind, h + 1, hg + 1)
                    if hg == 0:
                        convolve_x(XB - 1)
                    middle(kind, h, hg, w)
                    if hg == 0:
                        split(E_OUT + RING - 1)
                    if h:
                        back(kind, h - 1)
                statistics(kind, count - 1, first + count - 1)
                normalise(kind, count - 1, first + count - 1)

            def convolve(n, x, width, taps, bias):
                eng.wait_ge(fill_done, n + 1)
                y = cy[:, n % 4, 0:width]
                do(ts(y, x[:, 0:width], taps[0], bias, ALU.mult, ALU.add))
                for j in range(1, len(taps)):
                    settle()
                    do(stt(out=y, in0=x[:, j:j + width], scalar=taps[j], in1=y, op0=ALU.mult, op1=ALU.add),
                       conv_done if j == len(taps) - 1 else None)

            def ffn(l):
                norm(2 * l + 1)
                t0 = START[f"up{l}"]
                for j in range(KF + 2):
                    if j < KF:
                        for x in range(2):
                            i = 2 * j + x
                            n = XB + 2 * KF * l + i
                            split(last_chunk(t0 + i) + 3)
                            wait_tile_empty(eng, t0 + i)
                            if x == 0 and j >= 2:
                                eng.wait_ge(silu_done, XB + KF * l + j - 1)
                            convolve(n, pad[:, n % 4, 1:], 304,
                                     [v("fcw", (2 * KF * l + i) * 3 + d) for d in range(3)],
                                     v("fcb", 2 * KF * l + i))
                    if 1 <= j <= KF:
                        p, sl = j - 1, (j - 1) % 2
                        eng.wait_ge(silu_done, XB + KF * l + p + 1)
                        eng.wait_ge(conv_done, XB + 2 * KF * l + 2 * p + 2)
                        if p >= 3:
                            eng.wait_ge(hidlo_ready, KF * l + p - 2)
                        g, u, o = sgate[:, sl, :], cy[:, 2 * sl + 1, :], hidF[:, p % 3, :]
                        do(tt(o[:, 0:TP], g[:, 0:TP], u[:, 0:TP], ALU.mult))
                        do(tt(smp(o), padded(g, W2, -W2)[:, :, W2:], padded(u, W2, -W2)[:, :, W2:],
                              ALU.mult), hid_ready)
                    if j >= 2:
                        p = j - 2
                        eng.wait_ge(hidhi_ready, KF * l + p + 1)
                        do(tt(HL[:, p, :], hidF[:, p % 3, :], HH[:, p, :].bitcast(F32), ALU.subtract), hidlo_ready)
                out_tiles(f"down{l}", 2 * l + 1)

            def gate_rows(t):
                b = bank[t % 4]
                a4, b16 = slice(0, AH), slice(0, BH)
                li, fx, dx, f3, d4, lf, dt = (rows[a4, 0, :], rows[a4, 1, :], rows[b16, 2, :], rows[a4, 3, :],
                                              rows[b16, 4, :], rows[a4, 5, :], rows[b16, 6, :])
                wait_tile(eng, t)
                do(ts(li, b[0:AH, 0:T], v("igb", p=AH), None, ALU.add))
                do(ts(fx, b[32:32 + AH, 0:T], v("fgb", p=AH), None, ALU.add))
                do(ts(dx, b[64:64 + BH, 0:T], v("dtb", p=BH), None, ALU.add), gemm_dve)
                settle()
                do(stt(out=f3, in0=fx, scalar=-1.0, in1=fx, op0=ALU.mult, op1=ALU.min))
                do(stt(out=d4, in0=dx, scalar=-1.0, in1=dx, op0=ALU.mult, op1=ALU.min), row_dve)
                eng.wait_ge(row_act, 1)
                do(stt(out=lf, in0=fx, scalar=0.0, in1=f3, op0=ALU.min, op1=ALU.subtract))
                do(stt(out=dt, in0=dx, scalar=0.0, in1=d4, op0=ALU.max, op1=ALU.add))
                settle()
                split(last_chunk(t) + 4)
                do(copy(slab[32:32 + BH, 1, :], dt))
                do(ts(rows[b16, 7, :], dt, rsm[b16, 5, 0:1], -1.0, ALU.mult, ALU.mult))
                settle()
                kp, dp = resets[:, 0, :], resets[:, 1, :]
                eng.wait_ge(resets_in, 16)
                scan = nc.vector.tensor_tensor_scan
                cum = rows[a4, 8, :]
                do(scan(out=cum, data0=kp[a4], data1=lf, initial=0.0, op0=ALU.mult, op1=ALU.add))
                do(scan(out=ac[b16, :], data0=kp[b16], data1=rows[b16, 7, :], initial=0.0, op0=ALU.mult, op1=ALU.add))
                settle()
                do(ts(slab[b16, 1, :], ac[b16, :], -1.0, None, ALU.mult))
                a = slab[a4, 0, :]
                do(tt(a, li, cum, ALU.subtract))
                settle()
                do(copy(li, a))
                settle()
                first = smp(li)[:, :, 0]
                do(tt(first, first, m0, ALU.max))
                settle()
                M = rows[a4, 1, :]
                do(scan(out=M, data0=dp[a4], data1=li, initial=0.0, op0=ALU.add, op1=ALU.max))
                settle()
                ends = rsm[a4, 0, 0:NB + 1]
                do(copy(ends[:, 0:1], M[:, TP - 1:TP]))
                do(copy(ends[:, 1:NB + 1], smp(M)[:, :, TS - 1]))
                do(ts(nM[a4, :], M, -1.0, None, ALU.mult))
                do(tt(rows[a4, 3, :], cum, M, ALU.add))
                settle()
                do(copy(rsm[a4, 1, 0:1], rows[a4, 3, TP - 1:TP]))
                do(copy(rsm[a4, 1, 1:NB + 1], smp(rows[a4, 3, :])[:, :, TS - 1]))
                do(tt(smp(rows[a4, 4, :]), bc(m0, 2, TS), smp(M), ALU.subtract))
                do(ts(rows[a4, 5, 0:TP], a[:, 0:TP], ends[:, 0:1], None, ALU.subtract))
                do(tt(smp(rows[a4, 5, :]), smp(a), bc(ends[:, 1:NB + 1], 2, TS), ALU.subtract))
                do(tt(rsm[a4, 2, 0:NB], m0, ends[:, 1:NB + 1], ALU.subtract))
                do(ts(rows[b16, 2, 0:TP], ac[b16, 0:TP], ac[b16, TP - 1:TP], None, ALU.subtract))
                do(tt(smp(rows[b16, 2, :]), smp(ac[b16, :]), bc(smp(ac[b16, :])[:, :, TS - 1], 2, TS), ALU.subtract), row_dve)
                split(last_chunk(t) + 5)
                eng.wait_ge(row_act, 2)
                do(ts(slab[96:96 + AH, 0, :], rows[a4, 5, :], KSCALE, None, ALU.mult))
                do(tt(dg[b16], bc(rsm[b16, 3, 0:NB], 2, BH), bc(ident[b16, 0:BH], 1, NB), ALU.mult), slab_ready)

            def gate_columns():
                for c in range(2):
                    turned(f"col{c}", lambda g, p: cols[0:p, g, c * P:(c + 1) * P])
                wait_job(eng, "adec")
                do(copy(adec[:], mb("adec")[:, 0:AH * NB].rearrange("p (h b) -> p h b", h=AH)), mix_dve)
                wait_job(eng, "sdec")
                do(copy(sdec[:], mb("sdec")[:, 0:NB * BH].rearrange("p (b h) -> p b h", b=NB)), mix_dve)
                settle()

            def convolve_x(m):
                wait_tile_empty(eng, XBC0 + m)
                if m >= 4:
                    eng.wait_ge(silu_done, m - 3)
                convolve(m, pad[:, m % 4, :], 312, [v("scw", m * 4 + d) for d in range(4)], v("scb", m))

            norm(0)
            for t in range(T0, START["even_out"]):
                kind, i = TILES[t][1:3]
                split(last_chunk(t) + 3)
                if t == COLS + 1:
                    gate_columns()
                if t == FRONT + 1:
                    front("a", 0, 0)
                if kind == "gates":
                    eng.wait_ge(zeroed, 2)
                    gate_rows(t)
                if 10 <= t <= 17:
                    n = t - 10
                    if n == 0:
                        eng.wait_ge(zeroed, 2)
                    turned(f"v{n}", lambda g, p: vA[0:p, g, n // 2, (n % 2) * P:(n % 2) * P + P])
                if kind == "xbc" and i >= 1:
                    convolve_x(i - 1)
            heads("a", AH, 0, AV + 1)
            def xn(i):
                wait_job(eng, f"xn{i}")
                b = mb(f"xn{i}")
                dtc = cols[:, :, P + 32 + 2 * i:P + 32 + 2 * i + 2]
                do(tt(xdt[:, 0:2, i * P:(i + 1) * P].rearrange("p g (h e) -> p g h e", h=2),
                      b[:, 0:TP].rearrange("p (g h e) -> p g h e", g=2, h=2), bc(dtc[:, 0:2, :], 3, BP), ALU.mult))
                do(tt(xdt[0:NS, 2, i * P:(i + 1) * P].rearrange("p (h e) -> p h e", h=2),
                      b[0:NS, TP:TP + P].rearrange("p (h e) -> p h e", h=2), bc(dtc[0:NS, 2, :], 2, BP), ALU.mult), mix_dve)

            xn(0)
            xn(1)
            back("a", AH - 1)

            def si(g):
                wait_job(eng, f"si{g}")
                r3 = lambda a: a.rearrange("p (h e) -> p h e", h=HG)
                if g:
                    settle()
                do(tt(r3(itmp[0:NS, :]), r3(mb(f"si{g}")[0:NS, :]),
                      bc(cols[0:NS, 2, P + 64 + g * HG:P + 64 + (g + 1) * HG], 2, BP), ALU.mult), mix_dve)

            def add_si(g):
                settle()
                y = yn[0:NS, 2, g * GW:(g + 1) * GW]
                do(tt(y, y, itmp[0:NS, :], ALU.add), ynat_ready)

            def su(g, b_):
                x = sts[(g * NB + b_) % SSLOTS]
                if g and b_ in DECAY_DVE:
                    x3 = x.rearrange("p (h e) -> p h e", h=HG)
                    do(tt(x3, x3, bc(sdec[:, b_, g * HG:(g + 1) * HG], 2, BP), ALU.mult))
                wait_job(eng, f"su{g}.{b_}")
                if g and b_ in DECAY_DVE:
                    settle()
                else:
                    eng.wait_ge(dec_ready, g * NB + b_ + 1 - g * sum(d < b_ for d in DECAY_DVE))
                do(tt(x, mb(f"su{g}.{b_}")[:, :], x, ALU.add), mix_dve)

            for h in range(BH + 1):
                if h < BH:
                    wait_empty(eng, f"sbc{h}")
                    x, c = E2[:, h % 3, :], cbm[:, h // HG, :]
                    for part in ((slice(0, P), slice(0, TP + P)), (slice(0, NS), slice(TP + P, BLK))):
                        do(tt(x[part], x[part], c[part], ALU.mult),
                           e_ready if part[0].stop == NS else None)
                if h:
                    m = h - 1
                if h and m >= SU0:
                    wait_empty(eng, f"say{m}")
                    su(0, m - SU0)
                elif h:
                    wait_job(eng, f"say{m}")
                    b = mb(f"say{m}")
                    sl = slice(m * BP, h * BP)
                    do(copy(yn[:, 0:2, sl], b[:, 0:2 * BP].rearrange("p (g n) -> p g n", g=2)))
                    do(copy(yn[0:NS, 2, sl], b[0:NS, 2 * BP:3 * BP]), mix_dve)
                    if m == SI0:
                        si(0)
                    if h == HG:
                        add_si(0)
                if h < 6:
                    xn(h + 2)
                if h == 5:
                    settle()
                    eng.wait_ge(small_out, 32)
                    do(tt(xt[0:NS, :].rearrange("p (h e) -> p h e", h=BH), xdt[0:NS, 2, :].rearrange("p (h e) -> p h e", h=BH),
                          bc(cols[0:NS, 2, P + 96:P + 96 + BH], 2, BP), ALU.mult), xt_ready)
            for g in range(2):
                x = xdt[:, g, :].rearrange("p (h e) -> p h e", h=BH)
                do(tt(x, x, bc(cols[:, g, P + 96:P + 96 + BH], 2, BP), ALU.mult), xw_ready if g else None)
            si(1)
            add_si(1)
            for b_ in range(NB):
                su(1, b_)
            for i in range(8):
                wait_job(eng, f"sy{i}")
                do(stt(out=ty[:, i % 2, :], in0=xbcT[:, i, :], scalar=v("D", i), in1=mb(f"sy{i}")[:, 0:T],
                       op0=ALU.mult, op1=ALU.add), mix_dve)
                settle()
                do(tt(zT[:, i, :], zT[:, i, :], ty[:, i % 2, :], ALU.mult), zq_ready)
            split(E_OUT + RING)
            for i in range(9):
                if i == 2:
                    split(E_OUT + RING + 1)
                if i < 8:
                    eng.wait_ge(srs_ready, i // 4 + 1)
                    do(stt(out=zT[:, i, :], in0=zT[:, i, :], scalar=v("sg", i), in1=rst2[:, i // 4, :],
                           op0=ALU.mult, op1=ALU.mult), yg_ready)
                if i:
                    eng.wait_ge(yhi_ready, 8 + i)
                    do(tt(YL[:, i - 1, :], zT[:, i - 1, :], YH[:, i - 1, :].bitcast(F32), ALU.subtract), ylo_ready)
            out_tiles("even_out", 0)
            ffn(0)
            norm(2)
            eng.wait_ge(table_in, 16)
            cos, sin = const("cos"), const("sin")
            for j in range(len(ODD)):
                t = START["odd"] + j
                kind, i = TILES[t][1:3]
                split(last_chunk(t) + 3)
                b = bank[t % 4]
                if j == len(ODD) - 2:
                    front("r", 0, AH)
                if kind in ("rq", "rk"):
                    wait_tile(eng, t)
                    if j >= 2:
                        eng.wait_ge(rope_ready, j - 1)
                    do(tt(E[:, j % 2, 0:T], b[:, 0:T], cos, ALU.mult))
                    do(tt(Sp[0:64, j % 2, 0:T], b[64:P, 0:T], sin[64:P], ALU.mult))
                    do(tt(Sp[64:P, j % 2, 0:T], b[0:64, 0:T], sin[0:64], ALU.mult), gemm_dve)
                if 18 <= j <= 33:
                    n = j - 18
                    turned(f"rv{n}", lambda g, p: rvA[0:p, g, n // 2, (n % 2) * P:(n % 2) * P + P])
            split(R_OUT + RING - 1)
            heads("r", CH, AH, CV)
            back("r", CH - 1)
            out_tiles("odd_out", 2)
            ffn(1)
            norm(4)

        @block.gpsimd
        def _(eng):
            s = Steps(eng, pool_step)
            do, settle = s.do, s.settle
            tt, copy = nc.gpsimd.tensor_tensor, nc.gpsimd.tensor_copy

            eng.wait_ge(raw_in[RING - 1], 16)
            eng.dma_start(sst[:], sconv).then_inc(sst_in, 16)
            eng.dma_start(fst[:], fconv).then_inc(fst_in, 16)
            do(nc.gpsimd.memset(pad[:], 0.0), zeroed)
            do(nc.gpsimd.memset(slab[:], 0.0))
            do(nc.gpsimd.memset(cols[:], 1.0))
            do(nc.gpsimd.memset(vA[:, :, :, AV:AV + 1], 1.0), zeroed)
            settle()

            def zero_attention():
                do(nc.gpsimd.memset(num[:], 0.0))
                do(nc.gpsimd.memset(mv[:], 0.0), zeroed)

            def fill(n, x, kept, w):
                if n >= 4:
                    eng.wait_ge(conv_done, n - 3)
                do(copy(padded(x, w)[:, :, 0:w], kept), fill_done)

            def keep_rows(n, x, dst, w, t):
                wait_tile_empty(eng, t)
                do(copy(dst[:, 0:w], x[:, TP:TP + w]))
                do(copy(dst[:, w:(NB + 1) * w].rearrange("p (b r) -> p b r", b=NB), padded(x, w)[:, :, TS:TS + w]), tail_done)

            def queries(kind, h, hg, q):
                if hg >= 2:
                    kk, hh, _ = HEADS[hg - 2]
                    wait_job(eng, f"{kk}oi{hh}")
                if kind == "r":
                    eng.wait_ge(rope_ready, h + 1)
                do(tt(qTm[:, hg % 2], bc(q[:, TP:T], 1, NB), own, ALU.mult), qm_ready)

            def back(kind, h, Y):
                for i in range(2):
                    n = 2 * h + i
                    eng.wait_ge(yhi_ready, (16 if kind == "r" else 0) + n + 1)
                    hi, lo = Y[n // 8]
                    do(tt(lo[:, n % 8, :], yF[:, n % 2, :], hi[:, n % 8, :].bitcast(F32), ALU.subtract), ylo_ready)

            def split_keys(kind, h, hg):
                wait_empty(eng, f"{kind}kn{h}")
                eng.wait_ge(kst_hi, 2 * hg + 2)
                settle()
                do(tt(kst[ROW[1]], kgs[0:NS], kst[ROW[0]].bitcast(F32), ALU.subtract), klo_ready)
                settle()
                if h:
                    wait_job(eng, f"{kind}ss{h - 1}.{NB - 1}")
                do(tt(kgm[STACK], bc(kst[STACK].bitcast(F32), 1, NB), bc(mine[STACK], 2, P), ALU.mult), kgm_ready)

            def heads(kind, count, first, q, Y, w, values):
                if first:
                    queries(kind, 0, first, q(0))
                for h in range(count):
                    hg = first + h
                    if hg:
                        split_keys(kind, h, hg)
                    eng.wait_ge(vst_hi, 2 * hg + 2)
                    settle()
                    do(tt(vst[ROW[2], 0:w], values(h), vst[ROW[0], 0:w].bitcast(F32), ALU.subtract), vst_ready)
                    settle()
                    if h + 1 < count:
                        queries(kind, h + 1, hg + 1, q(h + 1))
                    if h:
                        back(kind, h - 1, Y)
                back(kind, count - 1, Y)

            def ffn(l):
                for i in range(2 * KF + 3):
                    n = XB + 2 * KF * l + i
                    if i < 2 * KF:
                        if l == 1 and i == 0:
                            eng.wait_ge(fout_out, 16)
                        fill(n, pad[:, n % 4, 1:], fst[:, l, i, :, :], W2)
                    if i >= 3:
                        m = i - 3
                        keep_rows(n - 3, pad[:, (n - 3) % 4, 1:], fout[:, m, :], W2, START[f"up{l}"] + m)
                eng.wait_ge(tail_done, XB + 2 * KF * (l + 1))
                eng.dma_start(f_out[l], fout[:]).then_inc(fout_out, 16)

            eng.wait_ge(sst_in, 16)
            eng.wait_ge(fst_in, 16)
            eng.wait_ge(table_in, 16)
            for i in range(XB + 3):
                if i == 4:
                    wait_empty(eng, "sdec")
                    zero_attention()
                    queries("a", 0, 0, qT[:, 0, :])
                    split_keys("a", 0, 0)
                if i < XB:
                    fill(i, pad[:, i % 4, :], sst[:, i], W1)
                if i >= 3:
                    keep_rows(i - 3, pad[:, (i - 3) % 4, :], sout[:, i - 3, :], W1, XBC0 + i - 3)
            eng.wait_ge(slab_ready, 1)
            eng.dma_start(m_out, rsm[0:AH, 1, 0:NB + 1]).then_inc(small_out, 16)
            eng.wait_ge(tail_done, XB)
            eng.dma_start(sconv_out, sout[:]).then_inc(small_out, 16)
            heads("a", AH, 0, lambda h: qT[:, h, :], YA, AV + 1, lambda h: vA[0:NS, 2, h, :])
            settle()
            for i in (3, 4):
                eng.wait_ge(st_out[i], 16)
            for g in range(BG):
                do(tt(cm[:, g], bc(xbcT[:, 10 + g, TP:T], 1, NB), own, ALU.mult), cm_ready if g else None)
            for i in range(2):
                eng.wait_ge(pout_out[i], 16 * (AH // 2))
            for g in range(BG):
                wait_empty(eng, f"bn{g}")
                settle()
                do(tt(bst[ROW[1], g, :], bnat[0:NS, 2, g, :], bst[ROW[0], g, :].bitcast(F32), ALU.subtract))
                settle()
                do(tt(bm[STACK, :, g, :], bc(bst[STACK, g, :].bitcast(F32), 1, NB), bc(mine[STACK], 2, P), ALU.mult), bm_ready)
            eng.wait_ge(xst_hi, 1)
            settle()
            do(tt(xws[ROW[2], :], xt[0:NS, :], xws[ROW[0], :].bitcast(F32), ALU.subtract), xws_ready)
            settle()
            for g in range(BG):
                wait_job(eng, f"si{g}")
                for b in (b for b in range(NB) if not (g and b in DECAY_DVE)):
                    x = sts[(g * NB + b) % SSLOTS].rearrange("p (h e) -> p h e", h=HG)
                    do(tt(x, x, bc(sdec[:, b, g * HG:(g + 1) * HG], 2, BP), ALU.mult), dec_ready)
            for i in range(SSLOTS):
                eng.wait_ge(sts_out[i], 16 * len(range(i, BG * NB, SSLOTS)))
            eng.wait_ge(pst_out, 16 * BG)
            eng.wait_ge(ylo_ready, 16)
            do(nc.gpsimd.memset(pad[:], 0.0), zeroed)
            settle()
            ffn(0)
            for j in range(2 * CH):
                i = j % CH
                wait_tile_empty(eng, START["odd"] + j)
                do(tt((rqT if j < CH else rkT)[:, i, :], E[:, j % 2, 0:T], Sp[:, j % 2, 0:T], ALU.add), rope_ready)
            zero_attention()
            s.count[ylo_ready.name] += 8
            heads("r", CH, AH, lambda h: rqT[:, h, :], YR, CV, lambda h: rvA[0:NS, 2, h, :])
            for i in range(SLOTS):
                eng.wait_ge(st_out[i], 16 * len(range(i, 2 * (AH + CH), SLOTS)))
            for i in range(2):
                eng.wait_ge(pout_out[i], 16 * ((AH + CH) // 2))
            eng.wait_ge(ylo_ready, 32)
            do(nc.gpsimd.memset(pad[:], 0.0), zeroed)
            settle()
            ffn(1)
            eng.wait_ge(fout_out, 32)
            eng.wait_ge(small_out, 32)


def constants():
    c = np.zeros((P, CONST_W), np.float32)

    def put(name, a):
        at, w = CONSTS[name]
        c[:a.shape[0], at:at + w] = a.reshape(a.shape[0], -1)

    key, query = np.arange(P)[:, None], np.arange(TP)[None, :]
    ns = np.arange(NS)
    put("ident", np.eye(P))
    put("ones", np.ones((P, P)))
    gap = np.full((P, BLK), -1.0)
    gap[:, 0:TP] = query - key
    gap[:, TP:TP + P] = query[:, :P] - key
    same = ns[:, None] // TS == ns[None, :] // TS
    gap[:NS, TP + P:] = np.where(same, ns[None, :] - ns[:, None], -1)
    put("drop", np.where(gap >= 0, 0, -1e30))
    put("dist", np.where(gap >= 0, gap, 1e9))
    put("own", np.broadcast_to(np.arange(NB)[:, None] == ns[None, :] // TS, (P, NB, NS)))
    put("mine", np.tile(ns, 3)[:, None] // TS == np.arange(NB)[None, :])
    inv = (np.float32(10000.0) ** (-np.arange(64, dtype=np.float32) / np.float32(64))).astype(np.float32)
    pos = np.concatenate([np.arange(TP), 2048 + ns % TS]).astype(np.float32)
    angle = (pos[None, :] * inv[:, None]).astype(np.float32).astype(np.float64)
    put("cos", np.concatenate([np.cos(angle)] * 2))
    put("sin", np.concatenate([np.sin(angle), -np.sin(angle)]))
    lg = np.array(LOG_GAMMA)[None, :]
    rk = np.zeros((P, 3, CH))
    for g in range(2):
        rk[:, g] = np.exp(lg * (TP - 1 - g * P - np.arange(P))[:, None])
    rk[:NS, 2] = np.exp(lg * (TS - 1 - ns % TS)[:, None])
    put("retk", rk * KSCALE)
    put("retq", np.exp(lg * (ns % TS + 1)[:, None]))
    return c


def starts():
    first = np.zeros(T)
    first[0] = 1
    first[TP::TS] = 1
    drop = -1e30 * first
    drop[0] = 0
    return np.broadcast_to(np.stack([1 - first, drop]).astype(np.float32), (BH, 2, T))


def kernel(**inputs):
    import concourse.bacc as bacc
    from concourse.bass_utils import run_bass_kernel_spmd

    a = {k: np.asarray(x) for k, x in inputs.items()}

    def tiled(x):
        return np.moveaxis(x.reshape(*x.shape[:-1], -1, P), -1, 0)

    def paired(x):
        n = x.shape[:-1]
        return np.swapaxes(x.reshape(*n, 2, KF, P), -3, -2).reshape(*n, 2 * KF * P)

    tokens = np.concatenate([a["x_prompt"].reshape(TP, D), a["x_sample"].reshape(NS, D)])
    xin = np.ascontiguousarray(np.swapaxes(tiled(tokens), 1, 2))

    def weight_tiles(w):
        k, n = w.shape
        return w.reshape(k // P, P, n // P, P).transpose(2, 0, 1, 3).reshape(-1, P, P)

    def halves(w):
        return weight_tiles(w).reshape(-1, 4, 2, CHUNK, P, P).swapaxes(1, 2).reshape(-1, P, P)

    w = a["even_w_in"][0]
    gates = np.zeros((D, P), np.float32)
    gates[:, 0:AH] = w[:, 2048:2052]
    gates[:, 32:32 + AH] = w[:, 2052:2056]
    gates[:, 64:64 + BH] = w[:, 5640:5656]
    w_even = np.concatenate([w[:, :2048], gates, w[:, 2056:5640]], axis=1)
    streams = [weight_tiles(w_even), halves(a["even_w_out"][0]),
               weight_tiles(paired(a["ffn_w_up"][0])), weight_tiles(a["ffn_w_down"][0]),
               weight_tiles(a["odd_w_in"][0]), halves(a["odd_w_out"][0]),
               weight_tiles(paired(a["ffn_w_up"][1])), weight_tiles(a["ffn_w_down"][1])]
    wts = np.concatenate(streams).reshape(CHUNKS, CHUNK, P, P).transpose(0, 2, 1, 3).reshape(CHUNKS, P, CHUNK * P)

    vecs = np.zeros((P, VEC_W), np.float32)

    def put(name, x):
        at, n = VECS[name]
        vecs[:x.shape[0], at:at + n] = x.reshape(x.shape[0], -1)

    for i, g in enumerate((a["norm_mix_g"][0], a["norm_ffn_g"][0], a["norm_mix_g"][1], a["norm_ffn_g"][1],
                           a["norm_final_g"])):
        put(f"norm{i}", tiled(g))
    put("ag", tiled(a["mlstm_norm_g"][0]))
    put("scw", np.swapaxes(tiled(a["ssd_conv_w"][0]), 1, 2))
    put("scb", tiled(a["ssd_conv_b"][0]))
    put("D", tiled(np.repeat(a["ssd_D"][0], BP)))
    put("sg", tiled(a["ssd_norm_g"][0]))
    put("rg", tiled(a["ret_norm_g"][0]))
    put("fcw", np.swapaxes(tiled(paired(a["ffn_conv_w"])), 2, 3))
    put("fcb", tiled(paired(a["ffn_conv_b"])))
    for name, x in (("igb", a["mlstm_igate_b"]), ("fgb", a["mlstm_fgate_b"]), ("dtb", a["ssd_dt_bias"]),
                    ("alog", a["ssd_A_log"])):
        put(name, x[0][:, None])
    put("m0", a["state_mlstm_m"][0].T)
    vecs[:, VECS["eps"][0]] = EPS

    sconv = np.ascontiguousarray(tiled(a["state_ssd_conv"][0]).transpose(0, 3, 1, 2))
    fconv = np.ascontiguousarray(tiled(paired(a["state_ffn_conv"])).transpose(0, 1, 4, 2, 3))
    c_in = np.concatenate([a["state_mlstm_C"][0], a["state_mlstm_n"][0][..., None]], axis=-1).transpose(1, 2, 0, 3)
    r_in = a["state_ret_S"][0].transpose(1, 2, 0, 3)
    h_in = a["state_ssd_h"][0].reshape(NB, BH * BP, P).transpose(0, 2, 1)
    ins = {"xin": xin, "wts": wts, "consts": constants(), "starts": starts(), "vecs": vecs, "sconv": sconv, "fconv": fconv,
           "c_in": c_in, "r_in": r_in, "h_in": h_in}
    outs = {"y_out": (P, KD, T), "c_out": (AH, P, NB, AV + 1), "cp_out": (AH, P, AV + 1), "m_out": (AH, NB + 1),
            "sconv_out": (P, XB, 27), "h_out": (NB, P, D), "hp_out": (P, D), "r_out": (CH, P, NB, CV),
            "rp_out": (CH, P, CV), "f_out": (2, P, 2 * KF, 18)}
    ins = {k: np.ascontiguousarray(x) for k, x in ins.items()}
    nc = bacc.Bacc("TRN2", target_bir_lowering=False, num_devices=1)
    args = [nc.dram_tensor(k, x.shape, F32, kind="ExternalInput").ap() for k, x in ins.items()]
    args += [nc.dram_tensor(k, s, F32, kind="ExternalOutput").ap() for k, s in outs.items()]
    build(nc, *args)
    r = run_bass_kernel_spmd(nc, [ins], core_ids=[0]).results[0]

    def untiled(x):
        return np.moveaxis(x, 0, -1).reshape(*x.shape[1:-1], -1)

    def unpaired(x):
        return np.swapaxes(x.reshape(*x.shape[:-1], KF, 2, P), -3, -2).reshape(x.shape)

    y = untiled(np.swapaxes(r["y_out"], 1, 2))
    c = r["c_out"].transpose(2, 0, 1, 3)
    cp = r["cp_out"]
    m = r["m_out"]
    sc = untiled(np.swapaxes(r["sconv_out"], 1, 2))
    fc = unpaired(untiled(r["f_out"].transpose(1, 0, 3, 2)))
    h = r["h_out"].transpose(0, 2, 1).reshape(NB, BH, BP, P)
    hp = r["hp_out"].T.reshape(1, BH, BP, P)
    return (y[:TP].reshape(1, TP, D), y[TP:].reshape(NB, TS, D),
            cp[None, None, ..., :AV], cp[None, None, ..., AV], m[:, 0][None, None],
            sc[:W1][None, None], hp[None], r["rp_out"][None, None], fc[:, :W2][:, None],
            c[None, ..., :AV], c[None, ..., AV], m[:, 1:].T[None],
            sc[W1:].reshape(1, NB, W1, -1), h[None], r["r_out"].transpose(2, 0, 1, 3)[None],
            fc[:, W2:].reshape(2, NB, W2, -1))
```
